# Optimizing a Trainium2 kernel written in Bass

```python
import jax, jax.numpy as jnp
from jax import lax
import numpy as np

D_MODEL = 1024
BATCH = 1
SEQ = 1024
DEPTH = 2
DEC_BATCH = 8
DEC_SEQ = 1
PAST_LEN = 256
PAGE_SIZE = 128

HA = 4
DA = 128
WA = HA * DA
HB = 4
DKB = 64
DVB = 64
WB = HB * DVB
DC = 256
CONV_W = 31
D_FF = 2816
FFN_CONV_W = 3
Q_BLOCK = 128
RET_CHUNK = 128
ROPE_BASE = 10000.0
EPS = 1e-6
COL_SIZES = (WA, WA, WA, HA, HB * DKB, HB * DKB, WB, WB, DC, DC)
N_IN = sum(COL_SIZES)

kernel_name = 'hybrid_fox_retnet_conformer_decoder_step'

F32 = jnp.float32

def _standardize(x):
    xf = x.astype(F32)
    mu = jnp.mean(xf, axis=-1, keepdims=True)
    xc = xf - mu
    return xc * lax.rsqrt(jnp.mean(xc * xc, axis=-1, keepdims=True) + EPS)

def rmsnorm(x, g):
    xf = x.astype(F32)
    y = xf * lax.rsqrt(jnp.mean(xf * xf, axis=-1, keepdims=True) + EPS)
    return (y * g.astype(F32)).astype(x.dtype)

def layernorm(x, g, b):
    return (_standardize(x) * g.astype(F32) + b.astype(F32)).astype(x.dtype)

def split_cols(p):
    offs = np.cumsum(COL_SIZES)[:-1].tolist()
    return jnp.split(p, offs, axis=-1)

def rope(x, pos):
    half = x.shape[-1] // 2
    inv = ROPE_BASE ** (-jnp.arange(half, dtype=F32) / half)
    ang = pos.astype(F32)[:, None] * inv[None, :]
    cos = jnp.cos(ang)[None, :, None, :]
    sin = jnp.sin(ang)[None, :, None, :]
    xf = x.astype(F32)
    x1, x2 = xf[..., :half], xf[..., half:]
    return jnp.concatenate([x1 * cos - x2 * sin, x1 * sin + x2 * cos], axis=-1).astype(x.dtype)

def causal_dwconv(ctx, u, w, b):
    ext = jnp.concatenate([ctx.astype(u.dtype), u], axis=1)
    y = lax.conv_general_dilated(ext, w[:, None, :].astype(u.dtype), window_strides=(1,), padding='VALID',
                                 dimension_numbers=('NWC', 'WIO', 'NWC'), feature_group_count=u.shape[-1])
    return y + b.astype(u.dtype), ext[:, -(w.shape[0] - 1):]

def fox_prompt(q, k, v, logf):
    n, s = q.shape[0], q.shape[1]
    nb = s // Q_BLOCK
    scale = DA ** -0.5
    cum = jnp.cumsum(logf, axis=1).transpose(0, 2, 1)
    qb = q.reshape(n, nb, Q_BLOCK, HA, DA).transpose(1, 0, 2, 3, 4)
    cqb = cum.reshape(n, HA, nb, Q_BLOCK).transpose(2, 0, 1, 3)
    kpos = jnp.arange(s)

    def block(args):
        bi, qi, ci = args
        qpos = bi * Q_BLOCK + jnp.arange(Q_BLOCK)
        logits = jnp.einsum('nqhd,nkhd->nhqk', qi, k).astype(F32) * scale
        logits = logits + ci[..., :, None] - cum[:, :, None, :]
        logits = jnp.where(kpos[None, :] <= qpos[:, None], logits, -jnp.inf)
        p = jax.nn.softmax(logits, axis=-1).astype(v.dtype)
        return jnp.einsum('nhqk,nkhd->nqhd', p, v)

    out = lax.map(block, (jnp.arange(nb), qb, cqb))
    return out.transpose(1, 0, 2, 3, 4).reshape(n, s, HA, DA)

def fox_sample(q, k, v, logf, pool_k, pool_v, pool_lf, page_table):
    n, t = q.shape[0], q.shape[1]
    past = page_table.shape[1] * PAGE_SIZE
    scale = DA ** -0.5
    k_all = jnp.concatenate([pool_k[page_table].reshape(n, past, HA, DA).astype(k.dtype), k], axis=1)
    v_all = jnp.concatenate([pool_v[page_table].reshape(n, past, HA, DA).astype(v.dtype), v], axis=1)
    lf_all = jnp.concatenate([pool_lf[page_table].reshape(n, past, HA).astype(F32), logf], axis=1)
    cum = jnp.cumsum(lf_all, axis=1).transpose(0, 2, 1)
    logits = jnp.einsum('nqhd,nkhd->nhqk', q, k_all).astype(F32) * scale
    logits = logits + cum[:, :, past:, None] - cum[:, :, None, :]
    kpos = jnp.arange(past + t)
    qpos = past + jnp.arange(t)
    logits = jnp.where(kpos[None, :] <= qpos[:, None], logits, -jnp.inf)
    p = jax.nn.softmax(logits, axis=-1).astype(v.dtype)
    return jnp.einsum('nhqk,nkhd->nqhd', p, v_all)

def retention(q, k, v, s0, chunk):
    n, L = q.shape[0], q.shape[1]
    nc = L // chunk
    log_g = jnp.log1p(-(2.0 ** (-5.0 - jnp.arange(HB, dtype=F32))))
    idx = jnp.arange(chunk, dtype=F32)
    rel = idx[:, None] - idx[None, :]
    decay = jnp.where(rel >= 0, jnp.exp(log_g[:, None, None] * jnp.maximum(rel, 0.0)[None]), 0.0)
    xi = jnp.exp(log_g[:, None] * (idx + 1.0)[None])
    zeta = jnp.exp(log_g[:, None] * (chunk - 1.0 - idx)[None])
    g_chunk = jnp.exp(log_g * chunk)

    def to_chunks(a):
        return a.astype(F32).reshape(n, nc, chunk, *a.shape[2:]).swapaxes(0, 1)

    def step(s, inp):
        qc, kc, vc = inp
        att = jnp.einsum('nchd,nmhd->nhcm', qc, kc) * decay[None]
        o = jnp.einsum('nhcm,nmhe->nche', att, vc)
        o = o + jnp.einsum('nchd,nhde->nche', qc, s) * xi.T[None, :, :, None]
        s = g_chunk[None, :, None, None] * s + jnp.einsum('nchd,hc,nche->nhde', kc, zeta, vc)
        return s, o

    s_fin, o = lax.scan(step, s0.astype(F32), (to_chunks(q), to_chunks(k), to_chunks(v)))
    return o.swapaxes(0, 1).reshape(n, L, HB, DVB), s_fin

def decoder_layer(x, c, pos, attn_fn, ret_s0, conv_ctx, ffn_ctx, ret_chunk,
                  ada_w, ada_b, norms, w_in, b_f, ret_gn_g, conv_w, conv_b, conv_ln_g, conv_ln_b,
                  w_o, ffn_up, ffn_conv_w, ffn_conv_b, ffn_down):
    n, L = x.shape[0], x.shape[1]
    mod = jnp.dot(jax.nn.silu(c), ada_w) + ada_b
    sh1, sc1, g1, sh2, sc2, g2 = jnp.split(mod[:, None, :], 6, axis=-1)

    h = rmsnorm(x, norms[0]) * (1 + sc1) + sh1
    aq, ak, av, af, bq, bk, bv, bg, ca, cb = split_cols(jnp.dot(h, w_in))
    logf = jax.nn.log_sigmoid((af + b_f).astype(F32))
    k_a = ak.reshape(n, L, HA, DA)
    v_a = av.reshape(n, L, HA, DA)
    o_a = attn_fn(aq.reshape(n, L, HA, DA), k_a, v_a, logf).reshape(n, L, WA)
    q_b = rope(bq.reshape(n, L, HB, DKB), pos)
    k_b = rope(bk.reshape(n, L, HB, DKB), pos) * (DKB ** -0.5)
    r, ret_s = retention(q_b, k_b, bv.reshape(n, L, HB, DVB), ret_s0, ret_chunk)
    r = (_standardize(r).reshape(n, L, WB) * ret_gn_g.astype(F32)).astype(x.dtype)
    o_b = r * jax.nn.silu(bg)
    u = ca * jax.nn.sigmoid(cb)
    cv, conv_state = causal_dwconv(conv_ctx, u, conv_w, conv_b)
    o_c = jax.nn.silu(layernorm(cv, conv_ln_g, conv_ln_b))
    mix = jnp.dot(jnp.concatenate([o_a, o_b, o_c], axis=-1), w_o)
    x = x + g1 * rmsnorm(mix, norms[1])

    h2 = rmsnorm(x, norms[2]) * (1 + sc2) + sh2
    up, ffn_state = causal_dwconv(ffn_ctx, jnp.dot(h2, ffn_up), ffn_conv_w, ffn_conv_b)
    a, b = jnp.split(up, 2, axis=-1)
    f = jnp.dot(jax.nn.silu(a) * b, ffn_down)
    x = x + g2 * rmsnorm(f, norms[3])
    return x, k_a, v_a, logf, ret_s.astype(ret_s0.dtype), conv_state, ffn_state

def setup_inputs(seed: int = 0) -> dict:
    key = jax.random.key(seed)
    ks = jax.random.split(key, 32)
    n_pages = PAST_LEN // PAGE_SIZE
    n_used = DEC_BATCH * n_pages
    n_pool = n_used + (n_used + 3) // 4
    perm = jax.random.permutation(ks[0], n_pool)
    page_table = perm[:n_used].reshape(DEC_BATCH, n_pages).astype(jnp.int32)

    def nrm(k, shape, s):
        return jax.random.normal(k, shape, F32) * s

    return {
        'x_prompt': nrm(ks[1], (BATCH, SEQ, D_MODEL), 1.0),
        'x_sample': nrm(ks[2], (DEC_BATCH, DEC_SEQ, D_MODEL), 1.0),
        'cache_k': nrm(ks[3], (DEPTH, n_pool, PAGE_SIZE, HA, DA), 1.0),
        'cache_v': nrm(ks[4], (DEPTH, n_pool, PAGE_SIZE, HA, DA), 1.0),
        'cache_logf': jax.nn.log_sigmoid(4.0 + nrm(ks[5], (DEPTH, n_pool, PAGE_SIZE, HA), 1.0)),
        'state_ret': nrm(ks[6], (DEPTH, DEC_BATCH, HB, DKB, DVB), 0.5),
        'state_conv': nrm(ks[7], (DEPTH, DEC_BATCH, CONV_W - 1, DC), 1.0),
        'state_ffn_conv': nrm(ks[8], (DEPTH, DEC_BATCH, FFN_CONV_W - 1, 2 * D_FF), 1.0),
        'page_table': page_table,
        'c_prompt': nrm(ks[9], (BATCH, D_MODEL), 1.0),
        'c_sample': nrm(ks[10], (DEC_BATCH, D_MODEL), 1.0),
        'ada_w': nrm(ks[11], (DEPTH, D_MODEL, 6 * D_MODEL), 0.5 * D_MODEL ** -0.5),
        'ada_b': nrm(ks[12], (DEPTH, 6 * D_MODEL), 0.02),
        'norms': 1.0 + nrm(ks[13], (DEPTH, 4, D_MODEL), 0.1),
        'w_in': nrm(ks[14], (DEPTH, D_MODEL, N_IN), D_MODEL ** -0.5),
        'b_f': 4.0 + nrm(ks[15], (DEPTH, HA), 0.5),
        'ret_gn_g': 1.0 + nrm(ks[16], (DEPTH, WB), 0.1),
        'conv_w': nrm(ks[17], (DEPTH, CONV_W, DC), CONV_W ** -0.5),
        'conv_b': nrm(ks[18], (DEPTH, DC), 0.02),
        'conv_ln_g': 1.0 + nrm(ks[19], (DEPTH, DC), 0.1),
        'conv_ln_b': nrm(ks[20], (DEPTH, DC), 0.02),
        'w_o': nrm(ks[21], (DEPTH, D_MODEL, D_MODEL), D_MODEL ** -0.5),
        'ffn_up': nrm(ks[22], (DEPTH, D_MODEL, 2 * D_FF), D_MODEL ** -0.5),
        'ffn_conv_w': nrm(ks[23], (DEPTH, FFN_CONV_W, 2 * D_FF), FFN_CONV_W ** -0.5),
        'ffn_conv_b': nrm(ks[24], (DEPTH, 2 * D_FF), 0.02),
        'ffn_down': nrm(ks[25], (DEPTH, D_FF, D_MODEL), D_FF ** -0.5),
    }

def reference(x_prompt, x_sample, cache_k, cache_v, cache_logf, state_ret, state_conv, state_ffn_conv,
              page_table, c_prompt, c_sample, ada_w, ada_b, norms, w_in, b_f, ret_gn_g, conv_w, conv_b,
              conv_ln_g, conv_ln_b, w_o, ffn_up, ffn_conv_w, ffn_conv_b, ffn_down):
    bp, sp_len = x_prompt.shape[0], x_prompt.shape[1]
    pos_p = jnp.arange(sp_len)
    pos_s = page_table.shape[1] * PAGE_SIZE + jnp.arange(x_sample.shape[1])
    xp, xs = x_prompt, x_sample
    p_out, s_out = [], []
    for l in range(DEPTH):
        wl = (ada_w[l], ada_b[l], norms[l], w_in[l], b_f[l], ret_gn_g[l], conv_w[l], conv_b[l],
              conv_ln_g[l], conv_ln_b[l], w_o[l], ffn_up[l], ffn_conv_w[l], ffn_conv_b[l], ffn_down[l])
        ret0 = jnp.zeros((bp, HB, DKB, DVB), F32)
        conv0 = jnp.zeros((bp, CONV_W - 1, DC), xp.dtype)
        ffn0 = jnp.zeros((bp, FFN_CONV_W - 1, 2 * D_FF), xp.dtype)
        xp, *st_p = decoder_layer(xp, c_prompt, pos_p, fox_prompt, ret0, conv0, ffn0, RET_CHUNK, *wl)
        p_out.append(st_p)
        attn_s = (lambda q, k, v, lf, l=l: fox_sample(q, k, v, lf, cache_k[l], cache_v[l], cache_logf[l], page_table))
        xs, *st_s = decoder_layer(xs, c_sample, pos_s, attn_s, state_ret[l], state_conv[l], state_ffn_conv[l],
                                  xs.shape[1], *wl)
        s_out.append(st_s)
    pk, pv, plf, pret, pconv, pffn = [jnp.stack(a) for a in zip(*p_out)]
    sk, sv, slf, sret, sconv, sffn = [jnp.stack(a) for a in zip(*s_out)]
    return (xp, xs, pk, pv, plf, pret, pconv, pffn, sk, sv, slf, sret, sconv, sffn)


_drawn_inputs = setup_inputs


def setup_inputs(seed=0):
    import zlib

    import numpy as np

    out = dict(_drawn_inputs(seed))
    spreads = {}
    factors = {'cache_logf': 3.351, 'conv_b': 4.886, 'conv_ln_b': 8.0, 'ffn_conv_b': 5.34}
    for name, (base, spread) in spreads.items():
        noise = np.random.default_rng([zlib.crc32(name.encode()), seed]).standard_normal(out[name].shape)
        drawn = base * np.exp(spread * noise) if base else spread * noise
        out[name] = __import__('jax').numpy.asarray(drawn.astype(out[name].dtype))
    for name, factor in factors.items():
        out[name] = (out[name] * factor).astype(out[name].dtype)
    return out
```

```python
from contextlib import ExitStack

import numpy as np
import concourse.bass as bass
from concourse import mybir

F32 = mybir.dt.float32
F32R = mybir.dt.float32r
BF16 = mybir.dt.bfloat16
I32 = mybir.dt.int32
ALU = mybir.AluOpType
ACT = mybir.ActivationFunctionType
AX_X = mybir.AxisListType.X

P = 128
D_MODEL, TP, S, DEPTH = 1024, 1024, 8, 2
NT = TP + S
KD = D_MODEL // P
HA, DA, HB, DB, DC = 4, 128, 4, 64, 256
CONV_W, FW = 31, 3
CTX = CONV_W - 1
D_FF = 2816
FT = D_FF // P
PAST, PAGE = 256, 128
NPG = PAST // PAGE
EPS = 1e-6
NC8 = TP // P
TC = NC8 + 1
COL_F = 3 * HA * DA
COL_BQ = COL_F + HA
COL_CA = COL_BQ + 4 * HB * DB
N_IN = COL_CA + 2 * DC
A_SCALE = DA ** -0.5
RSQRT_MAGIC = float(0x5F3759DF)

BANK = 512
SLOT = 3 * BANK
OFF = 252
CHUNKS = ((0, BANK - OFF), (BANK - OFF, 2 * BANK - OFF), (2 * BANK - OFF, NT))
HALVES = ((0, 512), (512, 1024))

CONST = {}
_at = 0
for _name, _n in (("ident", 128), ("ones", 128), ("upto", 128), ("after", 128), ("mask", 128), ("pair", 128),
                  ("stack", 64), ("headsel", 2), ("sampsel", 8), ("decay", 512), ("xi", 256), ("zeta", 4), ("gchunk", 2),
                  ("gone", 2)):
    CONST[_name] = (_at, _n)
    _at += _n
N_CONST = _at


def constants():
    out = np.zeros((P, N_CONST), np.float32)

    def put(name, a):
        at, n = CONST[name]
        out[:, at:at + n] = np.asarray(a, np.float32).reshape(P, n)

    r = np.arange(P)
    put("ident", np.eye(P))
    put("ones", np.ones((P, P)))
    put("upto", r[:, None] <= r[None, :])
    put("after", r[:, None] > r[None, :])
    put("mask", np.where(r[None, :] <= r[:, None], 0.0, -1e30))
    put("pair", (r[:, None] // 64) == (r[None, :] // 64))
    put("stack", (r[:, None] % 64) == np.arange(64)[None, :])
    put("headsel", (r[:, None] // 64) == np.arange(2)[None, :])
    put("sampsel", r[:, None] == 120 + np.arange(8)[None, :])
    log_g = np.log1p(-(2.0 ** (-5.0 - np.arange(HB))))
    rel = r[None, :] - r[:, None]
    dec = np.stack([np.where(rel >= 0, np.exp(log_g[h] * np.maximum(rel, 0)), 0.0) for h in range(HB)])
    put("decay", dec.reshape(2, 2, P, P).transpose(2, 1, 0, 3))
    hp = r // 64
    put("xi", np.stack([[np.exp(log_g[2 * hh + p] * (r + 1.0)) for hh in range(2)] for p in hp]))
    put("zeta", np.exp(log_g[None, :] * (P - 1.0 - r[:, None])))
    put("gchunk", np.exp(np.stack([log_g[2 * hh + hp] for hh in range(2)], 1) * P))
    put("gone", np.exp(np.stack([log_g[2 * hh + hp] for hh in range(2)], 1)))
    half = DB // 2
    inv = np.float32(10000.0) ** (-np.arange(half, dtype=np.float32) / np.float32(half))
    pos = np.concatenate([np.arange(TP), np.full(S, PAST)]).astype(np.float32)
    ang = (pos[None, :] * inv[:, None].astype(np.float32)).astype(np.float32)
    cos, sin = np.cos(ang), np.sin(ang)
    rope = np.concatenate([np.tile(cos, (4, 1)), np.concatenate([-sin, sin, -sin, sin])], 1).astype(np.float32)
    return out, rope


class K:
    pass


def gated(e, sem, value, passed):
    e.wait_ge(sem, value)
    if not isinstance(value, int):
        e.sem_inc(passed, 1)


class Link:

    def __init__(self, e, sem):
        self.e, self.sem, self.n = e, sem, 0

    def __call__(self, ins):
        self.n += 1
        ins.then_inc(self.sem, 1)
        self.e.wait_ge(self.sem, self.n)


class Ahead:

    def __init__(self, k, tiles):
        self.k, self.tiles = k, tiles
        self.loaded, self.hi_done = [k.sem("ahead_loaded0"), k.sem("ahead_loaded1")], k.sem("ahead_hi_done")

    def load(self, sp):
        for s in range(2):
            sp.dma_start(self.k.w_raw[s][:, :, :], self.tiles[s]).then_inc(self.loaded[s], 16)

    def high(self, act):
        for s in range(2):
            act.wait_ge(self.loaded[s], 16)
            act.activation(self.k.w_hi[s][:, :, :], self.k.w_raw[s][:, :, :], ACT.Copy).then_inc(self.hi_done, 1)

    def low(self, pool):
        k = self.k
        for s in range(2):
            pool.wait_ge(self.hi_done, s + 1)
            pool.tensor_tensor(k.w_lo[s][:, :, :], k.w_raw[s][:, :, :], k.w_hi[s][:, :, :].bitcast(F32),
                               ALU.subtract).then_inc(k.quiet, 1)


def product3(e, out, w_hi, w_lo, x_hi, x_lo, kt, cols, x_ready=None):
    last = None
    for k in range(kt):
        if x_ready is not None:
            e.wait_ge(x_ready, k + 1)
        for w, x, first in ((w_hi, x_hi, True), (w_hi, x_lo, False), (w_lo, x_hi, False)):
            for a, b in CHUNKS:
                last = e.matmul(out[:, OFF + a:OFF + b], w[:, k, cols], x[:, k, a:b],
                                start=(k == 0 and first), stop=(k == kt - 1 and w is w_lo))
    return last


def rsqrt(dve, link, y, v, t):
    link(dve.tensor_scalar(y.bitcast(I32), v.bitcast(I32), -0.5, RSQRT_MAGIC, ALU.mult, ALU.add))
    for _ in range(3):
        link(dve.tensor_tensor(t, y, y, ALU.mult))
        link(dve.scalar_tensor_tensor(t, t, -0.5, v, ALU.mult, ALU.mult))
        link(dve.scalar_tensor_tensor(y, t, 1.5, y, ALU.add, ALU.mult))


def const(k, name):
    at, n = CONST[name]
    return k.consts[:, at:at + n]


def bc(ap, axis, n):
    shape = list(ap.shape)
    shape.insert(axis, n)
    return ap.unsqueeze(axis).to_broadcast(shape)


def block_entry(k):
    nc, d = k.nc, k.dram
    with ExitStack() as ctx:
        sb = lambda n, s, t=F32: ctx.enter_context(nc.sbuf_tensor(n, s, t))
        ps = lambda n, s, t=F32: ctx.enter_context(nc.psum_tensor(n, s, t))
        sem = lambda n: ctx.enter_context(nc.semaphore(n))
        xrow = sb("xrow", [P, TC, D_MODEL])
        crow = sb("crow", [1 + S, D_MODEL])
        tp = [ps(f"tp_{i}", [P, 512]) for i in range(2)]
        cp = ps("cp", [P, 512])
        loaded, const_loaded, turned, moved, csilu, cturned, zeroed = (
            sem(n) for n in ("loaded", "const_loaded", "turned", "moved", "csilu", "cturned", "zeroed"))
        block = ctx.enter_context(nc.Block())
        nx = 2 * KD + 1

        @block.sync
        def _(sp):
            sp.dma_start(k.consts[:, :], d["consts"]).then_inc(const_loaded, 16)
            sp.dma_start(crow[0:1, :], d["c_prompt"]).then_inc(const_loaded, 16)
            sp.dma_start(crow[1:1 + S, :], d["c_sample"]).then_inc(const_loaded, 16)
            sp.dma_start(k.pages[:, :], d["page_table"].rearrange("a b -> (a b)").unsqueeze(0)).then_inc(const_loaded, 16)
            sp.dma_start(xrow[:, 0:NC8, :], d["x_prompt"][0].rearrange("(c p) f -> p c f", p=P)).then_inc(loaded, 16)
            sp.dma_start(xrow[0:S, NC8, :], d["x_sample"].rearrange("a b f -> (a b) f")).then_inc(loaded, 16)

        @block.vector
        def _(dve):
            dve.wait_ge(const_loaded, 64)
            dve.tensor_copy(k.ident_bf[:, :], const(k, "ident"))
            dve.tensor_copy(k.mask_bf[:, :], const(k, "mask"))
            for f in range(KD):
                for half in range(2):
                    i = 2 * f + half
                    dve.wait_ge(turned, i + 1)
                    dve.tensor_copy(k.x[:, f, 512 * half:512 * half + 512], tp[i % 2][:, :]).then_inc(moved, 1)
            dve.wait_ge(cturned, 1)
            dve.tensor_copy(k.cT[:, :, :], cp[:, 0:KD * 9].rearrange("p (f c) -> p f c", c=9))
            dve.tensor_copy(k.x[:, :, TP:NT], cp[:, 128:128 + KD * S].rearrange("p (f c) -> p f c", c=S))

        @block.scalar
        def _(act):
            act.wait_ge(const_loaded, 64)
            act.activation(crow[:, :], crow[:, :], ACT.Silu).then_inc(csilu, 1)

        @block.tensor
        def _(pe):
            ident = const(k, "ident")
            pe.wait_ge(const_loaded, 64)
            pe.wait_ge(loaded, 32)
            for f in range(KD):
                for half in range(2):
                    i = 2 * f + half
                    if i >= 2:
                        pe.wait_ge(moved, i - 1)
                    for j in range(4):
                        last = pe.transpose(tp[i % 2][:, 128 * j:128 * j + 128],
                                            xrow[:, 4 * half + j, 128 * f:128 * f + 128], ident)
                    last.then_inc(turned, 1)
            pe.wait_ge(csilu, 1)
            for f in range(KD):
                pe.matmul(cp[:, 9 * f:9 * f + 9], crow[:, 128 * f:128 * f + 128], ident[0:9, 0:9], start=True, stop=True)
                last = pe.matmul(cp[:, 128 + S * f:128 + S * f + S], xrow[0:S, NC8, 128 * f:128 * f + 128],
                                 ident[0:S, 0:S], start=True, stop=True)
            last.then_inc(cturned, 1)


V_ADA, V_NORM, V_CB, V_LG, V_LB, V_GN = 0, 48, 80, 82, 84, 86


def block_modulation(k, L):
    nc, d = k.nc, k.dram
    W = 512
    STEPS = 4
    with ExitStack() as ctx:
        sb = lambda n, s, t=F32: ctx.enter_context(nc.sbuf_tensor(n, s, t))
        ps = lambda n, s, t=F32: ctx.enter_context(nc.psum_tensor(n, s, t))
        wada = [sb(f"wada{i}", [P, KD, W]) for i in range(STEPS)]
        mrow = [sb(f"mrow{i}", [P, W]) for i in range(2)]
        vrow = sb("vrow", [P, 4, P])
        sq = [sb(f"msq{i}", [P, NT]) for i in range(2)]
        acc = sb("macc", [P, NT])
        v, t = sb("mv", [P, TC]), sb("mt", [P, TC])
        vp, st = ps("vp", [P, BANK]), ps("mst", [P, BANK])
        mp = [ps(f"mp{i}", [P, BANK]) for i in range(2)]
        tp = [ps(f"mtp{i}", [P, BANK]) for i in range(2)]
        w_loaded = [k.sem(f"w_loaded{i}") for i in range(STEPS)]
        (product_done, row_ready, turned, added, rows_loaded, rows_turned, scaled, passed, sq_ready, summed, sums_ready,
         link_v) = (k.sem(n) for n in ("product_done", "row_ready", "turned", "added", "rows_loaded", "rows_turned", "scaled",
                                       "passed_m", "sq_ready", "summed", "sums_ready", "link_v"))
        block = ctx.enter_context(nc.Block())

        @block.sync
        def _(sp):
            def rows(dst, src):
                sp.dma_start(dst, src).then_inc(rows_loaded, 16)

            ada = d["ada_w"][L].rearrange("(k p) n -> p k n", p=P)
            rows(vrow[0:48, 0, :], d["ada_b"][L].rearrange("(r p) -> r p", p=P))
            rows(vrow[48:80, 0, :], d["norms"][L].rearrange("a (r p) -> (a r) p", p=P))
            for i, n in enumerate(("conv_b", "conv_ln_g", "conv_ln_b", "ret_gn_g")):
                rows(vrow[80 + 2 * i:82 + 2 * i, 0, :], d[n][L].rearrange("(r p) -> r p", p=P))
            rows(vrow[0:2 * CONV_W, 1, :], d["conv_w"][L].rearrange("w (r p) -> (w r) p", p=P))
            rows(vrow[0:88, 2, :], d["ffn_conv_w"][L, 0:2].rearrange("w (r p) -> (w r) p", p=P))
            rows(vrow[0:44, 3, :], d["ffn_conv_w"][L, 2].rearrange("(r p) -> r p", p=P))
            rows(vrow[44:88, 3, :], d["ffn_conv_b"][L].rearrange("(r p) -> r p", p=P))
            with sp.Fori(0, 6 * D_MODEL // (STEPS * W)) as i:
                for s in range(STEPS):
                    gated(sp, product_done, i * STEPS + (s + 1), passed)
                    sp.dma_start(wada[s][:, :, :], ada[:, :, bass.ds((i * STEPS + s) * W, W)]).then_inc(w_loaded[s], 16)

        @block.tensor
        def _(pe):
            for s in range(STEPS):
                pe.sem_inc(product_done, 1)
            pe.wait_ge(rows_loaded, 160)
            for j, n in enumerate((88, 2 * CONV_W, 88, 88)):
                last = pe.matmul(vp[:, 128 * j:128 * j + n], vrow[0:n, j, :], const(k, "ident")[0:n, 0:n],
                                 start=True, stop=True)
            last.then_inc(rows_turned, 1)
            pe.wait_ge(summed, KD - 1)
            pe_token_sums(k, pe, st, acc, True, True).then_inc(sums_ready, 1)

            def turn(i, s):
                gated(pe, row_ready, i * STEPS + (s + 3), passed)
                gated(pe, added, i * STEPS + (s + 1), passed)
                for j in range(4):
                    last = pe.transpose(tp[s % 2][:, P * j:P * j + P], mrow[s % 2][:, P * j:P * j + P], const(k, "ident"))
                last.then_inc(turned, 1)

            with pe.Fori(0, 6 * D_MODEL // (STEPS * W)) as i:
                for s in range(STEPS):
                    gated(pe, w_loaded[s], i * 16 + 16, passed)
                    gated(pe, row_ready, i * STEPS + (s + 1), passed)
                    for kk in range(KD):
                        last = pe.matmul(mp[s % 2][0:1 + S, :], k.cT[:, kk, :], wada[s][:, kk, :], start=(kk == 0), stop=(kk == KD - 1))
                    last.then_inc(product_done, 1)
                    if s >= 1:
                        turn(i, s - 1)
                turn(i, STEPS - 1)

        @block.scalar
        def _(act):
            act_squares(k, act, k.x, sq, sq_ready, summed)
            act.wait_ge(k.zeroed, 2)
            act.sem_inc(row_ready, 1)
            act.sem_inc(row_ready, 1)
            with act.Fori(0, 6 * D_MODEL // (STEPS * W)) as i:
                for s in range(STEPS):
                    gated(act, product_done, i * STEPS + (s + 1 + STEPS), passed)
                    gated(act, added, i * STEPS + (s + 1), passed)
                    act.activation(mrow[s % 2][0:1 + S, :], mp[s % 2][0:1 + S, :], ACT.Copy).then_inc(row_ready, 1)

        @block.gpsimd
        def _(pool):
            for i in range(2):
                pool.memset(mrow[i][:, :], 0.0).then_inc(k.zeroed, 1)

        @block.vector
        def _(dve):
            link = Link(dve, link_v)
            dve.sem_inc(added, 1)
            dve.sem_inc(added, 1)
            dve_sum(k, dve, sq, acc, sq_ready, summed)
            dve.wait_ge(rows_turned, 1)
            for j, n in enumerate((88, 2 * CONV_W, 88, 88)):
                dve.tensor_copy(k.vecs[:, j, 0:n], vp[:, 128 * j:128 * j + n]).then_inc(scaled, 1)
            dve.wait_ge(sums_ready, 1)
            dve_inverse_rms(k, dve, link, st, v, t)
            dve.wait_ge(scaled, 4)
            with dve.Fori(0, 6 * D_MODEL // (STEPS * W)) as i:
                for s in range(STEPS):
                    gated(dve, turned, i * STEPS + (s + 1), passed)
                    part, at = i * 2 + s // 2, 4 * (s % 2)
                    bias = k.vecs[:, 0, 0:48].rearrange("p (a b) -> p a b", a=6)[:, bass.ds(part, 1), at:at + 4]
                    dve.tensor_tensor(k.mod[:, bass.ds(part, 1), at:at + 4, :].rearrange("p o a b -> p (o a) b"),
                                      tp[s % 2][:, :].rearrange("p (a b) -> p a b", b=P)[:, :, 0:1 + S],
                                      bias.rearrange("p o a -> p (o a)").unsqueeze(2).to_broadcast([P, 4, 1 + S]),
                                      ALU.add).then_inc(added, 1)
            dve.wait_ge(added, 2 + 6 * D_MODEL // W)
            for part, row, plus in ((1, 0, 1.0), (2, 1, 0.0), (4, 2, 1.0), (5, 3, 0.0)):
                gain = bc(k.vecs[:, 0, V_NORM + 8 * row:V_NORM + 8 * row + 8], 2, 9)
                dve.scalar_tensor_tensor(k.mod[:, part], k.mod[:, part], plus, gain, ALU.add, ALU.mult)


def act_squares(k, act, src, sq, sq_ready, summed):
    for kk in range(KD):
        if kk >= 2:
            act.wait_ge(summed, max(1, kk - 2))
        act.activation(sq[kk % 2][:, :], src[:, kk, :], ACT.Square).then_inc(sq_ready, 1)


def dve_sum(k, dve, sq, acc, sq_ready, summed):
    for kk in range(1, KD):
        dve.wait_ge(sq_ready, kk + 1)
        if kk > 1:
            dve.wait_ge(summed, kk - 1)
        dve.tensor_tensor(acc[:, :], sq[0][:, :] if kk == 1 else acc[:, :], sq[kk % 2][:, :], ALU.add).then_inc(summed, 1)


def pe_token_sums(k, pe, st, tile, first, final):
    for c in range(TC):
        w = min(P, NT - c * P)
        last = pe.matmul(st[0:w, c:c + 1], tile[:, c * P:c * P + w], const(k, "ones")[:, 0:1],
                         start=(first and c == 0), stop=final, skip_group_check=True)
    return last


def dve_row_scale(k, dve, link, st, n, v, y, t, scale):
    link(dve.memset(v[:, :], 1.0))
    link(dve.tensor_scalar(v[:, 0:NC8 * n], st[:, 0:NC8 * n], scale, EPS, ALU.mult, ALU.add))
    link(dve.tensor_scalar(v[0:S, NC8 * n:TC * n], st[0:S, NC8 * n:TC * n], scale, EPS, ALU.mult, ALU.add))
    rsqrt(dve, link, y[:, :], v[:, :], t[:, :])


def dve_inverse_rms(k, dve, link, st, v, t):
    dve_row_scale(k, dve, link, st, 1, v, k.inv, t, 1.0 / D_MODEL)


POOL_ADDS = (0, 2, 4, 6)
POOL_LOWS = (1, 3, 5)
PE_SUMS = (0, 2, 6, 7)
ACC_FIRST = 1


def block_join(k, L, tag, gate=None, shift=None, scale=None, tiles=None):
    nc = k.nc
    residual, norm = gate is not None, scale is not None
    both = residual and norm
    with ExitStack() as ctx:
        sb = lambda n, s, t=F32: ctx.enter_context(nc.sbuf_tensor(n + tag, s, t))
        ps = lambda n, s, t=F32: ctx.enter_context(nc.psum_tensor(n + tag, s, t))
        sq = [sb(f"sq{i}", [P, NT]) for i in range(2)]
        acc = sb("acc", [P, NT])
        h = [sb(f"h{i}", [P, TP]) for i in range(3)]
        hs = sb("hs", [P, KD, S])
        diag = sb("diag", [P, TC, P])
        v, t = sb("v", [P, TC]), sb("t", [P, TC])
        st, rb = ps("st", [P, BANK]), ps("rb", [P, SLOT])
        (diag_ready, rb_ready, samp, scaled, dve_added, pool_added, sq_ready, pe_used, acc_done, sums_ready, link_v, h_scaled,
         h_shifted, hi_done, dve_low, pool_low, hs_link, hs_hi) = (k.sem(n + tag) for n in (
             "diag_ready", "rb_ready", "samp", "scaled", "dve_added", "pool_added", "sq_ready", "pe_used", "acc_done",
             "sums_ready", "link_v", "h_scaled", "h_shifted", "hi_done", "dve_low", "pool_low", "hs_link", "hs_hi"))
        ahead = Ahead(k, tiles) if tiles is not None else None
        block = ctx.enter_context(nc.Block())
        ringed = [kk for kk in range(KD) if kk != ACC_FIRST]
        dve_sums = [kk for kk in ringed if kk not in PE_SUMS]
        cols = slice(OFF, OFF + TP)
        tail = slice(OFF + TP, OFF + NT)

        def square(kk):
            return acc if kk == ACC_FIRST else sq[ringed.index(kk) % 2]

        def added(e, kk):
            if kk in POOL_ADDS:
                e.wait_ge(pool_added, POOL_ADDS.index(kk) + 1)
            else:
                e.wait_ge(dve_added, kk + 1 - sum(p < kk for p in POOL_ADDS))

        def lowered(e, kk):
            if kk in POOL_LOWS:
                e.wait_ge(pool_low, POOL_LOWS.index(kk) + 1)
            else:
                e.wait_ge(dve_low, kk + 1 - sum(p < kk for p in POOL_LOWS))

        @block.sync
        def _(sp):
            if ahead:
                ahead.load(sp)

        @block.tensor
        def _(pe):
            def spread(n):
                pe.wait_ge(diag_ready, n)
                flat = diag[:, :, :].rearrange("p a b -> p (a b)")
                for a, b in CHUNKS:
                    last = pe.matmul(rb[:, OFF + a:OFF + b], const(k, "ones"), flat[:, a:b], start=True, stop=True)
                last.then_inc(rb_ready, 1)

            spread(1)
            if both:
                for n, kk in enumerate(PE_SUMS):
                    if n == len(PE_SUMS) - 1:
                        pe.wait_ge(acc_done, len(dve_sums))
                        pe_token_sums(k, pe, st, acc, False, False)
                    pe.wait_ge(sq_ready, kk + 1)
                    last = pe_token_sums(k, pe, st, square(kk), n == 0, n == len(PE_SUMS) - 1)
                    last.then_inc(sums_ready if n == len(PE_SUMS) - 1 else pe_used, 1)
                spread(2)

        @block.gpsimd
        def _(pool):
            if residual:
                for kk in POOL_ADDS:
                    pool.wait_ge(scaled, kk + 1)
                    pool.tensor_tensor(k.x[:, kk, 0:TP], k.x[:, kk, 0:TP], k.cat[:, kk, 0:TP], ALU.add).then_inc(pool_added, 1)
            if ahead:
                ahead.low(pool)
            if norm:
                for n, kk in enumerate(POOL_LOWS):
                    pool.wait_ge(hi_done, kk + 1)
                    pool.tensor_tensor(k.h_lo[:, kk, 0:TP], h[kk % 3][:, :], k.h_hi[:, kk, 0:TP].bitcast(F32),
                                       ALU.subtract).then_inc(pool_low, 1)

        @block.scalar
        def _(act):
            if ahead:
                ahead.high(act)
            if both:
                act.wait_ge(samp, 3)
                for kk in range(KD):
                    added(act, kk)
                    if kk != ACC_FIRST and ringed.index(kk) >= 2:
                        before = ringed[ringed.index(kk) - 2]
                        if before in PE_SUMS:
                            act.wait_ge(pe_used, PE_SUMS.index(before) + 1)
                        else:
                            act.wait_ge(acc_done, dve_sums.index(before) + 1)
                    act.activation(square(kk)[:, :], k.x[:, kk, :], ACT.Square).then_inc(sq_ready, 1)
            if norm:
                act.wait_ge(hs_link, 3)
                act.activation(k.h_hi[:, :, TP:NT], hs[:, :, :], ACT.Copy).then_inc(hs_hi, 1)
                for kk in range(KD):
                    act.wait_ge(h_scaled, kk + 1)
                    ht, hi, bias = h[kk % 3][:, :], k.h_hi[:, kk, 0:TP], k.mod[:, shift, kk, 0:1]
                    if kk in POOL_LOWS:
                        act.activation(ht, ht, ACT.Identity, bias=bias).then_inc(h_shifted, 1)
                        act.wait_ge(h_shifted, POOL_LOWS.index(kk) + 1)
                        act.activation(hi, ht, ACT.Copy).then_inc(hi_done, 1)
                    else:
                        act.activation(hi, ht, ACT.Identity, bias=bias).then_inc(hi_done, 1)

        @block.vector
        def _(dve):
            link = Link(dve, link_v)

            def spread():
                dve.tensor_tensor(diag[:, :, :], bc(const(k, "ident"), 1, TC), bc(k.inv[:, :], 2, P), ALU.mult).then_inc(diag_ready, 1)

            spread()
            if residual:
                ys, xs = k.cat[:, :, TP:NT], k.x[:, :, TP:NT]
                dve.tensor_tensor(ys, ys, k.mod[:, gate, :, 1:9], ALU.mult).then_inc(samp, 1)
                dve.wait_ge(samp, 1)
                dve.wait_ge(rb_ready, 1)
                dve.tensor_tensor(ys, ys, bc(rb[:, tail], 1, KD), ALU.mult).then_inc(samp, 1)
                dve.wait_ge(samp, 2)
                dve.tensor_tensor(xs, xs, ys, ALU.add).then_inc(samp, 1)

                def finish(kk):
                    if kk in range(KD) and kk not in POOL_ADDS:
                        dve.wait_ge(scaled, kk + 1)
                        dve.tensor_tensor(k.x[:, kk, 0:TP], k.x[:, kk, 0:TP], k.cat[:, kk, 0:TP], ALU.add).then_inc(dve_added, 1)
                    if both and kk - 2 in dve_sums:
                        dve.wait_ge(sq_ready, kk - 1)
                        if kk - 2 != dve_sums[0]:
                            dve.wait_ge(acc_done, dve_sums.index(kk - 2))
                        dve.tensor_tensor(acc[:, :], acc[:, :], square(kk - 2)[:, :], ALU.add).then_inc(acc_done, 1)

                for kk in range(KD + 1):
                    if kk < KD:
                        y = k.cat[:, kk, 0:TP]
                        dve.scalar_tensor_tensor(y, y, k.mod[:, gate, kk, 0:1], rb[:, cols], ALU.mult, ALU.mult).then_inc(scaled, 1)
                    finish(kk - 1)
            if both:
                dve.wait_ge(sums_ready, 1)
                dve_inverse_rms(k, dve, link, st, v, t)
                spread()
            if norm:
                slink = Link(dve, hs_link)
                dve.wait_ge(rb_ready, 2 if both else 1)
                slink(dve.tensor_tensor(hs[:, :, :], k.x[:, :, TP:NT], bc(rb[:, tail], 1, KD), ALU.mult))
                slink(dve.tensor_tensor(hs[:, :, :], hs[:, :, :], k.mod[:, scale, :, 1:9], ALU.mult))
                slink(dve.tensor_tensor(hs[:, :, :], hs[:, :, :], k.mod[:, shift, :, 1:9], ALU.add))
                for kk in range(KD + 1):
                    if kk < KD:
                        if kk >= 3:
                            lowered(dve, kk - 3)
                        dve.scalar_tensor_tensor(h[kk % 3][:, :], k.x[:, kk, 0:TP], k.mod[:, scale, kk, 0:1], rb[:, cols],
                                                 ALU.mult, ALU.mult).then_inc(h_scaled, 1)
                    if kk >= 1 and kk - 1 not in POOL_LOWS:
                        dve.wait_ge(hi_done, kk)
                        dve.scalar_tensor_tensor(k.h_lo[:, kk - 1, 0:TP], h[(kk - 1) % 3][:, :], k.mod[:, shift, kk - 1, 0:1],
                                                 k.h_hi[:, kk - 1, 0:TP].bitcast(F32), ALU.add, ALU.subtract).then_inc(dve_low, 1)
                dve.wait_ge(hs_hi, 1)
                dve.tensor_tensor(k.h_lo[:, :, TP:NT], hs[:, :, :], k.h_hi[:, :, TP:NT].bitcast(F32), ALU.subtract)


def block_project(k, L):
    nc, d = k.nc, k.dram
    tiles = [COL_CA, COL_CA + DC, COL_CA + P, COL_CA + DC + P] + [COL_BQ + P * j for j in range(8)]
    with ExitStack() as ctx:
        sb = lambda n, s, t=F32: ctx.enter_context(nc.sbuf_tensor(n, s, t))
        ps = lambda n, s, t=F32: ctx.enter_context(nc.psum_tensor(n, s, t))
        rope = sb("rope", [P, 2, NT])
        swap = sb("swap", [P, NT])
        u = sb("u", [P, 2, CTX + NT])
        sig = ft = swap
        bf = sb("bf", [P, HA])
        z, za = sb("z", [P, TC * HA]), sb("za", [P, TC * HA])
        crow = sb("ctxrow", [120, 2, DC])
        cctx = sb("cctx", [P, 2, 2 * 120])
        cprod = sb("cprod", [P, S, CTX])
        csum = sb("csum", [P, S])
        tail = sb("tail", [38, DC])
        slot = [ps(f"slot{i}", [P, SLOT]) for i in range(2)]
        misc = [ps(f"misc{i}", [P, 512]) for i in range(2)]
        raw_ready = [k.sem("raw_ready0"), k.sem("raw_ready1")]
        free = [k.sem("free0"), k.sem("free1")]
        (hi_done, lo_done, tile_done, side_loaded, f_done, z_link, conv_link, rope_raw,
         rope_swapped, rope_link, tail_turned, tail_done, ctx_turned, stored, passed, logf_ready, act_link) = (k.sem(n) for n in (
             "hi_done", "lo_done", "tile_done", "side_loaded", "f_done", "z_link",
             "conv_link", "rope_raw", "rope_swapped", "rope_link", "tail_turned", "tail_done", "ctx_turned", "stored",
             "passed_p", "logf_ready", "act_link"))
        block = ctx.enter_context(nc.Block())
        nt = len(tiles)
        ring = lambda m: (m + 1) % 2

        @block.sync
        def _(sp):
            w_in = d["w_in"][L].rearrange("(k p) n -> p k n", p=P)
            for m, col in enumerate([COL_F] + tiles):
                if m >= 2:
                    sp.wait_ge(lo_done, m - 1)
                    sp.dma_start(k.w_raw[ring(m)][:, :, :], w_in[:, :, col:col + P]).then_inc(raw_ready[ring(m)], 16)
                if m == 1:
                    sp.dma_start(bf[:, :], d["b_f"][L].unsqueeze(0).to_broadcast([P, HA])).then_inc(side_loaded, 16)
                    sp.dma_start(rope[:, :, :], d["rope"].rearrange("p (a n) -> p a n", a=2)).then_inc(side_loaded, 16)
                    for half in range(2):
                        sp.dma_start(crow[:, half, :], d["state_conv"][L, 4 * half:4 * half + 4].rearrange(
                            "s r c -> (s r) c")).then_inc(side_loaded, 16)
            sp.dma_start(d["conv_sample"][L, :, 0:CTX - 1, :], d["state_conv"][L, :, 1:CTX, :]).then_inc(stored, 16)
            sp.wait_ge(tail_done, 1)
            sp.dma_start(d["conv_prompt"][L, 0], tail[0:CTX, :]).then_inc(stored, 16)
            sp.dma_start(d["conv_sample"][L, :, CTX - 1, :], tail[CTX:CTX + S, :]).then_inc(stored, 16)
            sp.wait_ge(logf_ready, 1)
            sp.dma_start(d["logf_prompt"][L, 0, 0:7 * P].rearrange("(c p) h -> p c h", p=P),
                         k.logf[:, 0:7 * HA].rearrange("p (c h) -> p c h", h=HA)).then_inc(stored, 16)
            sp.dma_start(d["logf_prompt"][L, 0, 7 * P:TP], k.logf[:, 7 * HA:8 * HA]).then_inc(stored, 16)
            sp.dma_start(d["logf_sample"][L, :, 0, :], k.logf[120:128, 8 * HA:9 * HA]).then_inc(stored, 16)
            sp.wait_ge(stored, 96)

        @block.gpsimd
        def _(pool):
            pool.sem_inc(lo_done, 1)
            pool.sem_inc(lo_done, 1)
            for m in range(2, 1 + nt):
                pool.wait_ge(hi_done, m - 1)
                pool.wait_ge(tile_done, m - 1)
                w = ring(m)
                pool.tensor_tensor(k.w_lo[w][:, :, :], k.w_raw[w][:, :, :], k.w_hi[w][:, :, :].bitcast(F32),
                                   ALU.subtract).then_inc(lo_done, 1)

        @block.tensor
        def _(pe):
            ident = const(k, "ident")
            pe.wait_ge(lo_done, 1)
            product3(pe, slot[1], k.w_hi[1], k.w_lo[1], k.h_hi, k.h_lo, KD, slice(0, P)).then_inc(tile_done, 1)
            pe.wait_ge(side_loaded, 64)
            for half in range(2):
                for j in range(2):
                    last = pe.matmul(misc[1][:, 240 * j + 120 * half:240 * j + 120 * half + 120],
                                     crow[:, half, P * j:P * j + P], ident[0:120, 0:120], start=True, stop=True)
            last.then_inc(ctx_turned, 1)
            pe.wait_ge(free[1], 2)
            for c in range(TC):
                at = c * P if c < NC8 else NT - P
                last = pe.matmul(misc[0][:, HA * c:HA * c + HA], ft[0:HA, at:at + P], ident[0:HA, 0:HA], start=True, stop=True)
            last.then_inc(f_done, 1)
            with pe.Fori(0, nt // 2) as i:
                for s in range(2):
                    gated(pe, lo_done, i * 2 + (s + 2), passed)
                    gated(pe, free[s], i + (s + 1), passed)
                    product3(pe, slot[s], k.w_hi[s], k.w_lo[s], k.h_hi, k.h_lo, KD, slice(0, P)).then_inc(tile_done, 1)
            pe.wait_ge(free[0], 3)
            pe.wait_ge(z_link, 1)
            for j in range(2):
                last = pe.matmul(misc[0][0:38, 128 + P * j:128 + P * j + P], u[:, j, TP:TP + 38], ident, start=True, stop=True)
            last.then_inc(tail_turned, 1)

        @block.scalar
        def _(act):
            act.sem_inc(free[1], 1)

            def hi(m):
                act.wait_ge(raw_ready[ring(m)], 16 * (m // 2))
                act.wait_ge(tile_done, m - 1)
                act.activation(k.w_hi[ring(m)][:, :, :], k.w_raw[ring(m)][:, :, :], ACT.Copy).then_inc(hi_done, 1)

            act.wait_ge(tile_done, 1)
            act.activation(ft[0:HA, :], slot[1][0:HA, OFF:OFF + NT], ACT.Copy).then_inc(free[1], 1)
            for i in range(nt):
                if i + 2 < 1 + nt:
                    hi(i + 2)
                s = i % 2
                res = slot[s][:, OFF:OFF + NT]
                act.wait_ge(tile_done, i + 2)
                if i == 1:
                    act.wait_ge(f_done, 1)
                if i in (1, 3):
                    if i == 3:
                        act.wait_ge(free[0], 2)
                    act.activation(sig[:, :], res, ACT.Sigmoid).then_inc(free[1], 1)
                    if i == 3:
                        act.wait_ge(z_link, 1)
                        act.activation(za[:, :], z[:, :], ACT.Abs).then_inc(act_link, 1)
                        act.wait_ge(act_link, 1)
                        act.activation(za[:, :], za[:, :], ACT.Exp, scale=-1.0).then_inc(act_link, 1)
                        act.wait_ge(act_link, 2)
                        act.activation(za[:, :], za[:, :], ACT.Ln, bias=1.0).then_inc(act_link, 1)
                elif 4 <= i < 8:
                    j, dst = i % 2, (k.q_ret if i < 6 else k.k_ret)
                    scale = 1.0 if i < 6 else DB ** -0.5
                    act.activation(dst[:, j, :], res, ACT.Copy, scale=scale).then_inc(act_link, 1)
                    if i > 4:
                        act.wait_ge(rope_link, 3 * (i - 4))
                    else:
                        act.wait_ge(free[0], 3)
                    for quad in range(4):
                        src = 32 * (quad ^ 1)
                        op = act.activation(swap[32 * quad:32 * quad + 32, :], res[src:src + 32, :], ACT.Copy, scale=scale)
                        if quad < 3:
                            op.then_inc(rope_raw, 1)
                        else:
                            op.then_inc(free[s], 1)
                elif 8 <= i < 10:
                    act.activation(k.v_ret[:, i % 2, :], res, ACT.Copy).then_inc(free[s], 1)
                elif i >= 10:
                    act.activation(k.cat[:, 4 + i % 2, :], res, ACT.Silu).then_inc(free[s], 1)
            act.wait_ge(tail_turned, 1)
            act.activation(tail[:, :], misc[0][0:38, 128:128 + DC], ACT.Copy).then_inc(tail_done, 1)

        @block.vector
        def _(dve):
            clink = Link(dve, conv_link)
            dve.sem_inc(free[0], 1)
            for j in range(2):
                clink(dve.memset(u[:, j, 0:CTX], 0.0))
            dve.wait_ge(f_done, 1)
            dve.tensor_tensor(z[:, :].rearrange("p (c h) -> p c h", h=HA),
                              misc[0][:, 0:TC * HA].rearrange("p (c h) -> p c h", h=HA), bc(bf[:, :], 1, TC),
                              ALU.add).then_inc(z_link, 1)
            def taps(lo, hi):
                for j, w in todo[lo:hi]:
                    acc = k.cat[:, 6 + j, 0:TP]
                    if w == 0:
                        clink(dve.tensor_scalar(acc, u[:, j, 0:TP], k.vecs[:, 1, j:j + 1],
                                                k.vecs[:, 0, V_CB + j:V_CB + j + 1], ALU.mult, ALU.add))
                    else:
                        clink(dve.scalar_tensor_tensor(acc, u[:, j, w:w + TP], k.vecs[:, 1, 2 * w + j:2 * w + j + 1],
                                                       acc, ALU.mult, ALU.add))

            todo = [(j, w) for j in range(2) for w in range(CONV_W)]
            for j in range(2):
                dve.wait_ge(free[1], 3 + j)
                dve.tensor_tensor(u[:, j, CTX:CTX + NT], slot[0][:, OFF:OFF + NT], sig[:, :], ALU.mult).then_inc(free[0], 1)
                dve.wait_ge(free[0], 2 + j)
                taps(*((0, 14) if j == 0 else (14, 18)))
            dve.wait_ge(act_link, 3)
            dve.scalar_tensor_tensor(k.logf[:, :], z[:, :], 0.0, za[:, :], ALU.min, ALU.subtract).then_inc(logf_ready, 1)
            at = 18
            for i in range(4, 8):
                j, dst = i % 2, (k.q_ret if i < 6 else k.k_ret)
                dve.wait_ge(act_link, i)
                dve.tensor_tensor(dst[:, j, :], dst[:, j, :], rope[:, 0, :], ALU.mult).then_inc(rope_link, 1)
                dve.wait_ge(rope_raw, 3 * (i - 3))
                dve.wait_ge(free[i % 2], {4: 4, 5: 5, 6: 5, 7: 6}[i])
                dve.tensor_tensor(swap[:, :], swap[:, :], rope[:, 1, :], ALU.mult).then_inc(rope_link, 1)
                dve.wait_ge(rope_link, 3 * (i - 4) + 2)
                dve.tensor_tensor(dst[:, j, :], dst[:, j, :], swap[:, :], ALU.add).then_inc(rope_link, 1)
                taps(at, at + 8)
                at += 8
            taps(at, len(todo))
            dve.wait_ge(ctx_turned, 1)
            clink(dve.tensor_copy(cctx[:, :, :], misc[1][:, 0:480].rearrange("p (j n) -> p j n", j=2)))
            for j in range(2):
                w = k.vecs[:, 1, j:j + 2 * CTX:2]
                clink(dve.tensor_tensor(cprod[:, :, :], cctx[:, j, :].rearrange("p (s r) -> p s r", s=S), bc(w, 1, S), ALU.mult))
                clink(dve.tensor_reduce(csum[:, :], cprod[:, :, :], AX_X, ALU.add))
                clink(dve.scalar_tensor_tensor(csum[:, :], u[:, j, CTX + TP:CTX + NT], k.vecs[:, 1, 2 * CTX + j:2 * CTX + j + 1],
                                               csum[:, :], ALU.mult, ALU.add))
                clink(dve.tensor_scalar(k.cat[:, 6 + j, TP:NT], csum[:, :], k.vecs[:, 0, V_CB + j:V_CB + j + 1], None, ALU.add))


def block_retention(k, L):
    nc, d = k.nc, k.dram
    with ExitStack() as ctx:
        sb = lambda n, s, t=F32: ctx.enter_context(nc.sbuf_tensor(n, s, t))
        state = sb("state", [P, 2, DB])
        kz = [sb(f"kz{i}", [P, 2 * P]) for i in range(2)]
        vt = [sb(f"vt{i}", [P, 2 * P]) for i in range(2)]
        att = [sb(f"att{i}", [P, 2, 2 * P]) for i in range(2)]
        qxi = [sb(f"qxi{i}", [P, 2, P]) for i in range(2)]
        s0 = sb("s0", [P, 2, S, DB])
        vst = sb("vst", [P, 2 * S, DB])
        small = sb("small", [P, 2, 2 * S])
        pre = sb("pre", [P, NC8 * HA])
        ps = lambda n, s: ctx.enter_context(nc.psum_tensor(n, s, F32))
        kv_bank = [ps(f"kv_bank{i}", [P, 512]) for i in range(2)]
        sc_bank = [ps(f"sc_bank{i}", [P, 1024]) for i in range(2)]
        o_bank, up_bank = ps("o_bank", [P, 512]), ps("up_bank", [P, 512])
        (state_loaded, turned, scored, kz_done, kv_moved, att_done, qxi_done, o_ready, up_ready, state_done, r_moved,
         pre_link, cum_ready, qk_ready, vst_ready, samp_ready, samp_link, stored) = (k.sem(n) for n in (
             "state_loaded", "turned", "scored", "kz_done", "kv_moved", "att_done", "qxi_done", "o_ready", "up_ready",
             "state_done", "r_moved", "pre_link", "cum_ready", "qk_ready", "vst_ready", "samp_ready", "samp_link", "stored"))
        qr, kr, vr = k.q_ret, k.k_ret, k.v_ret
        block = ctx.enter_context(nc.Block())

        @block.sync
        def _(sp):
            for hh in range(2):
                sp.dma_start(s0[:, hh, :, :], d["state_ret"][L, :, 2 * hh:2 * hh + 2].rearrange(
                    "s h d e -> (h d) s e")).then_inc(state_loaded, 16)
            sp.wait_ge(state_done, 1 + NC8)
            for hh in range(2):
                sp.dma_start(d["ret_prompt"][L, 0, 2 * hh:2 * hh + 2].rearrange("h d e -> (h d) e"),
                             state[:, hh, :]).then_inc(stored, 16)
            sp.wait_ge(samp_link, 5)
            for hh in range(2):
                sp.dma_start(d["ret_sample"][L, :, 2 * hh:2 * hh + 2].rearrange("s h d e -> (h d) s e"),
                             s0[:, hh, :, :]).then_inc(stored, 16)
            sp.wait_ge(stored, 64)

        @block.tensor
        def _(pe):
            ident, pair = const(k, "ident"), const(k, "pair")

            def front(c):
                b = c % 2
                if c >= 2:
                    pe.wait_ge(kv_moved, c - 1)
                    pe.wait_ge(att_done, c - 1)
                at = slice(P * c, P * c + P)
                for n, src in enumerate((kr, vr)):
                    for hh in range(2):
                        last = pe.transpose(kv_bank[b][:, 256 * n + P * hh:256 * n + P * hh + P], src[:, hh, at], ident)
                last.then_inc(turned, 1)
                for hp in range(2):
                    rows = slice(64 * hp, 64 * hp + 64)
                    for hh in range(2):
                        last = pe.matmul(sc_bank[b][:, 512 * hp + P * hh:512 * hp + P * hh + P], kr[rows, hh, at],
                                         qr[rows, hh, at], start=True, stop=True)
                last.then_inc(scored, 1)

            def back(c):
                b = c % 2
                pe.wait_ge(kv_moved, c + 1)
                pe.wait_ge(att_done, c + 1)
                pe.wait_ge(qxi_done, c + 1)
                pe.wait_ge(state_done, c + 1)
                if c >= 1:
                    pe.wait_ge(r_moved, c)
                for hh in range(2):
                    for hp in range(2):
                        rows = slice(64 * hp, 64 * hp + 64)
                        out = o_bank[rows, P * hh:P * hh + P]
                        pe.matmul(out, vt[b][:, P * hh + 64 * hp:P * hh + 64 * hp + 64],
                                  att[b][:, hp, P * hh:P * hh + P], start=True, stop=False)
                        last = pe.matmul(out, state[rows, hh, :], qxi[b][rows, hh, :], start=False, stop=True)
                last.then_inc(o_ready, 1)
                for hh in range(2):
                    for hp in range(2):
                        cols = slice(P * hh + 64 * hp, P * hh + 64 * hp + 64)
                        last = pe.matmul(up_bank[64 * hp:64 * hp + 64, 64 * hh:64 * hh + 64], kz[b][:, cols], vt[b][:, cols],
                                         start=True, stop=True)
                last.then_inc(up_ready, 1)

            front(0)
            for c in range(NC8):
                if c + 1 < NC8:
                    front(c + 1)
                back(c)
            pe.wait_ge(pre_link, NC8)
            pe.wait_ge(kv_moved, NC8)
            pe.matmul(kv_bank[0][:, 0:NC8 * HA], const(k, "upto"), k.logf[:, 0:NC8 * HA], start=True, stop=False)
            pe.matmul(kv_bank[0][:, 0:NC8 * HA], const(k, "ones"), pre[:, :], start=False, stop=True).then_inc(cum_ready, 1)
            pe.wait_ge(att_done, NC8)
            pe.wait_ge(qk_ready, 1)
            pe.matmul(kv_bank[1][:, 0:2 * S], pair, small[:, 0, :], start=True, stop=True)
            pe.wait_ge(vst_ready, 1)
            flat = vst[:, :, :].rearrange("p a b -> p (a b)")
            for n in range(2):
                pe.matmul(sc_bank[0][:, 512 * n:512 * n + 512], pair, flat[:, 512 * n:512 * n + 512], start=True, stop=True)
            pe.wait_ge(state_loaded, 32)
            pe.wait_ge(r_moved, NC8)
            for hh in range(2):
                for s in range(S):
                    for hp in range(2):
                        rows = slice(64 * hp, 64 * hp + 64)
                        last = pe.matmul(o_bank[rows, S * hh + s:S * hh + s + 1], s0[rows, hh, s, :],
                                         qr[rows, hh, TP + s:TP + s + 1], start=True, stop=True)
            last.then_inc(samp_ready, 1)

        @block.scalar
        def _(act):
            def values(c):
                act.wait_ge(kz_done, c + 1)
                if c >= 2:
                    act.wait_ge(up_ready, c - 1)
                act.activation(vt[c % 2][:, :], kv_bank[c % 2][:, 256:512], ACT.Copy).then_inc(kv_moved, 1)

            values(0)
            for c in range(NC8):
                if c + 1 < NC8:
                    values(c + 1)
                act.wait_ge(o_ready, c + 1)
                act.activation(qr[:, :, P * c:P * c + P], o_bank[:, 0:256].rearrange("p (a b) -> p a b", a=2),
                               ACT.Copy).then_inc(r_moved, 1)

        @block.vector
        def _(dve):
            plink, slink = Link(dve, pre_link), Link(dve, samp_link)
            zeta, decay, xi = const(k, "zeta"), const(k, "decay"), const(k, "xi")

            def prepare(c):
                b = c % 2
                dve.wait_ge(turned, c + 1)
                if c >= 2:
                    dve.wait_ge(up_ready, c - 1)
                dve.tensor_tensor(kz[b][:, :].rearrange("p (h e) -> p h e", h=HB),
                                  kv_bank[b][:, 0:256].rearrange("p (h e) -> p h e", h=HB), bc(zeta, 2, DB),
                                  ALU.mult).then_inc(kz_done, 1)
                dve.tensor_tensor(qxi[b][:, :, :], qr[:, :, P * c:P * c + P], xi.rearrange("p (a b) -> p a b", a=2),
                                  ALU.mult).then_inc(qxi_done, 1)
                dve.wait_ge(scored, c + 1)
                dve.tensor_tensor(att[b][:, :, :], sc_bank[b][:, :].rearrange("p (a b) -> p a b", a=2)[:, :, 0:256],
                                  decay.rearrange("p (a b) -> p a b", a=2), ALU.mult).then_inc(att_done, 1)

            dve.memset(state[:, :, :], 0.0).then_inc(state_done, 1)
            prepare(0)
            for c in range(NC8):
                if c + 1 < NC8:
                    prepare(c + 1)
                dve.wait_ge(up_ready, c + 1)
                for hh in range(2):
                    op = dve.scalar_tensor_tensor(state[:, hh, :], state[:, hh, :], const(k, "gchunk")[:, hh:hh + 1],
                                                  up_bank[:, 64 * hh:64 * hh + 64], ALU.mult, ALU.add)
                    if hh == 0:
                        op.then_inc(k.quiet, 1)
                    else:
                        op.then_inc(state_done, 1)
                dve.wait_ge(state_done, c + 2)
            plink(dve.memset(pre[:, 0:HA], 0.0))
            for c in range(1, NC8):
                plink(dve.tensor_tensor(pre[:, HA * c:HA * c + HA], pre[:, HA * c - HA:HA * c], k.logf[:, HA * c - HA:HA * c], ALU.add))
            dve.wait_ge(cum_ready, 1)
            dve.tensor_scalar(k.ncum[:, :], kv_bank[0][:, 0:NC8 * HA], -1.0 / A_SCALE, None, ALU.mult).then_inc(k.quiet, 1)
            ks, qs, vs = (b[:, :, TP:NT] for b in (kr, qr, vr))
            sq3 = lambda i: small[:, i, :].rearrange("p (a s) -> p a s", a=2)
            dve.tensor_tensor(sq3(0), qs, ks, ALU.mult).then_inc(qk_ready, 1)
            for hh in range(2):
                op = dve.tensor_tensor(vst[:, S * hh:S * hh + S, :], bc(const(k, "stack"), 1, S), bc(vs[:, hh, :], 2, DB), ALU.mult)
                op.then_inc(k.quiet, 1) if hh == 0 else op.then_inc(vst_ready, 1)
            dve.wait_ge(samp_ready, 1)
            slink(dve.tensor_tensor(sq3(1), kv_bank[1][:, 0:2 * S].rearrange("p (a s) -> p a s", a=2), vs, ALU.mult))
            for hh in range(2):
                dve.tensor_tensor(vst[:, S * hh:S * hh + S, :], sc_bank[0][:, 512 * hh:512 * hh + 512].rearrange(
                    "p (s e) -> p s e", s=S), bc(ks[:, hh, :], 2, DB), ALU.mult).then_inc(samp_link, 1)
            dve.wait_ge(samp_link, 3)
            for hh in range(2):
                dve.scalar_tensor_tensor(s0[:, hh, :, :], s0[:, hh, :, :], const(k, "gone")[:, hh:hh + 1],
                                         vst[:, S * hh:S * hh + S, :], ALU.mult, ALU.add).then_inc(samp_link, 1)
                dve.scalar_tensor_tensor(qr[:, hh, TP:NT], o_bank[:, S * hh:S * hh + S], const(k, "gone")[:, hh:hh + 1],
                                         small[:, 1, S * hh:S * hh + S], ALU.mult, ALU.add).then_inc(k.quiet, 1)


def block_group_norms(k, L):
    nc, d = k.nc, k.dram
    with ExitStack() as ctx:
        sb = lambda n, s, t=F32: ctx.enter_context(nc.sbuf_tensor(n, s, t))
        ps = lambda n, s: ctx.enter_context(nc.psum_tensor(n, s, F32))
        sq = [sb(f"gsq{i}", [P, NT]) for i in range(2)]
        diag = [sb(f"gdiag{i}", [P, TC, P]) for i in range(2)]
        n_st = TC * (HB + 1)
        v, y, t = (sb(n, [P, n_st]) for n in ("gv", "gy", "gt"))
        slot = [ps(f"gslot{i}", [P, SLOT]) for i in range(2)]
        st = ps("gst", [P, BANK])
        mean_ready, centred, sq_ready, sq_used, link_v, diag_ready, rb_ready, applied = (k.sem(n) for n in (
            "mean_ready", "centred", "sq_ready", "sq_used", "link_v", "diag_ready", "rb_ready", "applied"))
        tiles = [k.q_ret[:, 0, :], k.q_ret[:, 1, :], k.cat[:, 6, :], k.cat[:, 7, :]]
        block = ctx.enter_context(nc.Block())
        w_in = d["w_in"][L].rearrange("(k p) n -> p k n", p=P)
        ahead = Ahead(k, [w_in[:, :, 0:P], w_in[:, :, HA * DA:HA * DA + P]])
        v3 = lambda a: a[:, 0:TC * HB].rearrange("p (c h) -> p c h", h=HB)

        @block.sync
        def _(sp):
            ahead.load(sp)

        @block.gpsimd
        def _(pool):
            ahead.low(pool)

        @block.tensor
        def _(pe):
            ones, pair = const(k, "ones"), const(k, "pair")
            for j in range(2):
                for a, b in CHUNKS:
                    last = pe.matmul(slot[j][:, OFF + a:OFF + b], pair, tiles[j][:, a:b], start=True, stop=True)
                last.then_inc(mean_ready, 1)
            pe.wait_ge(centred, 1)
            for j in range(2):
                for a, b in CHUNKS:
                    last = pe.matmul(slot[0][:, OFF + a:OFF + b], ones, tiles[2 + j][:, a:b], start=(j == 0), stop=(j == 1))
            last.then_inc(mean_ready, 1)
            for n in range(4):
                pe.wait_ge(sq_ready, n + 1)
                for c in range(TC):
                    w = min(P, NT - c * P)
                    if n < 2:
                        out, rhs = st[0:w, HB * c + 2 * n:HB * c + 2 * n + 2], const(k, "headsel")
                    else:
                        out, rhs = st[0:w, TC * HB + c:TC * HB + c + 1], ones[:, 0:1]
                    last = pe.matmul(out, sq[n % 2][:, c * P:c * P + w], rhs, start=(n == 0 and c == 0), stop=True,
                                     skip_group_check=True)
                last.then_inc(sq_used, 1)
            for j in range(3):
                if j == 2:
                    pe.wait_ge(applied, 1)
                for hp in range(2 if j < 2 else 1):
                    n = 2 * j + hp
                    pe.wait_ge(diag_ready, n + 1)
                    flat = diag[n % 2][:, :, :].rearrange("p a b -> p (a b)")
                    for a, b in CHUNKS:
                        out = slot[j % 2][64 * hp:64 * hp + 64, OFF + a:OFF + b] if j < 2 else slot[0][:, OFF + a:OFF + b]
                        last = pe.matmul(out, ones[:, 0:64] if j < 2 else ones, flat[:, a:b], start=True, stop=True)
                    last.then_inc(rb_ready, 1)

        @block.scalar
        def _(act):
            ahead.high(act)
            for n in range(4):
                act.wait_ge(centred, (1, 2, 4, 4)[n])
                if n >= 2:
                    act.wait_ge(sq_used, n - 1)
                act.activation(sq[n % 2][:, :], tiles[n], ACT.Square).then_inc(sq_ready, 1)
            for j in range(2):
                act.wait_ge(applied, 5 + j)
                act.activation(k.cat[:, 6 + j, :], k.cat[:, 6 + j, :], ACT.Silu, scale=k.vecs[:, 0, V_LG + j:V_LG + j + 1],
                               bias=k.vecs[:, 0, V_LB + j:V_LB + j + 1]).then_inc(k.quiet, 1)

        @block.vector
        def _(dve):
            link = Link(dve, link_v)
            for j in range(2):
                dve.wait_ge(mean_ready, j + 1)
                dve.scalar_tensor_tensor(tiles[j], slot[j][:, OFF:OFF + NT], -1.0 / DB, tiles[j], ALU.mult, ALU.add).then_inc(centred, 1)
            dve.wait_ge(mean_ready, 3)
            for j in range(2, 4):
                dve.scalar_tensor_tensor(tiles[j], slot[0][:, OFF:OFF + NT], -1.0 / DC, tiles[j], ALU.mult, ALU.add).then_inc(centred, 1)
            dve.wait_ge(sq_used, 4)
            link(dve.memset(v[:, :], 1.0))
            for at, n, scale in ((0, HB, 1.0 / DB), (TC * HB, 1, 1.0 / DC)):
                link(dve.tensor_scalar(v[:, at:at + NC8 * n], st[:, at:at + NC8 * n], scale, EPS, ALU.mult, ALU.add))
                link(dve.tensor_scalar(v[0:S, at + NC8 * n:at + TC * n], st[0:S, at + NC8 * n:at + TC * n], scale, EPS,
                                       ALU.mult, ALU.add))
            rsqrt(dve, link, y[:, :], v[:, :], t[:, :])
            for n in range(HB + 1):
                if n >= 2:
                    dve.wait_ge(rb_ready, n - 1)
                row = v3(y)[:, :, n] if n < HB else y[:, TC * HB:n_st]
                dve.tensor_tensor(diag[n % 2][:, :, :], bc(const(k, "ident"), 1, TC), bc(row, 2, P), ALU.mult).then_inc(diag_ready, 1)
                if n in (2, 4):
                    j = n // 2 - 1
                    dve.wait_ge(rb_ready, 2 * j + 2)
                    dve.tensor_tensor(tiles[j], tiles[j], slot[j][:, OFF:OFF + NT], ALU.mult).then_inc(applied, 1)
                    dve.wait_ge(applied, 2 * j + 1)
                    dve.scalar_tensor_tensor(k.cat[:, 4 + j, :], tiles[j], k.vecs[:, 0, V_GN + j:V_GN + j + 1],
                                             k.cat[:, 4 + j, :], ALU.mult, ALU.mult).then_inc(applied, 1)
            dve.wait_ge(rb_ready, 5)
            for j in range(2):
                dve.tensor_tensor(tiles[2 + j], tiles[2 + j], slot[0][:, OFF:OFF + NT], ALU.mult).then_inc(applied, 1)


MOVES = [i if i <= 4 else 2 * i - 4 for i in range(NC8 + 1)]


def block_heads(k, L):
    nc, d = k.nc, k.dram
    with ExitStack() as ctx:
        sb = lambda n, s, t=F32: ctx.enter_context(nc.sbuf_tensor(n, s, t))
        ps = lambda n, s: ctx.enter_context(nc.psum_tensor(n, s, F32))
        q, kk_, v = sb("q", [P, NT]), sb("kf", [P, NT]), sb("vf", [P, NT])
        k_tok, v_tok = sb("k_tok", [P, NC8, P]), sb("v_tok", [P, NC8, P])
        bias = sb("bias", [P, TP])
        prob = [sb(f"prob{i}", [P, TP]) for i in range(2)]
        prob_t = sb("prob_t", [P, NC8, P])
        diag = prob_t
        kv_new = sb("kv_new", [S, 2, P])
        mx, nb, rs, rr = (sb(n, [P, 2]) for n in ("mx", "nb", "rs", "rr"))
        slot = [ps(f"hslot{i}", [P, SLOT]) for i in range(2)]
        misc = [ps(f"hmisc{i}", [P, 512]) for i in range(2)]
        raw_ready = [k.sem("raw_ready0"), k.sem("raw_ready1")]
        (hi_done, lo_done, tile_done, moved, turned, tok_moved, diag_ready, bias_ready, bias_moved, scored, top, neg, expd,
         summed, normed, p_turned, p_moved, o_ready, o_moved, stored, passed, begun) = (k.sem(n) for n in (
             "hi_done", "lo_done", "tile_done", "moved", "turned", "tok_moved", "diag_ready", "bias_ready", "bias_moved",
             "scored", "top", "neg", "expd", "summed", "normed", "p_turned", "p_moved", "o_ready", "o_moved", "stored",
             "passed_h", "begun"))
        block = ctx.enter_context(nc.Block())
        cols = [0, HA * DA, 2 * HA * DA]
        N_TILE, N_TOK, N_Q = 3, 5, NC8

        @block.sync
        def _(sp):
            w_in = d["w_in"][L].rearrange("(k p) n -> p k n", p=P)

            def load(h, t):
                gated(sp, lo_done, h * N_TILE + (t + 1 if t else 2), passed)
                sp.dma_start(k.w_raw[t % 2][:, :, :], w_in[:, :, bass.ds(h * DA + cols[t], DA)]).then_inc(raw_ready[t % 2], 16)

            def store(h):
                gated(sp, tok_moved, h * N_TOK + 5, passed)
                sp.dma_start(d["k_prompt"][L, 0, :, bass.ds(h, 1), :].rearrange("(c p) o n -> p c (o n)", p=P), k_tok[:, :, :]).then_inc(stored, 16)
                sp.dma_start(d["v_prompt"][L, 0, :, bass.ds(h, 1), :].rearrange("(c p) o n -> p c (o n)", p=P), v_tok[:, :, :]).then_inc(stored, 16)
                sp.dma_start(d["k_sample"][L, :, 0, bass.ds(h, 1), :].rearrange("s o n -> s (o n)"), kv_new[:, 0, :]).then_inc(stored, 16)
                sp.dma_start(d["v_sample"][L, :, 0, bass.ds(h, 1), :].rearrange("s o n -> s (o n)"), kv_new[:, 1, :]).then_inc(stored, 16)

            load(0, 2)
            store(0)
            with sp.Fori(0, HA - 1) as h:
                for t in range(3):
                    load(h + 1, t)
                store(h + 1)
            sp.wait_ge(stored, 64 * HA + 16)

        @block.gpsimd
        def _(pool):
            for _ in range(4):
                pool.sem_inc(lo_done, 1)

            def low(h, t):
                gated(pool, hi_done, h * N_TILE + (t + 1), passed)
                gated(pool, tile_done, h * N_TILE + (t + 1 if t else 2), passed)
                pool.tensor_tensor(k.w_lo[t % 2][:, :, :], k.w_raw[t % 2][:, :, :], k.w_hi[t % 2][:, :, :].bitcast(F32),
                                   ALU.subtract).then_inc(lo_done, 1)

            low(0, 2)
            with pool.Fori(0, HA - 1) as h:
                for t in range(3):
                    low(h + 1, t)

        @block.tensor
        def _(pe):
            ident, ones = const(k, "ident"), const(k, "ones")
            pe.sem_inc(tile_done, 1)
            pe.sem_inc(tile_done, 1)
            with pe.Fori(0, HA) as h:
                gated(pe, o_moved, h * N_Q + 1, passed)
                for t in range(3):
                    gated(pe, lo_done, h * N_TILE + (t + 3), passed)
                    if t == 2:
                        gated(pe, moved, h * 3 + 1, passed)
                    product3(pe, slot[t % 2], k.w_hi[t % 2], k.w_lo[t % 2], k.h_hi, k.h_lo, KD, slice(0, P)).then_inc(tile_done, 1)
                for n, src in enumerate((kk_, v)):
                    gated(pe, moved, h * 3 + (2 + n), passed)
                    for half in range(2):
                        if n == 1:
                            gated(pe, tok_moved, h * N_TOK + (1 + half), passed)
                        for j in range(4):
                            c = 4 * half + j
                            last = pe.transpose(misc[half][:, P * j:P * j + P], src[:, P * c:P * c + P], ident)
                        last.then_inc(turned, 1)
                for n, src in enumerate((kk_, v)):
                    last = pe.matmul(slot[0][0:S, P * n:P * n + P], src[:, TP:NT], ident, start=True, stop=True)
                last.then_inc(turned, 1)
                gated(pe, diag_ready, h + 1, passed)
                flat = diag[:, :, :].rearrange("p a b -> p (a b)")
                for a, b in HALVES:
                    last = pe.matmul(slot[1][:, a:b], ones, flat[:, a:b], start=True, stop=True)
                last.then_inc(bias_ready, 1)

                def scores(i):
                    if i == 0:
                        gated(pe, tok_moved, h * N_TOK + 5, passed)
                    elif i == 1:
                        gated(pe, bias_moved, h + 1, passed)
                    else:
                        gated(pe, top, h * N_Q + (i - 1), passed)
                    n = P * (i + 1)
                    pe.matmul(slot[i % 2][:, n - P:n], k.ident_bf[:, :], k.mask_bf[:, :], start=True, stop=False,
                              skip_group_check=True)
                    for a, b in HALVES:
                        if a < n:
                            last = pe.matmul(slot[i % 2][:, a:min(b, n)], q[:, P * i:P * i + P], kk_[:, a:min(b, n)],
                                             start=(b < n), stop=True, skip_group_check=True)
                    last.then_inc(scored, 1)

                scores(0)
                scores(1)
                for i in range(NC8):
                    gated(pe, normed, h * N_Q + (i + 1), passed)
                    banks = (i >= 4) + 1
                    for bank in range(banks):
                        if bank == 0 and i == 0:
                            gated(pe, tok_moved, h * N_TOK + 4, passed)
                        if bank == 1 and i == 4:
                            gated(pe, tok_moved, h * N_TOK + 4, passed)
                        for c in range(4 * bank, min(4 * bank + 4, i + 1)):
                            last = pe.transpose(misc[bank][:, P * (c % 4):P * (c % 4) + P], prob[i % 2][:, P * c:P * c + P], ident)
                        last.then_inc(p_turned, 1)
                    if i + 2 < NC8:
                        scores(i + 2)
                    gated(pe, p_moved, h * 12 + MOVES[i + 1], passed)
                    if i >= 2:
                        gated(pe, o_moved, h * N_Q + i, passed)
                    out = slot[i % 2][:, 1024:1024 + P]
                    for c in range(i + 1):
                        last = pe.matmul(out, v_tok[:, c, :], prob_t[:, c, :], start=(c == 0), stop=(c == i))
                    last.then_inc(o_ready, 1)

        @block.scalar
        def _(act):
            def hi(h, t):
                gated(act, raw_ready[t % 2], h * (32 if t % 2 == 0 else 16) + (32 if t == 2 else 16), passed)
                gated(act, tile_done, h * N_TILE + (t + 1 if t else 2), passed)
                act.activation(k.w_hi[t % 2][:, :, :], k.w_raw[t % 2][:, :, :], ACT.Copy).then_inc(hi_done, 1)

            def head(h, more):
                def move(t, dst):
                    gated(act, tile_done, h * N_TILE + (t + 3), passed)
                    act.activation(dst[:, :], slot[t % 2][:, OFF:OFF + NT], ACT.Copy).then_inc(moved, 1)

                move(0, q)
                hi(h, 2)
                move(1, kk_)
                move(2, v)
                gated(act, stored, h * 64 + 16, passed)
                for n, dst in enumerate((k_tok, v_tok)):
                    for half in range(2):
                        gated(act, turned, h * 5 + (2 * n + half + 1), passed)
                        act.activation(dst[:, 4 * half:4 * half + 4, :], misc[half][:, :].rearrange("p (c n) -> p c n", c=4),
                                       ACT.Copy).then_inc(tok_moved, 1)
                gated(act, turned, h * 5 + 5, passed)
                act.activation(kv_new[:, :, :], slot[0][0:S, 0:2 * P].rearrange("p (a n) -> p a n", a=2), ACT.Copy).then_inc(tok_moved, 1)
                gated(act, bias_ready, h + 1, passed)
                act.activation(bias[:, :], slot[1][:, 0:TP], ACT.Copy).then_inc(bias_moved, 1)

                def exp(i):
                    gated(act, neg, h * N_Q + (i + 1), passed)
                    n = P * (i + 1)
                    act.activation(prob[i % 2][:, 0:n], prob[i % 2][:, 0:n], ACT.Exp, scale=A_SCALE, bias=nb[:, i % 2:i % 2 + 1],
                                   accum_out=rs[:, i % 2:i % 2 + 1]).then_inc(expd, 1)

                exp(0)
                exp(1)
                for i in range(NC8):
                    if i == 0:
                        gated(act, bias_ready, h + 1, passed)
                    else:
                        gated(act, o_ready, h * N_Q + i, passed)
                    for bank in range((i >= 4) + 1):
                        gated(act, p_turned, h * 12 + (MOVES[i] + bank + 1), passed)
                        n = min(4, i + 1 - 4 * bank)
                        act.activation(prob_t[:, 4 * bank:4 * bank + n, :], misc[bank][:, 0:P * n].rearrange("p (c n) -> p c n", n=P),
                                       ACT.Copy).then_inc(p_moved, 1)
                    if i + 2 < NC8:
                        exp(i + 2)
                    if more and i in (2, 3):
                        hi(h + 1, i - 2)

            for s in range(2):
                act.sem_inc(raw_ready[s], 16)
                act.sem_inc(hi_done, 1)
            with act.Fori(0, HA - 1) as h:
                head(h, True)
            head(HA - 1, False)

        @block.vector
        def _(dve):
            dve.sem_inc(o_moved, 1)
            dve.sem_inc(stored, 16)
            with dve.Fori(0, HA) as h:
                hs = bass.ds(h, 1)
                for t, (src, dst) in enumerate(((q, k.q_new), (kk_, k.k_new), (v, k.v_new))):
                    gated(dve, moved, h * 3 + (t + 1), passed)
                    dve.tensor_copy(dst[:, hs, :].rearrange("p o s -> p (o s)"), src[:, TP:NT]).then_inc(begun, 1)
                gated(dve, o_moved, h * N_Q + 1, passed)
                row = k.ncum[:, :].rearrange("p (c h) -> p c h", h=HA)[:, :, hs]
                dve.tensor_tensor(diag[:, :, :], bc(const(k, "ident"), 1, NC8), row.to_broadcast([P, NC8, P]),
                                  ALU.mult).then_inc(diag_ready, 1)
                gated(dve, bias_moved, h + 1, passed)

                def top_of(i):
                    gated(dve, scored, h * N_Q + (i + 1), passed)
                    if i >= 2:
                        gated(dve, p_turned, h * 12 + MOVES[i - 1], passed)
                    n = P * (i + 1)
                    dve.tensor_tensor_reduce(out=prob[i % 2][:, 0:n], in0=slot[i % 2][:, 0:n], in1=bias[:, 0:n], scale=1.0,
                                             scalar=-3e38, op0=ALU.add, op1=ALU.max, accum_out=mx[:, i % 2:i % 2 + 1]).then_inc(top, 1)
                    gated(dve, top, h * N_Q + (i + 1), passed)
                    dve.tensor_scalar(nb[:, i % 2:i % 2 + 1], mx[:, i % 2:i % 2 + 1], -A_SCALE, None, ALU.mult).then_inc(neg, 1)

                def out_of(i):
                    gated(dve, o_ready, h * N_Q + (i + 1), passed)
                    dve.tensor_copy(k.cat[:, hs, P * i:P * i + P].rearrange("p o n -> p (o n)"),
                                    slot[i % 2][:, 1024:1024 + P]).then_inc(o_moved, 1)

                def normalize(i):
                    gated(dve, expd, h * N_Q + (i + 1), passed)
                    dve.reciprocal(rr[:, i % 2:i % 2 + 1], rs[:, i % 2:i % 2 + 1]).then_inc(summed, 1)
                    gated(dve, summed, h * N_Q + (i + 1), passed)
                    n = P * (i + 1)
                    dve.tensor_scalar(prob[i % 2][:, 0:n], prob[i % 2][:, 0:n], rr[:, i % 2:i % 2 + 1], None, ALU.mult).then_inc(normed, 1)

                top_of(0)
                top_of(1)
                normalize(0)
                for i in range(NC8):
                    if i + 1 < NC8:
                        normalize(i + 1)
                    if i + 2 < NC8:
                        top_of(i + 2)
                    out_of(i)


def block_samples(k, L):
    nc, d = k.nc, k.dram
    R = S * HA
    with ExitStack() as ctx:
        sb = lambda n, s, t=F32: ctx.enter_context(nc.sbuf_tensor(n, s, t))
        ps = lambda n, s: ctx.enter_context(nc.psum_tensor(n, s, F32))
        kp = sb("kp", [P, S, NPG, HA * DA])
        vp = sb("vpg", [P, S, NPG, HA * DA])
        lf = sb("lf", [P, S, NPG, HA])
        e_new = sb("e_new", [P, S, HA])
        qd = [sb(f"qd{i}", [P, HA, P]) for i in range(2)]
        prod = [sb(f"prod{i}", [P, NPG, HA * DA]) for i in range(2)]
        lg = sb("lg", [P, NPG, S, HA])
        qk = sb("qk", [P, S, HA])
        rows = sb("rows", [R, PAST + 1])
        one = sb("one", [R, 4])
        pt = sb("pt", [P, NPG, S * (R + HA)])
        orow = sb("orow", [R, HA * DA])
        dnew = sb("dnew", [R, R])
        vn = sb("vn", [P, S, HA])
        q_bank = [ps(f"q_bank{i}", [P, 512]) for i in range(2)]
        b_bank, r_bank, t_bank, o_bank, n_bank = (ps(n, [P, 512]) for n in ("b_bank", "r_bank", "t_bank", "so_bank", "n_bank"))
        k_loaded = [k.sem(f"k_loaded{i}") for i in range(S)]
        (lf_loaded, v_loaded, qd_ready, q_ready, prod_done, lg_done, e_ready, b_ready, lg_ready, qk_ready, rows_ready,
         rows_link, neg_ready, exp_done, prob_ready, pt_ready, pt_moved, o_ready, orow_ready, turned) = (k.sem(n) for n in (
             "lf_loaded", "v_loaded", "qd_ready", "q_ready", "prod_done", "lg_done", "e_ready", "b_ready", "lg_ready",
             "qk_ready", "rows_ready", "rows_link", "neg_ready", "exp_done", "prob_ready", "pt_ready", "pt_moved", "o_ready",
             "orow_ready", "turned"))
        block = ctx.enter_context(nc.Block())
        N_POOL = d["cache_k"].shape[1]

        @block.sync
        def _(sp):
            for s in range(S):
                for pg in range(NPG):
                    page = sp.value_load(k.pages[0:1, NPG * s + pg:NPG * s + pg + 1], min_val=0, max_val=N_POOL - 1)
                    pool = lambda n: d[n][L, bass.ds(page, 1)]
                    sp.dma_start(kp[:, s, pg, :], pool("cache_k").rearrange("o p h n -> p (o h n)")).then_inc(k_loaded[s], 16)
                    sp.dma_start(lf[:, s, pg, :], pool("cache_logf").rearrange("o p h -> p (o h)")).then_inc(lf_loaded, 16)

        @block.tensor
        def _(pe):
            ident, ones, after = const(k, "ident"), const(k, "ones"), const(k, "after")
            for s in range(S):
                pe.wait_ge(qd_ready, s + 1)
                if s >= 2:
                    pe.wait_ge(prod_done, s - 1)
                pe.matmul(q_bank[s % 2][:, :], ones, qd[s % 2][:, :, :].rearrange("p h n -> p (h n)"), start=True,
                          stop=True).then_inc(q_ready, 1)
            pe.wait_ge(lf_loaded, 16 * S * NPG)
            pe.wait_ge(e_ready, 1)
            new = e_new[:, :, :]
            for pg in range(NPG):
                out = b_bank[:, R * pg:R * pg + R]
                pe.matmul(out, after, lf[:, :, pg, :], start=True, stop=False)
                for later in range(pg + 1, NPG):
                    pe.matmul(out, ones, lf[:, :, later, :], start=False, stop=False)
                last = pe.matmul(out, ones, new, start=False, stop=True)
            last.then_inc(b_ready, 1)
            pe.wait_ge(lg_ready, 1)
            for pg in range(NPG):
                pe.matmul(r_bank[0:R, P * pg:P * pg + P], lg[:, pg, :, :].rearrange("p s h -> p (s h)"), ident, start=True, stop=True)
            pe.wait_ge(qk_ready, 1)
            pe.matmul(r_bank[0:R, PAST:PAST + 1], qk[:, :, :].rearrange("p s h -> p (s h)"), ones[:, 0:1], start=True,
                      stop=True).then_inc(rows_ready, 1)
            pe.wait_ge(prob_ready, 2)
            for pg in range(NPG):
                pe.matmul(t_bank[:, R * pg:R * pg + R], rows[:, P * pg:P * pg + P], ident[0:R, 0:R], start=True, stop=True)
            pe.matmul(n_bank[:, 0:R], ones[0:R, :], dnew[:, :], start=True, stop=True).then_inc(pt_ready, 1)
            pe.wait_ge(pt_moved, 1)
            pe.wait_ge(v_loaded, 16 * S * NPG)
            for s in range(S):
                for pg in range(NPG):
                    n = s * NPG + pg
                    last = pe.matmul(o_bank[0:R, :], pt[:, pg, R * s:R * s + R], vp[:, s, pg, :], start=(n == 0),
                                     stop=(n == S * NPG - 1))
            last.then_inc(o_ready, 1)
            pe.wait_ge(orow_ready, 1)
            for h in range(HA):
                last = pe.matmul(q_bank[0][:, S * h:S * h + S], orow[:, DA * h:DA * h + DA], ident[0:R, h:R:HA], start=True, stop=True)
            last.then_inc(turned, 1)

        @block.scalar
        def _(act):
            for s in range(S):
                for pg in range(NPG):
                    page = act.value_load(k.pages[0:1, NPG * s + pg:NPG * s + pg + 1], min_val=0, max_val=N_POOL - 1)
                    act.dma_start(vp[:, s, pg, :], d["cache_v"][L, bass.ds(page, 1)].rearrange("o p h n -> p (o h n)")).then_inc(v_loaded, 16)
            act.wait_ge(neg_ready, 1)
            act.activation(rows[:, :], rows[:, :], ACT.Exp, bias=one[:, 1:2], accum_out=one[:, 2:3]).then_inc(exp_done, 1)
            act.wait_ge(o_ready, 1)
            act.activation(orow[:, :], o_bank[0:R, :], ACT.Copy).then_inc(orow_ready, 1)

        @block.gpsimd
        def _(pool):
            pool.memset(pt[:, :, :], 0.0).then_inc(k.zeroed, 1)
            for s in range(S):
                if s >= 2:
                    pool.wait_ge(q_ready, s - 1)
                pool.tensor_tensor(qd[s % 2][:, :, :], bc(const(k, "ident"), 1, HA), bc(k.q_new[:, :, s], 2, P),
                                   ALU.mult).then_inc(qd_ready, 1)

        @block.vector
        def _(dve):
            link = Link(dve, rows_link)
            dve.tensor_tensor(e_new[:, :, :], bc(const(k, "sampsel"), 2, HA), bc(k.logf[:, 8 * HA:9 * HA], 1, S), ALU.mult).then_inc(e_ready, 1)
            dve.tensor_tensor(qk[:, :, :], k.q_new[:, :, :].rearrange("p h s -> p s h"), k.k_new[:, :, :].rearrange("p h s -> p s h"),
                              ALU.mult).then_inc(qk_ready, 1)
            for s in range(S):
                dve.wait_ge(k_loaded[s], 16 * NPG)
                dve.wait_ge(q_ready, s + 1)
                if s >= 2:
                    dve.wait_ge(lg_done, s - 1)
                dve.tensor_tensor(prod[s % 2][:, :, :], kp[:, s, :, :], bc(q_bank[s % 2][:, :], 1, NPG), ALU.mult).then_inc(prod_done, 1)
                dve.wait_ge(prod_done, s + 1)
                dve.tensor_reduce(lg[:, :, s, :], prod[s % 2][:, :, :].rearrange("p g (h n) -> p g h n", h=HA), AX_X,
                                  ALU.add).then_inc(lg_done, 1)
            dve.wait_ge(b_ready, 1)
            dve.wait_ge(lg_done, S)
            flat = lg[:, :, :, :].rearrange("p g s h -> p (g s h)")
            dve.scalar_tensor_tensor(flat, flat, A_SCALE, b_bank[:, 0:NPG * R], ALU.mult, ALU.add).then_inc(lg_ready, 1)
            dve.wait_ge(rows_ready, 1)
            link(dve.tensor_copy(rows[:, 0:PAST], r_bank[0:R, 0:PAST]))
            link(dve.tensor_scalar(rows[:, PAST:PAST + 1], r_bank[0:R, PAST:PAST + 1], A_SCALE, None, ALU.mult))
            link(dve.tensor_reduce(one[:, 0:1], rows[:, :], AX_X, ALU.max))
            dve.tensor_scalar(one[:, 1:2], one[:, 0:1], -1.0, None, ALU.mult).then_inc(neg_ready, 1)
            dve.wait_ge(exp_done, 1)
            link(dve.reciprocal(one[:, 3:4], one[:, 2:3]))
            dve.tensor_scalar(rows[:, :], rows[:, :], one[:, 3:4], None, ALU.mult).then_inc(prob_ready, 1)
            dve.wait_ge(prob_ready, 1)
            dve.tensor_scalar(dnew[:, :], const(k, "ident")[0:R, 0:R], rows[:, PAST:PAST + 1], None, ALU.mult).then_inc(prob_ready, 1)
            dve.wait_ge(pt_ready, 1)
            dve.wait_ge(k.zeroed, 1)
            dve.tensor_copy(pt[:, :, :].rearrange("p g (s x) -> p g s x", s=S)[:, :, :, 0:HA],
                            t_bank[:, 0:NPG * R].rearrange("p (g s h) -> p g s h", g=NPG, s=S)).then_inc(pt_moved, 1)
            link(dve.tensor_tensor(vn[:, :, :], k.v_new[:, :, :].rearrange("p h s -> p s h"),
                                   n_bank[:, 0:R].rearrange("p (s h) -> p s h", h=HA), ALU.mult))
            dve.wait_ge(turned, 1)
            dve.tensor_tensor(k.cat[:, 0:HA, TP:NT], vn[:, :, :].rearrange("p s h -> p h s"),
                              q_bank[0][:, 0:R].rearrange("p (h s) -> p h s", h=HA), ALU.add).then_inc(k.quiet, 1)


def block_output(k, L):
    nc, d = k.nc, k.dram
    with ExitStack() as ctx:
        ps = lambda n, s: ctx.enter_context(nc.psum_tensor(n, s, F32))
        slot = [ps(f"oslot{i}", [P, SLOT]) for i in range(2)]
        st = ps("ost", [P, BANK])
        sb = lambda n, s: ctx.enter_context(nc.sbuf_tensor(n, s, F32))
        sq, acc = [sb(f"osq{i}", [P, NT]) for i in range(2)], sb("oacc", [P, NT])
        v, t = sb("ov", [P, TC]), sb("ot", [P, TC])
        raw_ready = [k.sem("raw_ready0"), k.sem("raw_ready1")]
        x_hi, x_lo, hi_done, lo_done, tile_done, moved, passed, sq_ready, summed, sums_ready, link_v = (k.sem(n) for n in (
            "x_hi", "x_lo", "hi_done", "lo_done", "tile_done", "moved", "passed_o", "sq_ready", "summed", "sums_ready", "link_v"))
        block = ctx.enter_context(nc.Block())

        @block.sync
        def _(sp):
            w = d["w_o"][L].rearrange("(k p) n -> p k n", p=P)
            with sp.Fori(0, KD // 2) as i:
                for s in range(2):
                    gated(sp, lo_done, i * 2 + (s + 1), passed)
                    sp.dma_start(k.w_raw[s][:, :, :], w[:, :, bass.ds((i * 2 + s) * P, P)]).then_inc(raw_ready[s], 16)

        @block.gpsimd
        def _(pool):
            pool.sem_inc(lo_done, 1)
            pool.sem_inc(lo_done, 1)
            with pool.Fori(0, KD // 2) as i:
                for s in range(2):
                    gated(pool, hi_done, i * 2 + (s + 1), passed)
                    gated(pool, tile_done, i * 2 + (s + 1), passed)
                    pool.tensor_tensor(k.w_lo[s][:, :, :], k.w_raw[s][:, :, :], k.w_hi[s][:, :, :].bitcast(F32),
                                       ALU.subtract).then_inc(lo_done, 1)

        @block.tensor
        def _(pe):
            pe.sem_inc(tile_done, 1)
            pe.sem_inc(tile_done, 1)
            with pe.Fori(0, KD // 2) as i:
                for s in range(2):
                    gated(pe, lo_done, i * 2 + (s + 3), passed)
                    gated(pe, moved, i * 2 + (s + 1), passed)
                    product3(pe, slot[s], k.w_hi[s], k.w_lo[s], k.h_hi, k.h_lo, KD, slice(0, P), x_lo).then_inc(tile_done, 1)
            pe.wait_ge(summed, 1 + KD)
            pe_token_sums(k, pe, st, acc, True, True).then_inc(sums_ready, 1)

        @block.scalar
        def _(act):
            act.sem_inc(moved, 1)
            act.sem_inc(moved, 1)

            def hi(i, s):
                gated(act, raw_ready[s], i * 16 + 16, passed)
                gated(act, tile_done, i * 2 + (s + 1), passed)
                act.activation(k.w_hi[s][:, :, :], k.w_raw[s][:, :, :], ACT.Copy).then_inc(hi_done, 1)

            for kk in range(KD):
                if kk in (3, 5):
                    hi(0, (kk - 3) // 2)
                act.activation(k.h_hi[:, kk, :], k.cat[:, kk, :], ACT.Copy).then_inc(x_hi, 1)

            def finish(i, more):
                for s in range(2):
                    gated(act, tile_done, i * 2 + (s + 3), passed)
                    gated(act, summed, i * 2 + (s + 1), passed)
                    act.activation(sq[s][:, :], slot[s][:, OFF:OFF + NT], ACT.Square).then_inc(sq_ready, 1)
                    act.activation(k.cat[:, bass.ds(i * 2 + s, 1), :].rearrange("p o n -> p (o n)"), slot[s][:, OFF:OFF + NT],
                                   ACT.Copy).then_inc(moved, 1)
                    if more:
                        hi(i + 1, s)

            with act.Fori(0, KD // 2 - 1) as i:
                finish(i, True)
            finish(KD // 2 - 1, False)

        @block.vector
        def _(dve):
            for kk in range(KD):
                dve.wait_ge(x_hi, kk + 1)
                dve.tensor_tensor(k.h_lo[:, kk, :], k.cat[:, kk, :], k.h_hi[:, kk, :].bitcast(F32), ALU.subtract).then_inc(x_lo, 1)
            dve.memset(acc[:, :], 0.0).then_inc(summed, 1)
            with dve.Fori(0, KD // 2) as i:
                for s in range(2):
                    gated(dve, sq_ready, i * 2 + (s + 1), passed)
                    gated(dve, summed, i * 2 + (s + 1), passed)
                    dve.tensor_tensor(acc[:, :], acc[:, :], sq[s][:, :], ALU.add).then_inc(summed, 1)
            link = Link(dve, link_v)
            dve.wait_ge(sums_ready, 1)
            dve_inverse_rms(k, dve, link, st, v, t)


SLOT_OF = (1, 0, 1, 0, 0, 1, 0, 1)
LAST_USE = [(FT - 1) * 5 + 1 + m // 2 for m in range(KD)]


def block_ffn(k, L):
    nc, d = k.nc, k.dram
    with ExitStack() as ctx:
        sb = lambda n, s, t=F32: ctx.enter_context(nc.sbuf_tensor(n, s, t))
        ps = lambda n, s: ctx.enter_context(nc.psum_tensor(n, s, F32))
        raw = sb("raw", [P, NT])
        t_ab = [sb(f"t_ab{i}", [P, NT]) for i in range(2)]
        f_hi, f_lo = ([sb(f"f_{n}{i}", [P, NT], F32R) for i in range(2)] for n in ("hi", "lo"))
        d_raw = sb("d_raw", [P, D_MODEL])
        d_hi, d_lo = sb("d_hi", [P, D_MODEL], F32R), sb("d_lo", [P, D_MODEL], F32R)
        srow = sb("srow", [2 * S, 2, P])
        sctx = sb("sctx", [P, 2, 2 * S])
        keep = sb("keep", [P, 2, 10])
        tail = sb("ftail", [10, 2, P])
        slot = [ps(f"fslot{i}", [P, SLOT]) for i in range(2)]
        v, t = sb("fv", [P, TC]), sb("ftmp", [P, TC])
        sq, acc = (raw, t_ab[0]), t_ab[1]
        c_bank, t_bank = ps("c_bank", [P, 512]), ps("ft_bank", [P, 512])
        raw_ready = [k.sem("raw_ready0"), k.sem("raw_ready1")]
        free = [k.sem("free0"), k.sem("free1")]
        (hi_done, lo_done, up_done, down_done, d_ready, d_hi_done, d_lo_done, s_ready, ctx_turned, ctx_moved, tapped, kept,
         conv, gate_done, f_done, f_hi_done, f_lo_done, tail_turned, tail_moved, stored, passed, samp, raw_used, sq_ready, summed, sums_ready, link_v) = (k.sem(n) for n in (
             "hi_done", "lo_done", "up_done", "down_done", "d_ready", "d_hi_done", "d_lo_done", "s_ready", "ctx_turned",
             "ctx_moved", "tapped", "kept", "conv", "gate_done", "f_done", "f_hi_done", "f_lo_done", "tail_turned",
             "tail_moved", "stored", "passed_f", "samp", "raw_used", "sq_ready", "summed",
             "sums_ready", "link_v"))
        block = ctx.enter_context(nc.Block())
        vec = k.vecs
        up = d["ffn_up"][L].rearrange("(k p) n -> p k n", p=P)

        @block.sync
        def _(sp):
            sp.dma_start(d["ffn_conv_sample"][L, :, 0, :], d["state_ffn_conv"][L, :, 1, :]).then_inc(stored, 16)

            def load_up(i):
                for half in range(2):
                    at = i * P + half * D_FF
                    gated(sp, lo_done, i * 2 + (half + 1), passed)
                    sp.dma_start(k.w_raw[half][:, :, :], up[:, :, bass.ds(at, P)]).then_inc(raw_ready[half], 16)

            def load_rest(i):
                gated(sp, ctx_turned, i + 1, passed)
                for half in range(2):
                    sp.dma_start(srow[:, half, :], d["state_ffn_conv"][L, :, :, bass.ds(i * P + half * D_FF, P)].rearrange(
                        "s r n -> (s r) n")).then_inc(s_ready, 16)
                gated(sp, d_lo_done, i + 1, passed)
                sp.dma_start(d_raw[:, :], d["ffn_down"][L, bass.ds(i * P, P), :]).then_inc(d_ready, 16)

            load_rest(0)
            with sp.Fori(0, FT - 1) as i:
                load_up(i + 1)
                load_rest(i + 1)
            sp.wait_ge(stored, 32 + 64 * FT)

        @block.gpsimd
        def _(pool):
            for _ in range(4):
                pool.sem_inc(lo_done, 1)
            pool.sem_inc(d_lo_done, 1)
            pool.memset(k.cat[:, :, :], 0.0).then_inc(k.zeroed, 1)

            def lo(i, half):
                gated(pool, hi_done, i * 2 + (half + 1), passed)
                gated(pool, up_done, i * 2 + (half + 1), passed)
                pool.tensor_tensor(k.w_lo[half][:, :, :], k.w_raw[half][:, :, :], k.w_hi[half][:, :, :].bitcast(F32),
                                   ALU.subtract).then_inc(lo_done, 1)

            def down_lo(i):
                gated(pool, d_hi_done, i + 1, passed)
                gated(pool, down_done, i * 8 + 1, passed)
                pool.tensor_tensor(d_lo[:, :], d_raw[:, :], d_hi[:, :].bitcast(F32), ALU.subtract).then_inc(d_lo_done, 1)

            lo(1, 0)
            lo(1, 1)
            with pool.Fori(0, FT - 2) as i:
                down_lo(i)
                lo(i + 2, 0)
                lo(i + 2, 1)
            down_lo(FT - 2)
            down_lo(FT - 1)

        @block.tensor
        def _(pe):
            ident = const(k, "ident")
            pe.sem_inc(up_done, 1)
            pe.sem_inc(up_done, 1)
            pe.sem_inc(down_done, 1)
            pe.sem_inc(ctx_turned, 1)

            def turn_context(i):
                gated(pe, s_ready, i * 32 + 32, passed)
                gated(pe, ctx_moved, i + 1, passed)
                for half in range(2):
                    last = pe.matmul(c_bank[:, 16 * half:16 * half + 16], srow[:, half, :], ident[0:16, 0:16], start=True, stop=True)
                last.then_inc(ctx_turned, 1)

            def turn_tail(i):
                gated(pe, kept, i * 2 + 2, passed)
                gated(pe, tail_moved, i + 1, passed)
                for half in range(2):
                    last = pe.matmul(t_bank[0:10, P * half:P * half + P], keep[:, half, :], ident, start=True, stop=True)
                last.then_inc(tail_turned, 1)

            def project_up(i, half, use):
                gated(pe, lo_done, i * 2 + (half + 3), passed)
                gated(pe, free[half], use + 1, passed)
                product3(pe, slot[half], k.w_hi[half], k.w_lo[half], k.h_hi, k.h_lo, KD, slice(0, P)).then_inc(up_done, 1)

            def project_down(m, use, b):
                s = SLOT_OF[m]
                gated(pe, free[s], use + 1, passed)
                cols = slice(P * m, P * m + P)
                for w, x, n in ((d_hi, f_hi[b], 0), (d_hi, f_lo[b], 1), (d_lo, f_hi[b], 2)):
                    for lo, hi in CHUNKS:
                        last = pe.matmul(slot[s][:, OFF + lo:OFF + hi], w[:, cols], x[:, lo:hi], start=(n == 0), stop=(n == 2))
                last.then_inc(down_done, 1)

            def step(i, b):
                turn_context(i + 1)
                project_up(i + 1, 0, i * 5 + 1)
                gated(pe, f_lo_done, i + 1, passed)
                gated(pe, d_lo_done, i + 2, passed)
                for m, use in ((0, 1), (1, 2), (2, 2), (3, 3)):
                    project_down(m, i * 5 + use, b)
                project_up(i + 1, 1, i * 5 + 3)
                for m, use in ((4, 4), (5, 4)):
                    project_down(m, i * 5 + use, b)
                turn_tail(i + 1)
                for m, use in ((6, 5), (7, 5)):
                    project_down(m, i * 5 + use, b)

            turn_context(0)
            project_up(0, 0, 0)
            project_up(0, 1, 0)
            turn_tail(0)
            with pe.Fori(0, FT // 2 - 1) as n:
                for b in range(2):
                    step(n * 2 + b, b)
            step(FT - 2, 0)
            pe.wait_ge(f_lo_done, FT)
            pe.wait_ge(d_lo_done, FT + 1)
            for m in range(KD):
                project_down(m, LAST_USE[m], 1)
            pe.wait_ge(summed, KD - 1)
            pe.wait_ge(ctx_moved, FT + 1)
            pe_token_sums(k, pe, c_bank, acc, True, True).then_inc(sums_ready, 1)

        @block.scalar
        def _(act):
            act.sem_inc(ctx_moved, 1)
            act.sem_inc(tail_moved, 1)
            act.sem_inc(stored, 16)

            def split(i, half):
                gated(act, raw_ready[half], i * 16 + 16, passed)
                gated(act, up_done, i * 2 + (half + 1), passed)
                act.activation(k.w_hi[half][:, :, :], k.w_raw[half][:, :, :], ACT.Copy).then_inc(hi_done, 1)

            def split_down(i):
                gated(act, d_ready, i * 16 + 16, passed)
                gated(act, down_done, i * 8 + 1, passed)
                act.activation(d_hi[:, :], d_raw[:, :], ACT.Copy).then_inc(d_hi_done, 1)

            def context(i):
                gated(act, ctx_turned, i + 2, passed)
                if not isinstance(i, int) or i > 0:
                    gated(act, samp, i * 2, passed)
                act.activation(sctx[:, :, :], c_bank[:, 0:32].rearrange("p (a n) -> p a n", a=2), ACT.Copy).then_inc(ctx_moved, 1)

            def read_out(i, half, use):
                first = isinstance(i, int) and i == 0
                gated(act, up_done, i * 2 + (half + 3), passed)
                if half or not first:
                    gated(act, raw_used, i * 2 + half, passed)
                if not first:
                    gated(act, kept, i * 2 + half, passed)
                elif half:
                    act.wait_ge(kept, 1)
                act.activation(raw[:, :], slot[half][:, OFF:OFF + NT], ACT.Copy).then_inc(free[half], 1)
                gated(act, free[half], use + 2, passed)
                if not first:
                    if half == 0:
                        gated(act, f_done, i, passed)
                    else:
                        gated(act, f_hi_done, i, passed)
                        gated(act, f_lo_done, i, passed)
                c = i + (FT if half else 0)
                act.activation(t_ab[half][:, :], raw[:, :], ACT.Identity, scale=vec[:, 3, bass.ds(c, 1)],
                               bias=vec[:, 3, bass.ds(c + 2 * FT, 1)]).then_inc(tapped, 1)
                if not first:
                    gated(act, tail_turned, i, passed)
                act.activation(keep[:, half, :], raw[:, TP - 2:NT], ACT.Copy).then_inc(kept, 1)

            def gate(i):
                gated(act, samp, i * 2 + 1, passed)
                gated(act, raw_used, i * 2 + 1, passed)
                act.activation(t_ab[0][:, :], t_ab[0][:, :], ACT.Silu).then_inc(gate_done, 1)

            def split_hidden(i, b):
                gated(act, f_done, i + 1, passed)
                act.activation(f_hi[b][:, :], t_ab[1][:, :], ACT.Copy).then_inc(f_hi_done, 1)

            def tail_out(i):
                gated(act, tail_turned, i + 1, passed)
                gated(act, stored, i * 64 + 32, passed)
                act.activation(tail[:, :, :], t_bank[0:10, 0:2 * P].rearrange("p (a n) -> p a n", a=2), ACT.Copy).then_inc(tail_moved, 1)
                gated(act, tail_moved, i + 2, passed)
                for half in range(2):
                    cols = bass.ds(i * P + half * D_FF, P)
                    act.dma_start(d["ffn_conv_prompt"][L, 0, :, cols], tail[0:2, half, :]).then_inc(stored, 16)
                    act.dma_start(d["ffn_conv_sample"][L, :, 1, cols], tail[2:10, half, :]).then_inc(stored, 16)

            def step(i, b, ahead):
                split_down(i)
                split_hidden(i, b)
                context(i + 1)
                read_out(i + 1, 0, i * 5 + 1)
                if ahead:
                    split(i + 2, 0)
                tail_out(i)
                read_out(i + 1, 1, i * 5 + 3)
                gate(i + 1)
                if ahead:
                    split(i + 2, 1)

            for half in range(2):
                act.sem_inc(raw_ready[half], 16)
                act.sem_inc(hi_done, 1)
            context(0)
            read_out(0, 0, 0)
            split(1, 0)
            read_out(0, 1, 0)
            gate(0)
            split(1, 1)
            with act.Fori(0, FT // 2 - 1) as n:
                for b in range(2):
                    step(n * 2 + b, b, True)
            step(FT - 2, 0, False)
            split_down(FT - 1)
            split_hidden(FT - 1, 1)
            tail_out(FT - 1)
            act.wait_ge(f_lo_done, FT)
            for m in range(KD):
                act.wait_ge(free[SLOT_OF[m]], LAST_USE[m] + 2)
                if m >= 2:
                    act.wait_ge(summed, max(1, m - 2))
                act.activation(sq[m % 2][:, :], k.cat[:, m, :], ACT.Square).then_inc(sq_ready, 1)

        @block.vector
        def _(dve):
            dve.sem_inc(free[0], 1)
            dve.sem_inc(free[1], 1)
            dve.wait_ge(k.zeroed, 1)

            def taps(i, half):
                gated(dve, tapped, i * 2 + (half + 1), passed)
                gated(dve, ctx_moved, i + 2, passed)
                t, c = t_ab[half], i + (FT if half else 0)
                tap0, tap1 = vec[:, 2, bass.ds(c, 1)], vec[:, 2, bass.ds(c + 2 * FT, 1)]
                dve.scalar_tensor_tensor(t[:, 1:TP], raw[:, 0:TP - 1], tap1, t[:, 1:TP], ALU.mult, ALU.add).then_inc(conv, 1)
                dve.scalar_tensor_tensor(t[:, TP:NT], sctx[:, half, 1:16:2], tap1, t[:, TP:NT], ALU.mult, ALU.add).then_inc(conv, 1)
                gated(dve, conv, i * 4 + (2 * half + 2), passed)
                dve.scalar_tensor_tensor(t[:, 2:TP], raw[:, 0:TP - 2], tap0, t[:, 2:TP], ALU.mult, ALU.add).then_inc(raw_used, 1)
                dve.scalar_tensor_tensor(t[:, TP:NT], sctx[:, half, 0:16:2], tap0, t[:, TP:NT], ALU.mult, ALU.add).then_inc(samp, 1)

            def product(i, b):
                gated(dve, gate_done, i + 1, passed)
                gated(dve, raw_used, i * 2 + 2, passed)
                gated(dve, samp, i * 2 + 2, passed)
                dve.tensor_tensor(t_ab[1][:, :], t_ab[0][:, :], t_ab[1][:, :], ALU.mult).then_inc(f_done, 1)
                gated(dve, f_hi_done, i + 1, passed)
                dve.tensor_tensor(f_lo[b][:, :], t_ab[1][:, :], f_hi[b][:, :].bitcast(F32), ALU.subtract).then_inc(f_lo_done, 1)

            def gather(i, some):
                for m in some:
                    s = SLOT_OF[m]
                    gated(dve, down_done, i * 8 + (m + 2), passed)
                    dve.tensor_tensor(k.cat[:, m, :], k.cat[:, m, :], slot[s][:, OFF:OFF + NT], ALU.add).then_inc(free[s], 1)

            def step(i, b):
                gather(i, range(4))
                taps(i + 1, 0)
                gather(i, range(4, 8))
                taps(i + 1, 1)
                product(i + 1, 1 - b)

            taps(0, 0)
            taps(0, 1)
            product(0, 0)
            with dve.Fori(0, FT // 2 - 1) as n:
                for b in range(2):
                    step(n * 2 + b, b)
            step(FT - 2, 0)
            gather(FT - 1, range(2))
            for m in range(1, KD):
                if m + 1 < KD:
                    gather(FT - 1, (m + 1,))
                dve.wait_ge(sq_ready, m + 1)
                if m > 1:
                    dve.wait_ge(summed, m - 1)
                dve.tensor_tensor(acc[:, :], sq[0][:, :] if m == 1 else acc[:, :], sq[m % 2][:, :], ALU.add).then_inc(summed, 1)
            link = Link(dve, link_v)
            dve.wait_ge(sums_ready, 1)
            dve_inverse_rms(k, dve, link, c_bank, v, t)


def block_exit(k):
    nc, d = k.nc, k.dram
    with ExitStack() as ctx:
        sb = lambda n, s, t=F32: ctx.enter_context(nc.sbuf_tensor(n, s, t))
        ps = lambda n, s, t=F32: ctx.enter_context(nc.psum_tensor(n, s, t))
        sem = lambda n: ctx.enter_context(nc.semaphore(n))
        yrow = sb("yrow", [P, TC, D_MODEL])
        bank = [ps(f"ybank{i}", [P, 512]) for i in range(2)]
        turned, moved, stored = sem("y_turned"), sem("y_moved"), sem("y_stored")
        block = ctx.enter_context(nc.Block())
        steps = [(c, half) for c in range(TC) for half in range(2)]

        @block.tensor
        def _(pe):
            for n, (c, half) in enumerate(steps):
                if n >= 2:
                    pe.wait_ge(moved, n - 1)
                w = min(P, NT - c * P)
                for j in range(4):
                    src = k.x[:, 4 * half + j, P * c:P * c + w]
                    out = bank[n % 2][0:w, P * j:P * j + P]
                    last = pe.transpose(out, src, const(k, "ident")) if w == P else pe.matmul(out, src, const(k, "ident"), start=True, stop=True)
                last.then_inc(turned, 1)

        @block.vector
        def _(dve):
            for n, (c, half) in enumerate(steps):
                dve.wait_ge(turned, n + 1)
                w = min(P, NT - c * P)
                dve.tensor_copy(yrow[0:w, c, 512 * half:512 * half + 512], bank[n % 2][0:w, :]).then_inc(moved, 1)

        @block.sync
        def _(sp):
            for c in range(TC):
                sp.wait_ge(moved, 2 * c + 2)
                if c < NC8:
                    sp.dma_start(d["y_prompt"][0, P * c:P * c + P, :], yrow[:, c, :]).then_inc(stored, 16)
                else:
                    sp.dma_start(d["y_sample"][:, 0, :], yrow[0:S, c, :]).then_inc(stored, 16)
            sp.wait_ge(stored, 16 * TC)


def trunk(nc, dram):
    k = K()
    k.nc, k.dram = nc, dram
    with ExitStack() as ctx:
        sb = lambda n, s, t=F32: ctx.enter_context(nc.sbuf_tensor(n, s, t))
        k.x = sb("x_res", [P, KD, NT])
        k.cat = sb("cat", [P, KD, NT])
        k.consts = sb("consts", [P, N_CONST])
        k.ident_bf, k.mask_bf = sb("ident_bf", [P, P], BF16), sb("mask_bf", [P, P], BF16)
        k.pages = sb("pages", [1, S * NPG], I32)
        k.cT = sb("cT", [P, KD, 9])
        k.mod = sb("mod", [P, 6, KD, 9])
        k.vecs = sb("vecs", [P, 4, P])
        k.inv = sb("inv", [P, TC])
        k.logf = sb("logf", [P, TC * HA])
        k.ncum = sb("ncum", [P, NC8 * HA])
        k.q_new, k.k_new, k.v_new = (sb(n, [P, HA, S]) for n in ("q_new", "k_new", "v_new"))
        k.v_ret, k.q_ret = k.cat[:, 0:2, :], k.cat[:, 2:4, :]
        signals = [ctx.enter_context(nc.semaphore(f"signal{i}")) for i in range(36)]
        first, final = signals[0].num, signals[-1].num
        assert final - first == len(signals) - 1
        taken = [0]

        def signal(name):
            taken[0] += 1
            return signals[taken[0] - 1]

        k.sem = signal

        def run(block, *args):
            taken[0] = 0
            k.quiet = signal("quiet")
            k.zeroed = signal("zeroed")
            block(k, *args)
            nc.all_engine_barrier(sems_to_clear=range(first, final + 1))

        def tiles_of(weights, a, b):
            rows = weights.rearrange("(k p) n -> p k n", p=P)
            return [rows[:, :, a:a + P], rows[:, :, b:b + P]]

        block_entry(k)
        with nc.Fori(0, DEPTH) as L:
            run(block_modulation, L)
            with ExitStack() as wide:
                wsb = lambda n, s, t=F32: wide.enter_context(nc.sbuf_tensor(n, s, t))
                k.h_hi, k.h_lo = wsb("h_hi", [P, KD, NT], F32R), wsb("h_lo", [P, KD, NT], F32R)
                k.w_raw = [wsb(f"w_raw{i}", [P, KD, P]) for i in range(2)]
                k.w_hi = [wsb(f"w_hi{i}", [P, KD, P], F32R) for i in range(2)]
                k.w_lo = [wsb(f"w_lo{i}", [P, KD, P], F32R) for i in range(2)]
                run(block_join, L, "_n1", None, 0, 1, tiles_of(dram["w_in"][L], COL_CA, COL_F))
                with nc.sbuf_tensor("k_ret", [P, 2, NT], F32) as k.k_ret:
                    run(block_project, L)
                    run(block_retention, L)
                    run(block_group_norms, L)
                run(block_heads, L)
            run(block_samples, L)
            with ExitStack() as wide:
                wsb = lambda n, s, t=F32: wide.enter_context(nc.sbuf_tensor(n, s, t))
                k.h_hi, k.h_lo = wsb("g_hi", [P, KD, NT], F32R), wsb("g_lo", [P, KD, NT], F32R)
                k.w_raw = [wsb(f"v_raw{i}", [P, KD, P]) for i in range(2)]
                k.w_hi = [wsb(f"v_hi{i}", [P, KD, P], F32R) for i in range(2)]
                k.w_lo = [wsb(f"v_lo{i}", [P, KD, P], F32R) for i in range(2)]
                run(block_output, L)
                run(block_join, L, "_n2", 2, 3, 4, tiles_of(dram["ffn_up"][L], 0, D_FF))
                run(block_ffn, L)
                run(block_join, L, "_r2", 5)
        block_exit(k)


_INS = ["x_prompt", "x_sample", "cache_k", "cache_v", "cache_logf", "state_ret", "state_conv", "state_ffn_conv", "page_table",
        "c_prompt", "c_sample", "ada_w", "ada_b", "norms", "w_in", "b_f", "ret_gn_g", "conv_w", "conv_b", "conv_ln_g",
        "conv_ln_b", "w_o", "ffn_up", "ffn_conv_w", "ffn_conv_b", "ffn_down"]
_OUTS = [("y_prompt", (1, TP, D_MODEL)), ("y_sample", (S, 1, D_MODEL)),
         ("k_prompt", (DEPTH, 1, TP, HA, DA)), ("v_prompt", (DEPTH, 1, TP, HA, DA)), ("logf_prompt", (DEPTH, 1, TP, HA)),
         ("ret_prompt", (DEPTH, 1, HB, DB, DB)), ("conv_prompt", (DEPTH, 1, CTX, DC)),
         ("ffn_conv_prompt", (DEPTH, 1, FW - 1, 2 * D_FF)),
         ("k_sample", (DEPTH, S, 1, HA, DA)), ("v_sample", (DEPTH, S, 1, HA, DA)), ("logf_sample", (DEPTH, S, 1, HA)),
         ("ret_sample", (DEPTH, S, HB, DB, DB)), ("conv_sample", (DEPTH, S, CTX, DC)),
         ("ffn_conv_sample", (DEPTH, S, FW - 1, 2 * D_FF))]


def kernel(**inputs):
    import numpy as _np
    import concourse.bacc as _bacc
    from concourse import mybir as _mybir
    from concourse.bass_utils import run_bass_kernel_spmd as _run

    nc = _bacc.Bacc("TRN2", target_bir_lowering=False, num_devices=1)
    arrays, dram = {}, {}
    consts, rope = constants()
    for name, a in [(n, inputs[n]) for n in _INS] + [("consts", consts), ("rope", rope)]:
        a = _np.ascontiguousarray(a)
        arrays[f"in_{name}_dram"] = a
        dram[name] = nc.dram_tensor(f"in_{name}_dram", a.shape, _mybir.dt.from_np(a.dtype), kind="ExternalInput").ap()
    for name, shape in _OUTS:
        dram[name] = nc.dram_tensor(f"out_{name}_dram", shape, F32, kind="ExternalOutput").ap()
    trunk(nc, dram)
    r = _run(nc, [arrays], core_ids=[0])
    return tuple(r.results[0][f"out_{name}_dram"] for name, _ in _OUTS)
```

```python
from contextlib import ExitStack

import numpy as np
import concourse.bass as bass
from concourse import mybir

F32 = mybir.dt.float32
F32R = mybir.dt.float32r
BF16 = mybir.dt.bfloat16
I32 = mybir.dt.int32
ALU = mybir.AluOpType
ACT = mybir.ActivationFunctionType
AX_X = mybir.AxisListType.X

P = 128
D_MODEL, TP, S, DEPTH = 1024, 1024, 8, 2
NT = TP + S
KD = D_MODEL // P
HA, DA, HB, DB, DC = 4, 128, 4, 64, 256
CONV_W, FW = 31, 3
CTX = CONV_W - 1
D_FF = 2816
FT = D_FF // P
PAST, PAGE = 256, 128
NPG = PAST // PAGE
EPS = 1e-6
NC8 = TP // P
TC = NC8 + 1
COL_F = 3 * HA * DA
COL_BQ = COL_F + HA
COL_CA = COL_BQ + 4 * HB * DB
N_IN = COL_CA + 2 * DC
A_SCALE = DA ** -0.5
RSQRT_MAGIC = float(0x5F3759DF)

BANK = 512
SLOT = 3 * BANK
OFF = 252
CHUNKS = ((0, BANK - OFF), (BANK - OFF, 2 * BANK - OFF), (2 * BANK - OFF, NT))
HALVES = ((0, 512), (512, 1024))

CONST = {}
_at = 0
for _name, _n in (("ident", 128), ("ones", 128), ("upto", 128), ("after", 128), ("mask", 128), ("pair", 128),
                  ("stack", 64), ("headsel", 2), ("sampsel", 8), ("decay", 512), ("xi", 256), ("zeta", 4), ("gchunk", 2),
                  ("gone", 2)):
    CONST[_name] = (_at, _n)
    _at += _n
N_CONST = _at


def constants():
    out = np.zeros((P, N_CONST), np.float32)

    def put(name, a):
        at, n = CONST[name]
        out[:, at:at + n] = np.asarray(a, np.float32).reshape(P, n)

    r = np.arange(P)
    put("ident", np.eye(P))
    put("ones", np.ones((P, P)))
    put("upto", r[:, None] <= r[None, :])
    put("after", r[:, None] > r[None, :])
    put("mask", np.where(r[None, :] <= r[:, None], 0.0, -1e30))
    put("pair", (r[:, None] // 64) == (r[None, :] // 64))
    put("stack", (r[:, None] % 64) == np.arange(64)[None, :])
    put("headsel", (r[:, None] // 64) == np.arange(2)[None, :])
    put("sampsel", r[:, None] == 120 + np.arange(8)[None, :])
    log_g = np.log1p(-(2.0 ** (-5.0 - np.arange(HB))))
    rel = r[None, :] - r[:, None]
    dec = np.stack([np.where(rel >= 0, np.exp(log_g[h] * np.maximum(rel, 0)), 0.0) for h in range(HB)])
    put("decay", dec.reshape(2, 2, P, P).transpose(2, 1, 0, 3))
    hp = r // 64
    put("xi", np.stack([[np.exp(log_g[2 * hh + p] * (r + 1.0)) for hh in range(2)] for p in hp]))
    put("zeta", np.exp(log_g[None, :] * (P - 1.0 - r[:, None])))
    put("gchunk", np.exp(np.stack([log_g[2 * hh + hp] for hh in range(2)], 1) * P))
    put("gone", np.exp(np.stack([log_g[2 * hh + hp] for hh in range(2)], 1)))
    half = DB // 2
    inv = np.float32(10000.0) ** (-np.arange(half, dtype=np.float32) / np.float32(half))
    pos = np.concatenate([np.arange(TP), np.full(S, PAST)]).astype(np.float32)
    ang = (pos[None, :] * inv[:, None].astype(np.float32)).astype(np.float32)
    cos, sin = np.cos(ang), np.sin(ang)
    rope = np.concatenate([np.tile(cos, (4, 1)), np.concatenate([-sin, sin, -sin, sin])], 1).astype(np.float32)
    return out, rope


class K:
    pass


def gated(e, sem, value, passed):
    e.wait_ge(sem, value)
    if not isinstance(value, int):
        e.sem_inc(passed, 1)


class Link:

    def __init__(self, e, sem):
        self.e, self.sem, self.n = e, sem, 0

    def __call__(self, ins):
        self.n += 1
        ins.then_inc(self.sem, 1)
        self.e.wait_ge(self.sem, self.n)


class Ahead:

    def __init__(self, k, tiles):
        self.k, self.tiles = k, tiles
        self.loaded, self.hi_done = [k.sem("ahead_loaded0"), k.sem("ahead_loaded1")], k.sem("ahead_hi_done")

    def load(self, sp):
        for s in range(2):
            sp.dma_start(self.k.w_raw[s][:, :, :], self.tiles[s]).then_inc(self.loaded[s], 16)

    def high(self, act):
        for s in range(2):
            act.wait_ge(self.loaded[s], 16)
            act.activation(self.k.w_hi[s][:, :, :], self.k.w_raw[s][:, :, :], ACT.Copy).then_inc(self.hi_done, 1)

    def low(self, pool):
        k = self.k
        for s in range(2):
            pool.wait_ge(self.hi_done, s + 1)
            pool.tensor_tensor(k.w_lo[s][:, :, :], k.w_raw[s][:, :, :], k.w_hi[s][:, :, :].bitcast(F32),
                               ALU.subtract).then_inc(k.quiet, 1)


def product3(e, out, w_hi, w_lo, x_hi, x_lo, kt, cols, x_ready=None):
    last = None
    for k in range(kt):
        if x_ready is not None:
            x_ready(e, k)
        for w, x, first in ((w_hi, x_hi, True), (w_hi, x_lo, False), (w_lo, x_hi, False)):
            for a, b in CHUNKS:
                last = e.matmul(out[:, OFF + a:OFF + b], w[:, k, cols], x[:, k, a:b],
                                start=(k == 0 and first), stop=(k == kt - 1 and w is w_lo))
    return last


def rsqrt(dve, link, y, v, t):
    link(dve.tensor_scalar(y.bitcast(I32), v.bitcast(I32), -0.5, RSQRT_MAGIC, ALU.mult, ALU.add))
    for _ in range(3):
        link(dve.tensor_tensor(t, y, y, ALU.mult))
        link(dve.scalar_tensor_tensor(t, t, -0.5, v, ALU.mult, ALU.mult))
        link(dve.scalar_tensor_tensor(y, t, 1.5, y, ALU.add, ALU.mult))


def const(k, name):
    at, n = CONST[name]
    return k.consts[:, at:at + n]


def bc(ap, axis, n):
    shape = list(ap.shape)
    shape.insert(axis, n)
    return ap.unsqueeze(axis).to_broadcast(shape)


def block_entry(k):
    nc, d = k.nc, k.dram
    with ExitStack() as ctx:
        sb = lambda n, s, t=F32: ctx.enter_context(nc.sbuf_tensor(n, s, t))
        ps = lambda n, s, t=F32: ctx.enter_context(nc.psum_tensor(n, s, t))
        sem = lambda n: ctx.enter_context(nc.semaphore(n))
        xrow = sb("xrow", [P, TC, D_MODEL])
        crow = sb("crow", [1 + S, D_MODEL])
        tp = [ps(f"tp_{i}", [P, 512]) for i in range(2)]
        cp = ps("cp", [P, 512])
        x_loaded = [sem(f"x_loaded{c}") for c in range(NC8)]
        loaded, const_loaded, turned, moved, csilu, cturned = (
            sem(n) for n in ("loaded", "const_loaded", "turned", "moved", "csilu", "cturned"))
        block = ctx.enter_context(nc.Block())

        @block.sync
        def _(sp):
            sp.dma_start(k.consts[:, :], d["consts"]).then_inc(const_loaded, 16)
            sp.dma_start(crow[0:1, :], d["c_prompt"]).then_inc(const_loaded, 16)
            sp.dma_start(crow[1:1 + S, :], d["c_sample"]).then_inc(const_loaded, 16)
            sp.dma_start(k.pages[:, :], d["page_table"].rearrange("a b -> (a b)").unsqueeze(0)).then_inc(const_loaded, 16)
            for c in range(NC8):
                sp.dma_start(xrow[:, c, :], d["x_prompt"][0, P * c:P * c + P, :]).then_inc(x_loaded[c], 16)
            sp.dma_start(xrow[0:S, NC8, :], d["x_sample"].rearrange("a b f -> (a b) f")).then_inc(loaded, 16)

        @block.vector
        def _(dve):
            dve.wait_ge(const_loaded, 64)
            dve.tensor_copy(k.ident_bf[:, :], const(k, "ident"))
            dve.tensor_copy(k.mask_bf[:, :], const(k, "mask"))
            for c in range(NC8):
                for half in range(2):
                    i = 2 * c + half
                    dve.wait_ge(turned, i + 1)
                    dve.tensor_copy(k.x[:, 4 * half:4 * half + 4, P * c:P * c + P],
                                    tp[i % 2][:, :].rearrange("p (f n) -> p f n", n=P)).then_inc(moved, 1)
            dve.wait_ge(cturned, 1)
            dve.tensor_copy(k.cT[:, :, :], cp[:, 0:KD * 9].rearrange("p (f c) -> p f c", c=9))
            dve.tensor_copy(k.x[:, :, TP:NT], cp[:, 128:128 + KD * S].rearrange("p (f c) -> p f c", c=S))

        @block.scalar
        def _(act):
            act.wait_ge(const_loaded, 64)
            act.activation(crow[:, :], crow[:, :], ACT.Silu).then_inc(csilu, 1)

        @block.tensor
        def _(pe):
            ident = const(k, "ident")
            pe.wait_ge(const_loaded, 64)
            for c in range(NC8):
                pe.wait_ge(x_loaded[c], 16)
                for half in range(2):
                    i = 2 * c + half
                    if i >= 2:
                        pe.wait_ge(moved, i - 1)
                    for j in range(4):
                        last = pe.transpose(tp[i % 2][:, 128 * j:128 * j + 128],
                                            xrow[:, c, P * (4 * half + j):P * (4 * half + j) + P], ident)
                    last.then_inc(turned, 1)
            pe.wait_ge(csilu, 1)
            pe.wait_ge(loaded, 16)
            for f in range(KD):
                pe.matmul(cp[:, 9 * f:9 * f + 9], crow[:, 128 * f:128 * f + 128], ident[0:9, 0:9], start=True, stop=True)
                last = pe.matmul(cp[:, 128 + S * f:128 + S * f + S], xrow[0:S, NC8, 128 * f:128 * f + 128],
                                 ident[0:S, 0:S], start=True, stop=True)
            last.then_inc(cturned, 1)


V_ADA, V_NORM, V_CB, V_LG, V_LB, V_GN = 0, 48, 80, 82, 84, 86


def block_modulation(k, L):
    nc, d = k.nc, k.dram
    W = 256
    STEPS = 6
    ROUNDS = 6 * D_MODEL // (STEPS * W)
    TW = W // P
    with ExitStack() as ctx:
        sb = lambda n, s, t=F32: ctx.enter_context(nc.sbuf_tensor(n, s, t))
        ps = lambda n, s, t=F32: ctx.enter_context(nc.psum_tensor(n, s, t))
        a_raw = [sb(f"a_raw{i}", [P, KD, W]) for i in range(3)]
        a_hi, a_lo = ([sb(f"a_{n}{i}", [P, KD, W], F32R) for i in range(3)] for n in ("hi", "lo"))
        c_pad = sb("c_pad", [P, KD, P])
        c_hi, c_lo = sb("c_hi", [P, KD, P], F32R), sb("c_lo", [P, KD, P], F32R)
        mrow = [sb(f"mrow{i}", [P, W]) for i in range(2)]
        vrow = sb("vrow", [P, 4, P])
        sq, acc = sb("msq", [P, NT]), sb("macc", [P, NT])
        v, t = sb("mv", [P, TC]), sb("mt", [P, TC])
        vp, st = ps("vp", [P, BANK]), ps("mst", [P, BANK])
        mp = [ps(f"mp{i}", [P, BANK]) for i in range(2)]
        tp = [ps(f"mtp{i}", [P, BANK]) for i in range(2)]
        w_loaded = [k.sem(f"w_loaded{i}") for i in range(3)]
        (hi_done, lo_done, product_done, row_ready, turned, added, c_ready, c_split, rows_loaded, rows_turned, scaled, passed,
         summed, sums_ready, link_v) = (k.sem(n) for n in (
             "hi_done", "lo_done", "product_done", "row_ready", "turned", "added", "c_ready", "c_split", "rows_loaded",
             "rows_turned", "scaled", "passed_m", "summed", "sums_ready", "link_v"))
        w_in = d["w_in"][L].rearrange("(k p) n -> p k n", p=P)
        ahead = Ahead(k, [w_in[:, :, COL_CA:COL_CA + P], w_in[:, :, COL_F:COL_F + P]])
        block = ctx.enter_context(nc.Block())
        row = lambda a: a.rearrange("(r p) -> r p", p=P)
        rows = [(vrow[0:48, 0, :], row(d["ada_b"][L])), (vrow[48:80, 0, :], d["norms"][L].rearrange("a (r p) -> (a r) p", p=P)),
                (vrow[0:2 * CONV_W, 1, :], d["conv_w"][L].rearrange("w (r p) -> (w r) p", p=P)),
                (vrow[0:88, 2, :], d["ffn_conv_w"][L, 0:2].rearrange("w (r p) -> (w r) p", p=P)),
                (vrow[0:44, 3, :], row(d["ffn_conv_w"][L, 2])), (vrow[44:88, 3, :], row(d["ffn_conv_b"][L]))]
        rows += [(vrow[80 + 2 * i:82 + 2 * i, 0, :], row(d[n][L])) for i, n in enumerate(
            ("conv_b", "conv_ln_g", "conv_ln_b", "ret_gn_g"))]

        @block.sync
        def _(sp):
            ada = d["ada_w"][L].rearrange("(k p) n -> p k n", p=P)

            def load(i, s):
                gated(sp, lo_done, i * STEPS + (s + 1), passed)
                sp.dma_start(a_raw[s % 3][:, :, :], ada[:, :, bass.ds((i * STEPS + s) * W, W)]).then_inc(w_loaded[s % 3], 16)

            load(0, 0)
            for dst, src in rows[:5]:
                sp.dma_start(dst, src).then_inc(rows_loaded, 16)
            for s in range(1, STEPS):
                load(0, s)
            with sp.Fori(0, ROUNDS - 1) as i:
                for s in range(STEPS):
                    load(i + 1, s)

        @block.tensor
        def _(pe):
            for s in range(3):
                pe.sem_inc(product_done, 1)
            for s in range(2):
                pe.sem_inc(turned, 1)
            pe.wait_ge(rows_loaded, 160)
            for j, n in enumerate((88, 2 * CONV_W, 88, 88)):
                last = pe.matmul(vp[:, 128 * j:128 * j + n], vrow[0:n, j, :], const(k, "ident")[0:n, 0:n],
                                 start=True, stop=True)
            last.then_inc(rows_turned, 1)
            pe.wait_ge(c_split, 2)

            def turn(n, s):
                pe.wait_ge(row_ready, n + (s + 3))
                pe.wait_ge(added, n + (s + 1))
                for j in range(TW):
                    last = pe.transpose(tp[s % 2][:, P * j:P * j + P], mrow[s % 2][:, P * j:P * j + P], const(k, "ident"))
                last.then_inc(turned, 1)

            def steps(n):
                for s in range(STEPS):
                    pe.wait_ge(lo_done, n + (s + 4))
                    pe.wait_ge(row_ready, n + (s + 1))
                    for kk in range(KD):
                        for c, a, first in ((c_hi, a_hi, True), (c_hi, a_lo, False), (c_lo, a_hi, False)):
                            last = pe.matmul(mp[s % 2][:, 0:W], c[:, kk, :], a[s % 3][:, kk, :], start=(kk == 0 and first),
                                             stop=(kk == KD - 1 and c is c_lo))
                    last.then_inc(product_done, 1)
                    if s >= 1:
                        turn(n, s - 1)
                turn(n, STEPS - 1)

            with pe.Fori(0, ROUNDS - 1) as i:
                steps(i * STEPS)
            pe.wait_ge(summed, 2 * KD - 1)
            pe_token_sums(k, pe, st, acc, True, True).then_inc(sums_ready, 1)
            steps((ROUNDS - 1) * STEPS)

        @block.scalar
        def _(act):
            act.sem_inc(row_ready, 1)
            act.sem_inc(row_ready, 1)

            act.wait_ge(c_ready, 1)
            act.activation(c_hi[:, :, :], c_pad[:, :, :], ACT.Copy).then_inc(c_split, 1)
            for dst, src in rows[5:]:
                act.dma_start(dst, src).then_inc(rows_loaded, 16)
            act.wait_ge(k.zeroed, 3)

            def steps(i, more):
                n = i * STEPS
                for s in range(STEPS):
                    if more or s + 2 < STEPS:
                        high(i, s + 2)
                    gated(act, product_done, n + (s + 4), passed)
                    gated(act, turned, n + (s + 1), passed)
                    act.activation(mrow[s % 2][0:1 + S, :], mp[s % 2][0:1 + S, 0:W], ACT.Copy).then_inc(row_ready, 1)

            def high(i, s):
                gated(act, w_loaded[s % 3], i * 32 + (s // 3 * 16 + 16), passed)
                gated(act, product_done, i * STEPS + (s + 1), passed)
                act.activation(a_hi[s % 3][:, :, :], a_raw[s % 3][:, :, :], ACT.Copy).then_inc(hi_done, 1)

            high(0, 0)
            high(0, 1)
            ahead.load(act)
            with act.Fori(0, ROUNDS - 1) as i:
                steps(i, True)
            ahead.high(act)
            steps(ROUNDS - 1, False)

        @block.gpsimd
        def _(pool):
            pool.memset(c_pad[:, :, :], 0.0).then_inc(k.zeroed, 1)
            for i in range(2):
                pool.memset(mrow[i][:, :], 0.0).then_inc(k.zeroed, 1)
            link = Link(pool, summed)
            link(pool.tensor_tensor(acc[:, :], k.x[:, 0, :], k.x[:, 0, :], ALU.mult))
            for kk in range(1, KD):
                link(pool.tensor_tensor(sq[:, :], k.x[:, kk, :], k.x[:, kk, :], ALU.mult))
                link(pool.tensor_tensor(acc[:, :], acc[:, :], sq[:, :], ALU.add))
            ahead.low(pool)

        @block.vector
        def _(dve):
            link = Link(dve, link_v)
            for s in range(3):
                dve.sem_inc(lo_done, 1)
            for s in range(2):
                dve.sem_inc(added, 1)
            dve.wait_ge(k.zeroed, 1)
            dve.tensor_copy(c_pad[:, :, 0:1 + S], k.cT[:, :, :]).then_inc(c_ready, 1)
            dve.wait_ge(c_split, 1)
            dve.tensor_tensor(c_lo[:, :, :], c_pad[:, :, :], c_hi[:, :, :].bitcast(F32), ALU.subtract).then_inc(c_split, 1)

            def low(i, s):
                dve.wait_ge(hi_done, i * STEPS + (s + 1))
                dve.wait_ge(product_done, i * STEPS + (s + 1))
                dve.tensor_tensor(a_lo[s % 3][:, :, :], a_raw[s % 3][:, :, :], a_hi[s % 3][:, :, :].bitcast(F32),
                                  ALU.subtract).then_inc(lo_done, 1)

            mod = k.mod[:, :, :, :].rearrange("p a b c -> p (a b) c")

            def steps(i, more):
                for s in range(STEPS):
                    if more or s + 2 < STEPS:
                        low(i, s + 2)
                    dve.wait_ge(turned, i * STEPS + (s + 3))
                    at = bass.ds(i * (STEPS * TW) + s * TW, TW)
                    dve.tensor_tensor(mod[:, at, :], tp[s % 2][:, 0:W].rearrange("p (a b) -> p a b", b=P)[:, :, 0:1 + S],
                                      k.vecs[:, 0, at].unsqueeze(2).to_broadcast([P, TW, 1 + S]), ALU.add).then_inc(added, 1)

            low(0, 0)
            low(0, 1)
            dve.wait_ge(rows_turned, 1)
            for j, n in enumerate((88, 2 * CONV_W, 88, 88)):
                dve.tensor_copy(k.vecs[:, j, 0:n], vp[:, 128 * j:128 * j + n]).then_inc(scaled, 1)
            dve.wait_ge(scaled, 4)
            with dve.Fori(0, ROUNDS - 1) as i:
                steps(i, True)
            dve.wait_ge(sums_ready, 1)
            dve_inverse_rms(k, dve, link, st, v, t)
            steps(ROUNDS - 1, False)
            dve.wait_ge(added, 2 + ROUNDS * STEPS)
            for part, row, plus in ((1, 0, 1.0), (2, 1, 0.0), (4, 2, 1.0), (5, 3, 0.0)):
                gain = bc(k.vecs[:, 0, V_NORM + 8 * row:V_NORM + 8 * row + 8], 2, 9)
                dve.scalar_tensor_tensor(k.mod[:, part], k.mod[:, part], plus, gain, ALU.add, ALU.mult)


def pe_token_sums(k, pe, st, tile, first, final):
    for c in range(TC):
        w = min(P, NT - c * P)
        last = pe.matmul(st[0:w, c:c + 1], tile[:, c * P:c * P + w], const(k, "ones")[:, 0:1],
                         start=(first and c == 0), stop=final, skip_group_check=True)
    return last


def dve_row_scale(k, dve, link, st, n, v, y, t, scale):
    link(dve.memset(v[:, :], 1.0))
    link(dve.tensor_scalar(v[:, 0:NC8 * n], st[:, 0:NC8 * n], scale, EPS, ALU.mult, ALU.add))
    link(dve.tensor_scalar(v[0:S, NC8 * n:TC * n], st[0:S, NC8 * n:TC * n], scale, EPS, ALU.mult, ALU.add))
    rsqrt(dve, link, y[:, :], v[:, :], t[:, :])


def dve_inverse_rms(k, dve, link, st, v, t):
    dve_row_scale(k, dve, link, st, 1, v, k.inv, t, 1.0 / D_MODEL)


def dve_diagonal(k, dve, diag):
    return dve.tensor_tensor(diag[:, :, :], bc(const(k, "ident"), 1, TC), bc(k.inv[:, :], 2, P), ALU.mult)


def pe_spread(k, pe, diag, rb):
    flat = diag[:, :, :].rearrange("p a b -> p (a b)")
    for a, b in CHUNKS:
        last = pe.matmul(rb[:, OFF + a:OFF + b], const(k, "ones"), flat[:, a:b], start=True, stop=True)
    return last


POOL_ADDS = (0, 2, 4, 6)
POOL_LOWS = (0, 2, 4, 6)
PE_SUMS = (0, 2)
ACC_FIRST = 1


class Normed:

    def __init__(self, k, rb, h, hs, shift, scale):
        self.k, self.rb, self.h, self.hs, self.shift, self.scale = k, rb, h, hs, shift, scale
        (self.h_scaled, self.h_shifted, self.hi_done, self.dve_low, self.pool_low, self.hs_link, self.hs_hi) = (
            k.sem("n_" + n) for n in ("h_scaled", "h_shifted", "hi_done", "dve_low", "pool_low", "hs_link", "hs_hi"))

    def lowered(self, e, kk):
        if kk in POOL_LOWS:
            e.wait_ge(self.pool_low, POOL_LOWS.index(kk) + 1)
        else:
            e.wait_ge(self.dve_low, kk + 1 - sum(p < kk for p in POOL_LOWS))

    def on_pe(self, pe, kk):
        if kk == 0:
            pe.wait_ge(self.hs_link, 4)
        self.lowered(pe, kk)

    def on_pool(self, pool):
        k = self.k
        for kk in POOL_LOWS:
            pool.wait_ge(self.hi_done, kk + 1)
            pool.tensor_tensor(k.h_lo[:, kk, 0:TP], self.h[kk % 3], k.h_hi[:, kk, 0:TP].bitcast(F32),
                               ALU.subtract).then_inc(self.pool_low, 1)

    def on_act(self, act):
        k = self.k
        act.wait_ge(self.hs_link, 3)
        act.activation(k.h_hi[:, :, TP:NT], self.hs[:, :, :], ACT.Copy).then_inc(self.hs_hi, 1)
        for kk in range(KD):
            act.wait_ge(self.h_scaled, kk + 1)
            ht, hi, bias = self.h[kk % 3], k.h_hi[:, kk, 0:TP], k.mod[:, self.shift, kk, 0:1]
            if kk in POOL_LOWS:
                act.activation(ht, ht, ACT.Identity, bias=bias).then_inc(self.h_shifted, 1)
                act.wait_ge(self.h_shifted, POOL_LOWS.index(kk) + 1)
                act.activation(hi, ht, ACT.Copy).then_inc(self.hi_done, 1)
            else:
                act.activation(hi, ht, ACT.Identity, bias=bias).then_inc(self.hi_done, 1)

    def on_dve(self, dve):
        k, hs, rb = self.k, self.hs, self.rb
        tail = slice(OFF + TP, OFF + NT)
        slink = Link(dve, self.hs_link)
        slink(dve.tensor_tensor(hs[:, :, :], k.x[:, :, TP:NT], bc(rb[:, tail], 1, KD), ALU.mult))
        slink(dve.tensor_tensor(hs[:, :, :], hs[:, :, :], k.mod[:, self.scale, :, 1:9], ALU.mult))
        slink(dve.tensor_tensor(hs[:, :, :], hs[:, :, :], k.mod[:, self.shift, :, 1:9], ALU.add))
        for kk in range(KD + 1):
            if kk < KD:
                if kk >= 3:
                    self.lowered(dve, kk - 3)
                dve.scalar_tensor_tensor(self.h[kk % 3], k.x[:, kk, 0:TP], k.mod[:, self.scale, kk, 0:1], rb[:, OFF:OFF + TP],
                                         ALU.mult, ALU.mult).then_inc(self.h_scaled, 1)
            if kk == 0:
                dve.wait_ge(self.hs_hi, 1)
                dve.tensor_tensor(k.h_lo[:, :, TP:NT], hs[:, :, :], k.h_hi[:, :, TP:NT].bitcast(F32),
                                  ALU.subtract).then_inc(self.hs_link, 1)
            if kk >= 1 and kk - 1 not in POOL_LOWS:
                dve.wait_ge(self.hi_done, kk)
                dve.scalar_tensor_tensor(k.h_lo[:, kk - 1, 0:TP], self.h[(kk - 1) % 3], k.mod[:, self.shift, kk - 1, 0:1],
                                         k.h_hi[:, kk - 1, 0:TP].bitcast(F32), ALU.add, ALU.subtract).then_inc(self.dve_low, 1)


def block_join(k, L, tag, gate, tiles=None):
    nc = k.nc
    both = tiles is not None
    with ExitStack() as ctx:
        sb = lambda n, s, t=F32: ctx.enter_context(nc.sbuf_tensor(n + tag, s, t))
        ps = lambda n, s, t=F32: ctx.enter_context(nc.psum_tensor(n + tag, s, t))
        sq = [sb(f"sq{i}", [P, NT]) for i in range(2)]
        acc = sb("acc", [P, NT])
        diag = sb("diag", [P, TC, P])
        v, t = sb("v", [P, TC]), sb("t", [P, TC])
        st, rb = ps("st", [P, BANK]), k.slots[1]
        (diag_ready, rb_ready, samp, scaled, dve_added, pool_added, sq_ready, pe_used, acc_done, sums_ready, link_v) = (
            k.sem(n + tag) for n in ("diag_ready", "rb_ready", "samp", "scaled", "dve_added", "pool_added", "sq_ready",
                                     "pe_used", "acc_done", "sums_ready", "link_v"))
        ahead = Ahead(k, tiles) if both else None
        block = ctx.enter_context(nc.Block())
        ringed = [kk for kk in range(KD) if kk != ACC_FIRST]
        dve_sums = [kk for kk in ringed if kk not in PE_SUMS]
        cols = slice(OFF, OFF + TP)
        tail = slice(OFF + TP, OFF + NT)

        def square(kk):
            return acc if kk == ACC_FIRST else sq[ringed.index(kk) % 2]

        def added(e, kk):
            if kk in POOL_ADDS:
                e.wait_ge(pool_added, POOL_ADDS.index(kk) + 1)
            else:
                e.wait_ge(dve_added, kk + 1 - sum(p < kk for p in POOL_ADDS))

        @block.sync
        def _(sp):
            if both:
                ahead.load(sp)

        @block.tensor
        def _(pe):
            pe.wait_ge(diag_ready, 1)
            pe_spread(k, pe, diag, rb).then_inc(rb_ready, 1)
            if both:
                for n, kk in enumerate(PE_SUMS):
                    pe.wait_ge(sq_ready, kk + 1)
                    pe_token_sums(k, pe, st, square(kk), n == 0, False).then_inc(pe_used, 1)
                pe.wait_ge(acc_done, len(dve_sums))
                pe_token_sums(k, pe, st, acc, False, True).then_inc(sums_ready, 1)
                pe.wait_ge(diag_ready, 2)
                pe_spread(k, pe, diag, rb).then_inc(k.quiet, 1)

        @block.gpsimd
        def _(pool):
            for kk in POOL_ADDS:
                pool.wait_ge(scaled, kk + 1)
                pool.tensor_tensor(k.x[:, kk, 0:TP], k.x[:, kk, 0:TP], k.cat[:, kk, 0:TP], ALU.add).then_inc(pool_added, 1)
            if both:
                ahead.low(pool)

        @block.scalar
        def _(act):
            if both:
                ahead.high(act)
                act.wait_ge(samp, 3)
                for kk in range(KD):
                    added(act, kk)
                    if kk != ACC_FIRST and ringed.index(kk) >= 2:
                        before = ringed[ringed.index(kk) - 2]
                        if before in PE_SUMS:
                            act.wait_ge(pe_used, PE_SUMS.index(before) + 1)
                        else:
                            act.wait_ge(acc_done, dve_sums.index(before) + 1)
                    act.activation(square(kk)[:, :], k.x[:, kk, :], ACT.Square).then_inc(sq_ready, 1)

        @block.vector
        def _(dve):
            link = Link(dve, link_v)
            dve_diagonal(k, dve, diag).then_inc(diag_ready, 1)
            ys, xs = k.cat[:, :, TP:NT], k.x[:, :, TP:NT]
            dve.tensor_tensor(ys, ys, k.mod[:, gate, :, 1:9], ALU.mult).then_inc(samp, 1)
            dve.wait_ge(samp, 1)
            dve.wait_ge(rb_ready, 1)
            dve.tensor_tensor(ys, ys, bc(rb[:, tail], 1, KD), ALU.mult).then_inc(samp, 1)
            dve.wait_ge(samp, 2)
            dve.tensor_tensor(xs, xs, ys, ALU.add).then_inc(samp, 1)

            def finish(kk):
                if kk in range(KD) and kk not in POOL_ADDS:
                    dve.wait_ge(scaled, kk + 1)
                    dve.tensor_tensor(k.x[:, kk, 0:TP], k.x[:, kk, 0:TP], k.cat[:, kk, 0:TP], ALU.add).then_inc(dve_added, 1)
                if both and kk - 2 in dve_sums:
                    dve.wait_ge(sq_ready, kk - 1)
                    if kk - 2 != dve_sums[0]:
                        dve.wait_ge(acc_done, dve_sums.index(kk - 2))
                    dve.tensor_tensor(acc[:, :], acc[:, :], square(kk - 2)[:, :], ALU.add).then_inc(acc_done, 1)

            for kk in range(KD + 3):
                if kk < KD:
                    y = k.cat[:, kk, 0:TP]
                    dve.scalar_tensor_tensor(y, y, k.mod[:, gate, kk, 0:1], rb[:, cols], ALU.mult, ALU.mult).then_inc(scaled, 1)
                finish(kk - 1)
            if both:
                dve.wait_ge(sums_ready, 1)
                dve_inverse_rms(k, dve, link, st, v, t)
                dve_diagonal(k, dve, diag).then_inc(diag_ready, 1)


def block_project(k, L):
    nc, d = k.nc, k.dram
    tiles = [COL_CA, COL_CA + DC, COL_CA + P, COL_CA + DC + P] + [COL_BQ + P * j for j in range(8)]
    with ExitStack() as ctx:
        sb = lambda n, s, t=F32: ctx.enter_context(nc.sbuf_tensor(n, s, t))
        ps = lambda n, s, t=F32: ctx.enter_context(nc.psum_tensor(n, s, t))
        rope = sb("rope", [P, 2, NT])
        swap = sb("swap", [P, NT])
        u = sb("u", [P, 2, CTX + NT])
        sig = ft = swap
        bf = sb("bf", [P, HA])
        z, za = sb("z", [P, TC * HA]), sb("za", [P, TC * HA])
        crow = sb("ctxrow", [120, 2, DC])
        cctx = sb("cctx", [P, 2, 2 * 120])
        cprod = sb("cprod", [P, S, CTX])
        csum = sb("csum", [P, S])
        tail = sb("tail", [38, DC])
        slot = [ps(f"slot{i}", [P, SLOT]) for i in range(2)]
        diag, hs = sb("pdiag", [P, TC, P]), sb("phs", [P, KD, S])
        normed = Normed(k, slot[0], [u[:, 0, 0:TP], u[:, 1, 0:TP], swap[:, 0:TP]], hs, 0, 1)
        diag_ready, rb_ready = k.sem("diag_ready"), k.sem("rb_ready")
        misc = [ps(f"misc{i}", [P, 512]) for i in range(2)]
        raw_ready = [k.sem("raw_ready0"), k.sem("raw_ready1")]
        free = [k.sem("free0"), k.sem("free1")]
        (hi_done, lo_done, tile_done, side_loaded, f_done, z_link, conv_link, rope_raw,
         rope_link, tail_turned, tail_done, ctx_turned, stored, logf_ready, act_link) = (k.sem(n) for n in (
             "hi_done", "lo_done", "tile_done", "side_loaded", "f_done", "z_link",
             "conv_link", "rope_raw", "rope_link", "tail_turned", "tail_done", "ctx_turned", "stored",
             "logf_ready", "act_link"))
        block = ctx.enter_context(nc.Block())
        nt = len(tiles)
        U_DONE = 3
        ring = lambda m: (m + 1) % 2

        @block.sync
        def _(sp):
            w_in = d["w_in"][L].rearrange("(k p) n -> p k n", p=P)
            for m, col in enumerate([COL_F] + tiles):
                if m >= 2:
                    sp.wait_ge(lo_done, m - 1)
                    sp.dma_start(k.w_raw[ring(m)][:, :, :], w_in[:, :, col:col + P]).then_inc(raw_ready[ring(m)], 16)
                if m == 1:
                    sp.dma_start(bf[:, :], d["b_f"][L].unsqueeze(0).to_broadcast([P, HA])).then_inc(side_loaded, 16)
                    sp.dma_start(rope[:, :, :], d["rope"].rearrange("p (a n) -> p a n", a=2)).then_inc(side_loaded, 16)
                    for half in range(2):
                        sp.dma_start(crow[:, half, :], d["state_conv"][L, 4 * half:4 * half + 4].rearrange(
                            "s r c -> (s r) c")).then_inc(side_loaded, 16)
            sp.dma_start(d["conv_sample"][L, :, 0:CTX - 1, :], d["state_conv"][L, :, 1:CTX, :]).then_inc(stored, 16)
            sp.wait_ge(tail_done, 1)
            sp.dma_start(d["conv_prompt"][L, 0], tail[0:CTX, :]).then_inc(stored, 16)
            sp.dma_start(d["conv_sample"][L, :, CTX - 1, :], tail[CTX:CTX + S, :]).then_inc(stored, 16)
            sp.wait_ge(logf_ready, 1)
            sp.dma_start(d["logf_prompt"][L, 0, 0:7 * P].rearrange("(c p) h -> p c h", p=P),
                         k.logf[:, 0:7 * HA].rearrange("p (c h) -> p c h", h=HA)).then_inc(stored, 16)
            sp.dma_start(d["logf_prompt"][L, 0, 7 * P:TP], k.logf[:, 7 * HA:8 * HA]).then_inc(stored, 16)
            sp.dma_start(d["logf_sample"][L, :, 0, :], k.logf[120:128, 8 * HA:9 * HA]).then_inc(stored, 16)
            sp.wait_ge(stored, 96)

        @block.gpsimd
        def _(pool):
            normed.on_pool(pool)
            pool.sem_inc(lo_done, 1)
            pool.sem_inc(lo_done, 1)
            for m in range(2, 1 + nt):
                pool.wait_ge(hi_done, m - 1)
                pool.wait_ge(tile_done, m - 1)
                w = ring(m)
                pool.tensor_tensor(k.w_lo[w][:, :, :], k.w_raw[w][:, :, :], k.w_hi[w][:, :, :].bitcast(F32),
                                   ALU.subtract).then_inc(lo_done, 1)

        @block.tensor
        def _(pe):
            ident = const(k, "ident")
            pe.wait_ge(diag_ready, 1)
            pe_spread(k, pe, diag, slot[0]).then_inc(rb_ready, 1)
            product3(pe, slot[1], k.w_hi[1], k.w_lo[1], k.h_hi, k.h_lo, KD, slice(0, P), normed.on_pe).then_inc(tile_done, 1)
            pe.wait_ge(side_loaded, 64)
            for half in range(2):
                for j in range(2):
                    last = pe.matmul(misc[1][:, 240 * j + 120 * half:240 * j + 120 * half + 120],
                                     crow[:, half, P * j:P * j + P], ident[0:120, 0:120], start=True, stop=True)
            last.then_inc(ctx_turned, 1)
            pe.wait_ge(free[1], 2)
            for c in range(TC):
                at = c * P if c < NC8 else NT - P
                last = pe.matmul(misc[0][:, HA * c:HA * c + HA], ft[0:HA, at:at + P], ident[0:HA, 0:HA], start=True, stop=True)
            last.then_inc(f_done, 1)

            def pair_of_tiles(i):
                for s in range(2):
                    pe.wait_ge(lo_done, i * 2 + (s + 2))
                    pe.wait_ge(free[s], i + (s + 1))
                    product3(pe, slot[s], k.w_hi[s], k.w_lo[s], k.h_hi, k.h_lo, KD, slice(0, P)).then_inc(tile_done, 1)

            with pe.Fori(0, U_DONE) as i:
                pair_of_tiles(i)
            pe.wait_ge(free[0], 3)
            pe.wait_ge(z_link, 1)
            for j in range(2):
                last = pe.matmul(misc[0][0:38, 128 + P * j:128 + P * j + P], u[:, j, TP:TP + 38], ident, start=True, stop=True)
            last.then_inc(tail_turned, 1)
            with pe.Fori(0, nt // 2 - U_DONE) as i:
                pair_of_tiles(i + U_DONE)

        @block.scalar
        def _(act):
            normed.on_act(act)
            act.sem_inc(free[1], 1)

            def hi(m):
                act.wait_ge(raw_ready[ring(m)], 16 * (m // 2))
                act.wait_ge(tile_done, m - 1)
                act.activation(k.w_hi[ring(m)][:, :, :], k.w_raw[ring(m)][:, :, :], ACT.Copy).then_inc(hi_done, 1)

            act.wait_ge(tile_done, 1)
            act.activation(ft[0:HA, :], slot[1][0:HA, OFF:OFF + NT], ACT.Copy).then_inc(free[1], 1)
            for i in range(nt):
                if i + 2 < 1 + nt:
                    hi(i + 2)
                s = i % 2
                res = slot[s][:, OFF:OFF + NT]
                act.wait_ge(tile_done, i + 2)
                if i == 2 * U_DONE:
                    act.wait_ge(tail_turned, 1)
                    act.activation(tail[:, :], misc[0][0:38, 128:128 + DC], ACT.Copy).then_inc(tail_done, 1)
                if i == 1:
                    act.wait_ge(f_done, 1)
                if i in (1, 3):
                    if i == 3:
                        act.wait_ge(free[0], 2)
                    act.activation(sig[:, :], res, ACT.Sigmoid).then_inc(free[1], 1)
                    if i == 3:
                        act.wait_ge(z_link, 1)
                        act.activation(za[:, :], z[:, :], ACT.Abs).then_inc(act_link, 1)
                        act.wait_ge(act_link, 1)
                        act.activation(za[:, :], za[:, :], ACT.Exp, scale=-1.0).then_inc(act_link, 1)
                        act.wait_ge(act_link, 2)
                        act.activation(za[:, :], za[:, :], ACT.Ln, bias=1.0).then_inc(act_link, 1)
                elif 4 <= i < 8:
                    j, dst = i % 2, (k.q_ret if i < 6 else k.k_ret)
                    scale = 1.0 if i < 6 else DB ** -0.5
                    act.activation(dst[:, j, :], res, ACT.Copy, scale=scale).then_inc(act_link, 1)
                    if i > 4:
                        act.wait_ge(rope_link, 3 * (i - 4))
                    else:
                        act.wait_ge(free[0], 3)
                    for quad in range(4):
                        src = 32 * (quad ^ 1)
                        op = act.activation(swap[32 * quad:32 * quad + 32, :], res[src:src + 32, :], ACT.Copy, scale=scale)
                        if quad < 3:
                            op.then_inc(rope_raw, 1)
                        else:
                            op.then_inc(free[s], 1)
                elif 8 <= i < 10:
                    act.activation(k.v_ret[:, i % 2, :], res, ACT.Copy).then_inc(free[s], 1)
                elif i >= 10:
                    act.activation(k.cat[:, 4 + i % 2, :], res, ACT.Silu).then_inc(free[s], 1)

        @block.vector
        def _(dve):
            dve_diagonal(k, dve, diag).then_inc(diag_ready, 1)
            dve.wait_ge(rb_ready, 1)
            normed.on_dve(dve)
            for kk in range(KD):
                normed.lowered(dve, kk)
            clink = Link(dve, conv_link)
            dve.sem_inc(free[0], 1)
            for j in range(2):
                clink(dve.memset(u[:, j, 0:CTX], 0.0))
            dve.wait_ge(f_done, 1)
            dve.tensor_tensor(z[:, :].rearrange("p (c h) -> p c h", h=HA),
                              misc[0][:, 0:TC * HA].rearrange("p (c h) -> p c h", h=HA), bc(bf[:, :], 1, TC),
                              ALU.add).then_inc(z_link, 1)
            def taps(lo, hi):
                for j, w in todo[lo:hi]:
                    acc = k.cat[:, 6 + j, 0:TP]
                    if w == 0:
                        clink(dve.tensor_scalar(acc, u[:, j, 0:TP], k.vecs[:, 1, j:j + 1],
                                                k.vecs[:, 0, V_CB + j:V_CB + j + 1], ALU.mult, ALU.add))
                    else:
                        clink(dve.scalar_tensor_tensor(acc, u[:, j, w:w + TP], k.vecs[:, 1, 2 * w + j:2 * w + j + 1],
                                                       acc, ALU.mult, ALU.add))

            todo = [(j, w) for j in range(2) for w in range(CONV_W)]
            for j in range(2):
                dve.wait_ge(free[1], 3 + j)
                dve.tensor_tensor(u[:, j, CTX:CTX + NT], slot[0][:, OFF:OFF + NT], sig[:, :], ALU.mult).then_inc(free[0], 1)
                dve.wait_ge(free[0], 2 + j)
                taps(*((0, 17) if j == 0 else (17, 26)))
            dve.wait_ge(act_link, 3)
            dve.scalar_tensor_tensor(k.logf[:, :], z[:, :], 0.0, za[:, :], ALU.min, ALU.subtract).then_inc(logf_ready, 1)
            at = 26
            for i in range(4, 8):
                j, dst = i % 2, (k.q_ret if i < 6 else k.k_ret)
                dve.wait_ge(act_link, i)
                dve.tensor_tensor(dst[:, j, :], dst[:, j, :], rope[:, 0, :], ALU.mult).then_inc(rope_link, 1)
                dve.wait_ge(rope_raw, 3 * (i - 3))
                dve.wait_ge(free[i % 2], {4: 4, 5: 5, 6: 5, 7: 6}[i])
                dve.tensor_tensor(swap[:, :], swap[:, :], rope[:, 1, :], ALU.mult).then_inc(rope_link, 1)
                dve.wait_ge(rope_link, 3 * (i - 4) + 2)
                dve.tensor_tensor(dst[:, j, :], dst[:, j, :], swap[:, :], ALU.add).then_inc(rope_link, 1)
                taps(at, at + 8)
                at += 8
            dve.wait_ge(ctx_turned, 1)
            clink(dve.tensor_copy(cctx[:, :, :], misc[1][:, 0:480].rearrange("p (j n) -> p j n", j=2)))
            for j in range(2):
                w = k.vecs[:, 1, j:j + 2 * CTX:2]
                clink(dve.tensor_tensor(cprod[:, :, :], cctx[:, j, :].rearrange("p (s r) -> p s r", s=S), bc(w, 1, S), ALU.mult))
                clink(dve.tensor_reduce(csum[:, :], cprod[:, :, :], AX_X, ALU.add))
                clink(dve.scalar_tensor_tensor(csum[:, :], u[:, j, CTX + TP:CTX + NT], k.vecs[:, 1, 2 * CTX + j:2 * CTX + j + 1],
                                               csum[:, :], ALU.mult, ALU.add))
                clink(dve.tensor_scalar(k.cat[:, 6 + j, TP:NT], csum[:, :], k.vecs[:, 0, V_CB + j:V_CB + j + 1], None, ALU.add))
            taps(at, len(todo))


def block_retention(k, L):
    nc, d = k.nc, k.dram
    with ExitStack() as ctx:
        sb = lambda n, s, t=F32: ctx.enter_context(nc.sbuf_tensor(n, s, t))
        state = sb("state", [P, 2, DB])
        kz = [sb(f"kz{i}", [P, 2 * P]) for i in range(2)]
        vt = [sb(f"vt{i}", [P, 2 * P]) for i in range(2)]
        att = [sb(f"att{i}", [P, 2, 2 * P]) for i in range(2)]
        qxi = [sb(f"qxi{i}", [P, 2, P]) for i in range(2)]
        s0 = sb("s0", [P, 2, S, DB])
        vst = sb("vst", [P, 2 * S, DB])
        small = sb("small", [P, 2, 2 * S])
        pre = sb("pre", [P, NC8 * HA])
        ps = lambda n, s: ctx.enter_context(nc.psum_tensor(n, s, F32))
        kv_bank = [ps(f"kv_bank{i}", [P, 512]) for i in range(2)]
        sc_bank = [ps(f"sc_bank{i}", [P, 1024]) for i in range(2)]
        o_bank, up_bank = ps("o_bank", [P, 512]), ps("up_bank", [P, 512])
        (state_loaded, turned, scored, kz_done, kv_moved, att_done, qxi_done, o_ready, up_ready, state_done, r_moved,
         pre_link, cum_ready, qk_ready, vst_ready, samp_ready, samp_link, samp_read, cum_read, stored) = (k.sem(n) for n in (
             "state_loaded", "turned", "scored", "kz_done", "kv_moved", "att_done", "qxi_done", "o_ready", "up_ready",
             "state_done", "r_moved", "pre_link", "cum_ready", "qk_ready", "vst_ready", "samp_ready", "samp_link", "samp_read",
             "cum_read", "stored"))
        qr, kr, vr = k.q_ret, k.k_ret, k.v_ret
        block = ctx.enter_context(nc.Block())

        @block.sync
        def _(sp):
            for hh in range(2):
                sp.dma_start(s0[:, hh, :, :], d["state_ret"][L, :, 2 * hh:2 * hh + 2].rearrange(
                    "s h d e -> (h d) s e")).then_inc(state_loaded, 16)
            sp.wait_ge(samp_link, 5)
            for hh in range(2):
                sp.dma_start(d["ret_sample"][L, :, 2 * hh:2 * hh + 2].rearrange("s h d e -> (h d) s e"),
                             s0[:, hh, :, :]).then_inc(stored, 16)
            sp.wait_ge(state_done, 1 + NC8)
            for hh in range(2):
                sp.dma_start(d["ret_prompt"][L, 0, 2 * hh:2 * hh + 2].rearrange("h d e -> (h d) e"),
                             state[:, hh, :]).then_inc(stored, 16)
            sp.wait_ge(stored, 64)

        @block.tensor
        def _(pe):
            ident, pair = const(k, "ident"), const(k, "pair")

            def front(c):
                b = c % 2
                if c >= 2:
                    pe.wait_ge(kv_moved, c - 1)
                    pe.wait_ge(att_done, c - 1)
                if c == 1:
                    pe.wait_ge(samp_link, 3)
                at = slice(P * c, P * c + P)
                for n, src in enumerate((kr, vr)):
                    for hh in range(2):
                        last = pe.transpose(kv_bank[b][:, 256 * n + P * hh:256 * n + P * hh + P], src[:, hh, at], ident)
                last.then_inc(turned, 1)
                for hp in range(2):
                    rows = slice(64 * hp, 64 * hp + 64)
                    for hh in range(2):
                        last = pe.matmul(sc_bank[b][:, 512 * hp + P * hh:512 * hp + P * hh + P], kr[rows, hh, at],
                                         qr[rows, hh, at], start=True, stop=True)
                last.then_inc(scored, 1)

            def back(c):
                b = c % 2
                pe.wait_ge(kv_moved, c + 1)
                pe.wait_ge(att_done, c + 1)
                pe.wait_ge(qxi_done, c + 1)
                pe.wait_ge(state_done, c + 1)
                if c == 0:
                    pe.wait_ge(samp_read, 2)
                    pe.wait_ge(cum_read, 1)
                if c >= 1:
                    pe.wait_ge(r_moved, c)
                for hh in range(2):
                    for hp in range(2):
                        rows = slice(64 * hp, 64 * hp + 64)
                        out = o_bank[rows, P * hh:P * hh + P]
                        pe.matmul(out, vt[b][:, P * hh + 64 * hp:P * hh + 64 * hp + 64],
                                  att[b][:, hp, P * hh:P * hh + P], start=True, stop=False)
                        last = pe.matmul(out, state[rows, hh, :], qxi[b][rows, hh, :], start=False, stop=True)
                last.then_inc(o_ready, 1)
                for hh in range(2):
                    for hp in range(2):
                        cols = slice(P * hh + 64 * hp, P * hh + 64 * hp + 64)
                        last = pe.matmul(up_bank[64 * hp:64 * hp + 64, 64 * hh:64 * hh + 64], kz[b][:, cols], vt[b][:, cols],
                                         start=True, stop=True)
                last.then_inc(up_ready, 1)

            front(0)
            pe.wait_ge(pre_link, NC8)
            pe.matmul(up_bank[:, 0:NC8 * HA], const(k, "upto"), k.logf[:, 0:NC8 * HA], start=True, stop=False)
            pe.matmul(up_bank[:, 0:NC8 * HA], const(k, "ones"), pre[:, :], start=False, stop=True).then_inc(cum_ready, 1)
            pe.wait_ge(qk_ready, 1)
            pe.matmul(kv_bank[1][:, 0:2 * S], pair, small[:, 0, :], start=True, stop=True)
            pe.wait_ge(vst_ready, 1)
            flat = vst[:, :, :].rearrange("p a b -> p (a b)")
            for n in range(2):
                pe.matmul(sc_bank[1][:, 512 * n:512 * n + 512], pair, flat[:, 512 * n:512 * n + 512], start=True, stop=True)
            pe.wait_ge(state_loaded, 32)
            for hh in range(2):
                for s in range(S):
                    for hp in range(2):
                        rows = slice(64 * hp, 64 * hp + 64)
                        last = pe.matmul(o_bank[rows, S * hh + s:S * hh + s + 1], s0[rows, hh, s, :],
                                         qr[rows, hh, TP + s:TP + s + 1], start=True, stop=True)
            last.then_inc(samp_ready, 1)
            for c in range(NC8):
                if c + 1 < NC8:
                    front(c + 1)
                back(c)

        @block.scalar
        def _(act):
            def values(c):
                act.wait_ge(kz_done, c + 1)
                if c >= 2:
                    act.wait_ge(up_ready, c - 1)
                act.activation(vt[c % 2][:, :], kv_bank[c % 2][:, 256:512], ACT.Copy).then_inc(kv_moved, 1)

            values(0)
            for c in range(NC8):
                if c + 1 < NC8:
                    values(c + 1)
                act.wait_ge(o_ready, c + 1)
                act.activation(qr[:, :, P * c:P * c + P], o_bank[:, 0:256].rearrange("p (a b) -> p a b", a=2),
                               ACT.Copy).then_inc(r_moved, 1)

        @block.vector
        def _(dve):
            slink = Link(dve, samp_link)
            zeta, decay, xi = const(k, "zeta"), const(k, "decay"), const(k, "xi")

            def prepare(c):
                b = c % 2
                dve.wait_ge(turned, c + 1)
                if c >= 2:
                    dve.wait_ge(up_ready, c - 1)
                dve.tensor_tensor(kz[b][:, :].rearrange("p (h e) -> p h e", h=HB),
                                  kv_bank[b][:, 0:256].rearrange("p (h e) -> p h e", h=HB), bc(zeta, 2, DB),
                                  ALU.mult).then_inc(kz_done, 1)
                dve.tensor_tensor(qxi[b][:, :, :], qr[:, :, P * c:P * c + P], xi.rearrange("p (a b) -> p a b", a=2),
                                  ALU.mult).then_inc(qxi_done, 1)
                dve.wait_ge(scored, c + 1)
                dve.tensor_tensor(att[b][:, :, :], sc_bank[b][:, :].rearrange("p (a b) -> p a b", a=2)[:, :, 0:256],
                                  decay.rearrange("p (a b) -> p a b", a=2), ALU.mult).then_inc(att_done, 1)

            ks, qs, vs = (b[:, :, TP:NT] for b in (kr, qr, vr))
            sq3 = lambda i: small[:, i, :].rearrange("p (a s) -> p a s", a=2)
            dve.tensor_tensor(sq3(0), qs, ks, ALU.mult).then_inc(qk_ready, 1)
            for hh in range(2):
                op = dve.tensor_tensor(vst[:, S * hh:S * hh + S, :], bc(const(k, "stack"), 1, S), bc(vs[:, hh, :], 2, DB), ALU.mult)
                op.then_inc(k.quiet, 1) if hh == 0 else op.then_inc(vst_ready, 1)
            dve.memset(state[:, :, :], 0.0).then_inc(state_done, 1)
            prepare(0)
            dve.wait_ge(cum_ready, 1)
            dve.tensor_scalar(k.ncum[:, :], up_bank[:, 0:NC8 * HA], -1.0 / A_SCALE, None, ALU.mult).then_inc(cum_read, 1)
            dve.wait_ge(samp_ready, 1)
            slink(dve.tensor_tensor(sq3(1), kv_bank[1][:, 0:2 * S].rearrange("p (a s) -> p a s", a=2), vs, ALU.mult))
            for hh in range(2):
                dve.tensor_tensor(vst[:, S * hh:S * hh + S, :], sc_bank[1][:, 512 * hh:512 * hh + 512].rearrange(
                    "p (s e) -> p s e", s=S), bc(ks[:, hh, :], 2, DB), ALU.mult).then_inc(samp_link, 1)
            for hh in range(2):
                dve.scalar_tensor_tensor(qr[:, hh, TP:NT], o_bank[:, S * hh:S * hh + S], const(k, "gone")[:, hh:hh + 1],
                                         small[:, 1, S * hh:S * hh + S], ALU.mult, ALU.add).then_inc(samp_read, 1)
            dve.wait_ge(samp_link, 3)
            for hh in range(2):
                dve.scalar_tensor_tensor(s0[:, hh, :, :], s0[:, hh, :, :], const(k, "gone")[:, hh:hh + 1],
                                         vst[:, S * hh:S * hh + S, :], ALU.mult, ALU.add).then_inc(samp_link, 1)
            for c in range(NC8):
                if c + 1 < NC8:
                    prepare(c + 1)
                dve.wait_ge(up_ready, c + 1)
                for hh in range(2):
                    op = dve.scalar_tensor_tensor(state[:, hh, :], state[:, hh, :], const(k, "gchunk")[:, hh:hh + 1],
                                                  up_bank[:, 64 * hh:64 * hh + 64], ALU.mult, ALU.add)
                    if hh == 0:
                        op.then_inc(k.quiet, 1)
                    else:
                        op.then_inc(state_done, 1)
                dve.wait_ge(state_done, c + 2)

        @block.gpsimd
        def _(pool):
            plink = Link(pool, pre_link)
            plink(pool.memset(pre[:, 0:HA], 0.0))
            for c in range(1, NC8):
                plink(pool.tensor_tensor(pre[:, HA * c:HA * c + HA], pre[:, HA * c - HA:HA * c], k.logf[:, HA * c - HA:HA * c], ALU.add))


def block_group_norms(k, L):
    nc, d = k.nc, k.dram
    with ExitStack() as ctx:
        sb = lambda n, s, t=F32: ctx.enter_context(nc.sbuf_tensor(n, s, t))
        ps = lambda n, s: ctx.enter_context(nc.psum_tensor(n, s, F32))
        sq = [sb(f"gsq{i}", [P, NT]) for i in range(2)]
        both = sb("gboth", [P, NT])
        diag = [sb(f"gdiag{i}", [P, TC, P]) for i in range(2)]
        n_st = TC * (HB + 1)
        v, y, t = (sb(n, [P, n_st]) for n in ("gv", "gy", "gt"))
        slot = [ps(f"gslot{i}", [P, SLOT]) for i in range(2)]
        st = ps("gst", [P, BANK])
        mean_ready, centred, sq_ready, sq_used, link_v, diag_ready, rb_ready, applied, both_ready = (k.sem(n) for n in (
            "mean_ready", "centred", "sq_ready", "sq_used", "link_v", "diag_ready", "rb_ready", "applied",
            "both_ready"))
        tiles = [k.q_ret[:, 0, :], k.q_ret[:, 1, :], k.cat[:, 6, :], k.cat[:, 7, :]]
        block = ctx.enter_context(nc.Block())
        w_in = d["w_in"][L].rearrange("(k p) n -> p k n", p=P)
        ahead = Ahead(k, [w_in[:, :, 2 * HA * DA:2 * HA * DA + P], w_in[:, :, 0:P]])
        v3 = lambda a: a[:, 0:TC * HB].rearrange("p (c h) -> p c h", h=HB)

        @block.sync
        def _(sp):
            ahead.load(sp)

        @block.gpsimd
        def _(pool):
            ahead.low(pool)

        @block.tensor
        def _(pe):
            ones, pair = const(k, "ones"), const(k, "pair")
            for j in range(2):
                for a, b in CHUNKS:
                    last = pe.matmul(slot[j][:, OFF + a:OFF + b], pair, tiles[j][:, a:b], start=True, stop=True)
                last.then_inc(mean_ready, 1)
            pe.wait_ge(centred, 1)
            pe.wait_ge(both_ready, 1)
            for a, b in CHUNKS:
                last = pe.matmul(slot[0][:, OFF + a:OFF + b], ones, both[:, a:b], start=True, stop=True)
            last.then_inc(mean_ready, 1)
            for n in range(3):
                if n < 2:
                    pe.wait_ge(sq_ready, n + 1)
                else:
                    pe.wait_ge(both_ready, 2)
                src = sq[n] if n < 2 else both
                for c in range(TC):
                    w = min(P, NT - c * P)
                    if n < 2:
                        out, rhs = st[0:w, HB * c + 2 * n:HB * c + 2 * n + 2], const(k, "headsel")
                    else:
                        out, rhs = st[0:w, TC * HB + c:TC * HB + c + 1], ones[:, 0:1]
                    last = pe.matmul(out, src[:, c * P:c * P + w], rhs, start=(n == 0 and c == 0), stop=True,
                                     skip_group_check=True)
                last.then_inc(sq_used, 1)
            for j in range(3):
                if j == 2:
                    pe.wait_ge(applied, 1)
                for hp in range(2 if j < 2 else 1):
                    n = 2 * j + hp
                    pe.wait_ge(diag_ready, n + 1)
                    flat = diag[n % 2][:, :, :].rearrange("p a b -> p (a b)")
                    for a, b in CHUNKS:
                        out = slot[j % 2][64 * hp:64 * hp + 64, OFF + a:OFF + b] if j < 2 else slot[0][:, OFF + a:OFF + b]
                        last = pe.matmul(out, ones[:, 0:64] if j < 2 else ones, flat[:, a:b], start=True, stop=True)
                    last.then_inc(rb_ready, 1)

        @block.scalar
        def _(act):
            ahead.high(act)
            for n in range(4):
                act.wait_ge(centred, (1, 2, 4, 4)[n])
                if n >= 2:
                    act.wait_ge(sq_used, n - 1)
                act.activation(sq[n % 2][:, :], tiles[n], ACT.Square).then_inc(sq_ready, 1)
            for j in range(2):
                act.wait_ge(applied, 5 + j)
                act.activation(k.cat[:, 6 + j, :], k.cat[:, 6 + j, :], ACT.Silu, scale=k.vecs[:, 0, V_LG + j:V_LG + j + 1],
                               bias=k.vecs[:, 0, V_LB + j:V_LB + j + 1]).then_inc(k.quiet, 1)

        @block.vector
        def _(dve):
            link = Link(dve, link_v)
            dve.tensor_tensor(both[:, :], tiles[2], tiles[3], ALU.add).then_inc(both_ready, 1)
            for j in range(2):
                dve.wait_ge(mean_ready, j + 1)
                dve.scalar_tensor_tensor(tiles[j], slot[j][:, OFF:OFF + NT], -1.0 / DB, tiles[j], ALU.mult, ALU.add).then_inc(centred, 1)
            dve.wait_ge(mean_ready, 3)
            for j in range(2, 4):
                dve.scalar_tensor_tensor(tiles[j], slot[0][:, OFF:OFF + NT], -1.0 / DC, tiles[j], ALU.mult, ALU.add).then_inc(centred, 1)
            dve.wait_ge(sq_ready, 4)
            dve.tensor_tensor(both[:, :], sq[0][:, :], sq[1][:, :], ALU.add).then_inc(both_ready, 1)
            dve.wait_ge(sq_used, 3)
            link(dve.memset(v[:, :], 1.0))
            for at, n, scale in ((0, HB, 1.0 / DB), (TC * HB, 1, 1.0 / DC)):
                link(dve.tensor_scalar(v[:, at:at + NC8 * n], st[:, at:at + NC8 * n], scale, EPS, ALU.mult, ALU.add))
                link(dve.tensor_scalar(v[0:S, at + NC8 * n:at + TC * n], st[0:S, at + NC8 * n:at + TC * n], scale, EPS,
                                       ALU.mult, ALU.add))
            rsqrt(dve, link, y[:, :], v[:, :], t[:, :])
            for n in range(HB + 1):
                if n >= 2:
                    dve.wait_ge(rb_ready, n - 1)
                row = v3(y)[:, :, n] if n < HB else y[:, TC * HB:n_st]
                dve.tensor_tensor(diag[n % 2][:, :, :], bc(const(k, "ident"), 1, TC), bc(row, 2, P), ALU.mult).then_inc(diag_ready, 1)
                if n in (2, 4):
                    j = n // 2 - 1
                    dve.wait_ge(rb_ready, 2 * j + 2)
                    dve.tensor_tensor(tiles[j], tiles[j], slot[j][:, OFF:OFF + NT], ALU.mult).then_inc(applied, 1)
                    dve.wait_ge(applied, 2 * j + 1)
                    dve.scalar_tensor_tensor(k.cat[:, 4 + j, :], tiles[j], k.vecs[:, 0, V_GN + j:V_GN + j + 1],
                                             k.cat[:, 4 + j, :], ALU.mult, ALU.mult).then_inc(applied, 1)
            dve.wait_ge(rb_ready, 5)
            for j in range(2):
                dve.tensor_tensor(tiles[2 + j], tiles[2 + j], slot[0][:, OFF:OFF + NT], ALU.mult).then_inc(applied, 1)


MOVES = [i if i <= 4 else 2 * i - 4 for i in range(NC8 + 1)]


def block_heads(k, L):
    nc, d = k.nc, k.dram
    with ExitStack() as ctx:
        sb = lambda n, s, t=F32: ctx.enter_context(nc.sbuf_tensor(n, s, t))
        ps = lambda n, s: ctx.enter_context(nc.psum_tensor(n, s, F32))
        q, kk_, v = sb("q", [P, NT]), sb("kf", [P, NT]), sb("vf", [P, NT])
        k_tok, v_tok = sb("k_tok", [P, NC8, P]), sb("v_tok", [P, NC8, P])
        bias = sb("bias", [P, TP])
        prob = [sb(f"prob{i}", [P, TP]) for i in range(2)]
        prob_t = sb("prob_t", [P, NC8, P])
        diag = prob_t
        kv_new = sb("kv_new", [S, 2, P])
        mx, nb, rs, rr = (sb(n, [P, 2]) for n in ("mx", "nb", "rs", "rr"))
        slot = [ps(f"hslot{i}", [P, SLOT]) for i in range(2)]
        misc = [ps(f"hmisc{i}", [P, 512]) for i in range(2)]
        raw_ready = [k.sem("raw_ready0"), k.sem("raw_ready1")]
        (hi_done, lo_done, tile_done, moved, turned, tok_moved, diag_ready, bias_ready, bias_moved, scored, top, neg, expd,
         summed, normed, p_turned, p_moved, o_ready, o_moved, stored, passed) = (k.sem(n) for n in (
             "hi_done", "lo_done", "tile_done", "moved", "turned", "tok_moved", "diag_ready", "bias_ready", "bias_moved",
             "scored", "top", "neg", "expd", "summed", "normed", "p_turned", "p_moved", "o_ready", "o_moved", "stored",
             "passed_h"))
        block = ctx.enter_context(nc.Block())
        cols = [2 * HA * DA, 0, HA * DA]
        N_TILE, N_TOK, N_Q = 3, 5, NC8

        @block.sync
        def _(sp):
            w_in = d["w_in"][L].rearrange("(k p) n -> p k n", p=P)

            def load(h, t):
                gated(sp, lo_done, h * N_TILE + (t + 1 if t else 2), passed)
                sp.dma_start(k.w_raw[t % 2][:, :, :], w_in[:, :, bass.ds(h * DA + cols[t], DA)]).then_inc(raw_ready[t % 2], 16)

            def store(h):
                gated(sp, tok_moved, h * N_TOK + 5, passed)
                sp.dma_start(d["k_prompt"][L, 0, :, bass.ds(h, 1), :].rearrange("(c p) o n -> p c (o n)", p=P), k_tok[:, :, :]).then_inc(stored, 16)
                sp.dma_start(d["v_prompt"][L, 0, :, bass.ds(h, 1), :].rearrange("(c p) o n -> p c (o n)", p=P), v_tok[:, :, :]).then_inc(stored, 16)
                sp.dma_start(d["k_sample"][L, :, 0, bass.ds(h, 1), :].rearrange("s o n -> s (o n)"), kv_new[:, 0, :]).then_inc(stored, 16)
                sp.dma_start(d["v_sample"][L, :, 0, bass.ds(h, 1), :].rearrange("s o n -> s (o n)"), kv_new[:, 1, :]).then_inc(stored, 16)

            load(0, 2)
            store(0)
            with sp.Fori(0, HA - 1) as h:
                for t in range(3):
                    load(h + 1, t)
                store(h + 1)
            sp.wait_ge(stored, 64 * HA + 16)

        @block.gpsimd
        def _(pool):
            for _ in range(4):
                pool.sem_inc(lo_done, 1)

            def low(h, t):
                gated(pool, hi_done, h * N_TILE + (t + 1), passed)
                gated(pool, tile_done, h * N_TILE + (t + 1 if t else 2), passed)
                pool.tensor_tensor(k.w_lo[t % 2][:, :, :], k.w_raw[t % 2][:, :, :], k.w_hi[t % 2][:, :, :].bitcast(F32),
                                   ALU.subtract).then_inc(lo_done, 1)

            low(0, 2)
            with pool.Fori(0, HA - 1) as h:
                for t in range(3):
                    low(h + 1, t)

        @block.tensor
        def _(pe):
            ident, ones = const(k, "ident"), const(k, "ones")
            pe.sem_inc(tile_done, 1)
            pe.sem_inc(tile_done, 1)

            def turn_blocks(h, src, banks):
                for half in range(2):
                    for j in range(4):
                        c = 4 * half + j
                        last = pe.transpose(banks[half][:, P * j:P * j + P], src[:, P * c:P * c + P], ident)
                    last.then_inc(turned, 1)

            with pe.Fori(0, HA) as h:
                pe.wait_ge(o_moved, h * N_Q + 1)
                for t in range(3):
                    pe.wait_ge(lo_done, h * N_TILE + (t + 3))
                    if t == 2:
                        pe.wait_ge(moved, h * 3 + 1)
                        turn_blocks(h, v, misc)
                    product3(pe, slot[t % 2], k.w_hi[t % 2], k.w_lo[t % 2], k.h_hi, k.h_lo, KD, slice(0, P)).then_inc(tile_done, 1)
                pe.wait_ge(moved, h * 3 + 2)
                pe.wait_ge(diag_ready, h + 1)
                flat = diag[:, :, :].rearrange("p a b -> p (a b)")
                for a, b in HALVES:
                    last = pe.matmul(slot[1][:, a:b], ones, flat[:, a:b], start=True, stop=True)
                last.then_inc(bias_ready, 1)
                pe.wait_ge(moved, h * 3 + 3)
                pe.wait_ge(tok_moved, h * N_TOK + 2)
                for n, src in enumerate((kk_, v)):
                    last = pe.matmul(misc[1][0:S, P * n:P * n + P], src[:, TP:NT], ident, start=True, stop=True)
                last.then_inc(turned, 1)

                def scores(i):
                    if i == 1:
                        pe.wait_ge(bias_moved, h + 1)
                    elif i > 1:
                        pe.wait_ge(top, h * N_Q + (i - 1))
                    n = P * (i + 1)
                    pe.matmul(slot[i % 2][:, n - P:n], k.ident_bf[:, :], k.mask_bf[:, :], start=True, stop=False,
                              skip_group_check=True)
                    for a, b in HALVES:
                        if a < n:
                            last = pe.matmul(slot[i % 2][:, a:min(b, n)], q[:, P * i:P * i + P], kk_[:, a:min(b, n)],
                                             start=(b < n), stop=True, skip_group_check=True)
                    last.then_inc(scored, 1)

                scores(0)
                scores(1)
                turn_blocks(h, kk_, [s[:, 1024:1536] for s in slot])
                for i in range(NC8):
                    pe.wait_ge(normed, h * N_Q + (i + 1))
                    banks = (i >= 4) + 1
                    for bank in range(banks):
                        if bank == 1 and i == 4:
                            pe.wait_ge(tok_moved, h * N_TOK + 3)
                        for c in range(4 * bank, min(4 * bank + 4, i + 1)):
                            last = pe.transpose(misc[bank][:, P * (c % 4):P * (c % 4) + P], prob[i % 2][:, P * c:P * c + P], ident)
                        last.then_inc(p_turned, 1)
                    if i + 2 < NC8:
                        scores(i + 2)
                    pe.wait_ge(p_moved, h * 12 + MOVES[i + 1])
                    if i >= 2:
                        pe.wait_ge(o_moved, h * N_Q + i)
                    else:
                        pe.wait_ge(tok_moved, h * N_TOK + (4 + i))
                    out = slot[i % 2][:, 1024:1024 + P]
                    for c in range(i + 1):
                        last = pe.matmul(out, v_tok[:, c, :], prob_t[:, c, :], start=(c == 0), stop=(c == i))
                    last.then_inc(o_ready, 1)

        @block.scalar
        def _(act):
            def hi(h, t):
                gated(act, raw_ready[t % 2], h * (32 if t % 2 == 0 else 16) + (32 if t == 2 else 16), passed)
                gated(act, tile_done, h * N_TILE + (t + 1 if t else 2), passed)
                act.activation(k.w_hi[t % 2][:, :, :], k.w_raw[t % 2][:, :, :], ACT.Copy).then_inc(hi_done, 1)

            def head(h, more):
                def move(t, dst):
                    gated(act, tile_done, h * N_TILE + (t + 3), passed)
                    act.activation(dst[:, :], slot[t % 2][:, OFF:OFF + NT], ACT.Copy).then_inc(moved, 1)

                def move_blocks(dst, half, bank, count):
                    gated(act, turned, h * N_TOK + count, passed)
                    act.activation(dst[:, 4 * half:4 * half + 4, :], bank.rearrange("p (c n) -> p c n", c=4),
                                   ACT.Copy).then_inc(tok_moved, 1)

                move(0, v)
                hi(h, 2)
                gated(act, stored, h * 64 + 16, passed)
                move(1, q)
                for half in range(2):
                    move_blocks(v_tok, half, misc[half][:, :], 1 + half)
                move(2, kk_)
                gated(act, bias_ready, h + 1, passed)
                act.activation(bias[:, :], slot[1][:, 0:TP], ACT.Copy).then_inc(bias_moved, 1)
                gated(act, turned, h * N_TOK + 3, passed)
                act.activation(kv_new[:, :, :], misc[1][0:S, 0:2 * P].rearrange("p (a n) -> p a n", a=2), ACT.Copy).then_inc(tok_moved, 1)

                def exp(i):
                    gated(act, neg, h * N_Q + (i + 1), passed)
                    n = P * (i + 1)
                    act.activation(prob[i % 2][:, 0:n], prob[i % 2][:, 0:n], ACT.Exp, scale=A_SCALE, bias=nb[:, i % 2:i % 2 + 1],
                                   accum_out=rs[:, i % 2:i % 2 + 1]).then_inc(expd, 1)

                for half in range(2):
                    exp(half)
                    move_blocks(k_tok, half, slot[half][:, 1024:1536], 4 + half)
                for i in range(NC8):
                    if i == 0:
                        gated(act, bias_ready, h + 1, passed)
                    else:
                        gated(act, o_ready, h * N_Q + i, passed)
                    for bank in range((i >= 4) + 1):
                        gated(act, p_turned, h * 12 + (MOVES[i] + bank + 1), passed)
                        n = min(4, i + 1 - 4 * bank)
                        act.activation(prob_t[:, 4 * bank:4 * bank + n, :], misc[bank][:, 0:P * n].rearrange("p (c n) -> p c n", n=P),
                                       ACT.Copy).then_inc(p_moved, 1)
                    if i + 2 < NC8:
                        exp(i + 2)
                    if more and i in (2, 3):
                        hi(h + 1, i - 2)

            for s in range(2):
                act.sem_inc(raw_ready[s], 16)
                act.sem_inc(hi_done, 1)
            with act.Fori(0, HA - 1) as h:
                head(h, True)
            head(HA - 1, False)

        @block.vector
        def _(dve):
            dve.sem_inc(o_moved, 1)
            dve.sem_inc(stored, 16)
            with dve.Fori(0, HA) as h:
                hs = bass.ds(h, 1)
                dve.wait_ge(o_moved, h * N_Q + 1)
                row = k.ncum[:, :].rearrange("p (c h) -> p c h", h=HA)[:, :, hs]
                dve.tensor_tensor(diag[:, :, :], bc(const(k, "ident"), 1, NC8), row.to_broadcast([P, NC8, P]),
                                  ALU.mult).then_inc(diag_ready, 1)
                for t, (src, dst) in enumerate(((v, k.v_new), (q, k.q_new), (kk_, k.k_new))):
                    dve.wait_ge(moved, h * 3 + (t + 1))
                    dve.tensor_copy(dst[:, hs, :].rearrange("p o s -> p (o s)"), src[:, TP:NT]).then_inc(k.quiet, 1)
                dve.wait_ge(bias_moved, h + 1)

                def top_of(i):
                    gated(dve, scored, h * N_Q + (i + 1), passed)
                    if i >= 2:
                        gated(dve, p_turned, h * 12 + MOVES[i - 1], passed)
                    n = P * (i + 1)
                    dve.tensor_tensor_reduce(out=prob[i % 2][:, 0:n], in0=slot[i % 2][:, 0:n], in1=bias[:, 0:n], scale=1.0,
                                             scalar=-3e38, op0=ALU.add, op1=ALU.max, accum_out=mx[:, i % 2:i % 2 + 1]).then_inc(top, 1)
                    gated(dve, top, h * N_Q + (i + 1), passed)
                    dve.tensor_scalar(nb[:, i % 2:i % 2 + 1], mx[:, i % 2:i % 2 + 1], -A_SCALE, None, ALU.mult).then_inc(neg, 1)

                def out_of(i):
                    dve.wait_ge(o_ready, h * N_Q + (i + 1))
                    dve.tensor_copy(k.cat[:, hs, P * i:P * i + P].rearrange("p o n -> p (o n)"),
                                    slot[i % 2][:, 1024:1024 + P]).then_inc(o_moved, 1)

                def normalize(i):
                    dve.wait_ge(expd, h * N_Q + (i + 1))
                    dve.reciprocal(rr[:, i % 2:i % 2 + 1], rs[:, i % 2:i % 2 + 1]).then_inc(summed, 1)
                    dve.wait_ge(summed, h * N_Q + (i + 1))
                    n = P * (i + 1)
                    dve.tensor_scalar(prob[i % 2][:, 0:n], prob[i % 2][:, 0:n], rr[:, i % 2:i % 2 + 1], None, ALU.mult).then_inc(normed, 1)

                top_of(0)
                top_of(1)
                normalize(0)
                for i in range(NC8):
                    if i + 1 < NC8:
                        normalize(i + 1)
                    if i + 2 < NC8:
                        top_of(i + 2)
                    out_of(i)


def block_samples(k, L):
    nc, d = k.nc, k.dram
    R = S * HA
    with ExitStack() as ctx:
        sb = lambda n, s, t=F32: ctx.enter_context(nc.sbuf_tensor(n, s, t))
        ps = lambda n, s: ctx.enter_context(nc.psum_tensor(n, s, F32))
        kp = sb("kp", [P, S, NPG, HA * DA])
        vp = sb("vpg", [P, S, NPG, HA * DA])
        lf = sb("lf", [P, S, NPG, HA])
        e_new = sb("e_new", [P, S, HA])
        qd = [sb(f"qd{i}", [P, HA, P]) for i in range(2)]
        prod = [sb(f"prod{i}", [P, NPG, HA * DA]) for i in range(2)]
        lg = sb("lg", [P, NPG, S, HA])
        qk = sb("qk", [P, S, HA])
        rows = sb("rows", [R, PAST + 1])
        one = sb("one", [R, 4])
        pt = sb("pt", [P, NPG, S * (R + HA)])
        orow = sb("orow", [R, HA * DA])
        dnew = sb("dnew", [R, R])
        vn = sb("vn", [P, S, HA])
        q_bank = [ps(f"q_bank{i}", [P, 512]) for i in range(2)]
        b_bank, r_bank, t_bank, o_bank, n_bank = (ps(n, [P, 512]) for n in ("b_bank", "r_bank", "t_bank", "so_bank", "n_bank"))
        k_loaded = [k.sem(f"k_loaded{i}") for i in range(S)]
        (lf_loaded, v_loaded, qd_ready, q_ready, prod_done, lg_done, e_ready, b_ready, lg_ready, qk_ready, rows_ready,
         rows_link, neg_ready, exp_done, prob_ready, pt_ready, pt_moved, o_ready, orow_ready, turned) = (k.sem(n) for n in (
             "lf_loaded", "v_loaded", "qd_ready", "q_ready", "prod_done", "lg_done", "e_ready", "b_ready", "lg_ready",
             "qk_ready", "rows_ready", "rows_link", "neg_ready", "exp_done", "prob_ready", "pt_ready", "pt_moved", "o_ready",
             "orow_ready", "turned"))
        block = ctx.enter_context(nc.Block())
        w_o = d["w_o"][L].rearrange("(k p) n -> p k n", p=P)
        ahead = Ahead(k, [w_o[:, :, P * i:P * i + P] for i in range(2)])
        N_POOL = d["cache_k"].shape[1]

        @block.sync
        def _(sp):
            for s in range(S):
                for pg in range(NPG):
                    page = sp.value_load(k.pages[0:1, NPG * s + pg:NPG * s + pg + 1], min_val=0, max_val=N_POOL - 1)
                    sp.dma_start(kp[:, s, pg, :], d["cache_k"][L, bass.ds(page, 1)].rearrange("o p h n -> p (o h n)")).then_inc(k_loaded[s], 16)
            for s in range(0, S, 2):
                for pg in range(NPG):
                    page = sp.value_load(k.pages[0:1, NPG * s + pg:NPG * s + pg + 1], min_val=0, max_val=N_POOL - 1)
                    sp.dma_start(vp[:, s, pg, :], d["cache_v"][L, bass.ds(page, 1)].rearrange("o p h n -> p (o h n)")).then_inc(v_loaded, 16)
            ahead.load(sp)

        @block.tensor
        def _(pe):
            ident, ones, after = const(k, "ident"), const(k, "ones"), const(k, "after")
            for s in range(S):
                pe.wait_ge(qd_ready, s + 1)
                if s >= 2:
                    pe.wait_ge(prod_done, s - 1)
                pe.matmul(q_bank[s % 2][:, :], ones, qd[s % 2][:, :, :].rearrange("p h n -> p (h n)"), start=True,
                          stop=True).then_inc(q_ready, 1)
            pe.wait_ge(lf_loaded, 16 * S * NPG)
            pe.wait_ge(e_ready, 1)
            new = e_new[:, :, :]
            for pg in range(NPG):
                out = b_bank[:, R * pg:R * pg + R]
                pe.matmul(out, after, lf[:, :, pg, :], start=True, stop=False)
                for later in range(pg + 1, NPG):
                    pe.matmul(out, ones, lf[:, :, later, :], start=False, stop=False)
                last = pe.matmul(out, ones, new, start=False, stop=True)
            last.then_inc(b_ready, 1)
            pe.wait_ge(lg_ready, 1)
            for pg in range(NPG):
                pe.matmul(r_bank[0:R, P * pg:P * pg + P], lg[:, pg, :, :].rearrange("p s h -> p (s h)"), ident, start=True, stop=True)
            pe.wait_ge(qk_ready, 1)
            pe.matmul(r_bank[0:R, PAST:PAST + 1], qk[:, :, :].rearrange("p s h -> p (s h)"), ones[:, 0:1], start=True,
                      stop=True).then_inc(rows_ready, 1)
            pe.wait_ge(prob_ready, 2)
            for pg in range(NPG):
                pe.matmul(t_bank[:, R * pg:R * pg + R], rows[:, P * pg:P * pg + P], ident[0:R, 0:R], start=True, stop=True)
            pe.matmul(n_bank[:, 0:R], ones[0:R, :], dnew[:, :], start=True, stop=True).then_inc(pt_ready, 1)
            pe.wait_ge(pt_moved, 1)
            pe.wait_ge(v_loaded, 16 * S * NPG)
            for s in range(S):
                for pg in range(NPG):
                    n = s * NPG + pg
                    last = pe.matmul(o_bank[0:R, :], pt[:, pg, R * s:R * s + R], vp[:, s, pg, :], start=(n == 0),
                                     stop=(n == S * NPG - 1))
            last.then_inc(o_ready, 1)
            pe.wait_ge(orow_ready, 1)
            for h in range(HA):
                last = pe.matmul(q_bank[0][:, S * h:S * h + S], orow[:, DA * h:DA * h + DA], ident[0:R, h:R:HA], start=True, stop=True)
            last.then_inc(turned, 1)

        @block.scalar
        def _(act):
            for s in range(S):
                for pg in range(NPG):
                    page = act.value_load(k.pages[0:1, NPG * s + pg:NPG * s + pg + 1], min_val=0, max_val=N_POOL - 1)
                    act.dma_start(lf[:, s, pg, :], d["cache_logf"][L, bass.ds(page, 1)].rearrange("o p h -> p (o h)")).then_inc(lf_loaded, 16)
            for s in range(1, S, 2):
                for pg in range(NPG):
                    page = act.value_load(k.pages[0:1, NPG * s + pg:NPG * s + pg + 1], min_val=0, max_val=N_POOL - 1)
                    act.dma_start(vp[:, s, pg, :], d["cache_v"][L, bass.ds(page, 1)].rearrange("o p h n -> p (o h n)")).then_inc(v_loaded, 16)
            act.wait_ge(neg_ready, 1)
            act.activation(rows[:, :], rows[:, :], ACT.Exp, bias=one[:, 1:2], accum_out=one[:, 2:3]).then_inc(exp_done, 1)
            ahead.high(act)
            act.wait_ge(o_ready, 1)
            act.activation(orow[:, :], o_bank[0:R, :], ACT.Copy).then_inc(orow_ready, 1)

        @block.gpsimd
        def _(pool):
            pool.memset(pt[:, :, :], 0.0).then_inc(k.zeroed, 1)
            for s in range(S):
                if s >= 2:
                    pool.wait_ge(q_ready, s - 1)
                pool.tensor_tensor(qd[s % 2][:, :, :], bc(const(k, "ident"), 1, HA), bc(k.q_new[:, :, s], 2, P),
                                   ALU.mult).then_inc(qd_ready, 1)
            ahead.low(pool)

        @block.vector
        def _(dve):
            link = Link(dve, rows_link)
            dve.tensor_tensor(e_new[:, :, :], bc(const(k, "sampsel"), 2, HA), bc(k.logf[:, 8 * HA:9 * HA], 1, S), ALU.mult).then_inc(e_ready, 1)
            dve.tensor_tensor(qk[:, :, :], k.q_new[:, :, :].rearrange("p h s -> p s h"), k.k_new[:, :, :].rearrange("p h s -> p s h"),
                              ALU.mult).then_inc(qk_ready, 1)
            for s in range(S):
                dve.wait_ge(k_loaded[s], 16 * NPG)
                dve.wait_ge(q_ready, s + 1)
                if s >= 2:
                    dve.wait_ge(lg_done, s - 1)
                dve.tensor_tensor(prod[s % 2][:, :, :], kp[:, s, :, :], bc(q_bank[s % 2][:, :], 1, NPG), ALU.mult).then_inc(prod_done, 1)
                dve.wait_ge(prod_done, s + 1)
                dve.tensor_reduce(lg[:, :, s, :], prod[s % 2][:, :, :].rearrange("p g (h n) -> p g h n", h=HA), AX_X,
                                  ALU.add).then_inc(lg_done, 1)
            dve.wait_ge(b_ready, 1)
            dve.wait_ge(lg_done, S)
            flat = lg[:, :, :, :].rearrange("p g s h -> p (g s h)")
            dve.scalar_tensor_tensor(flat, flat, A_SCALE, b_bank[:, 0:NPG * R], ALU.mult, ALU.add).then_inc(lg_ready, 1)
            dve.wait_ge(rows_ready, 1)
            link(dve.tensor_copy(rows[:, 0:PAST], r_bank[0:R, 0:PAST]))
            link(dve.tensor_scalar(rows[:, PAST:PAST + 1], r_bank[0:R, PAST:PAST + 1], A_SCALE, None, ALU.mult))
            link(dve.tensor_reduce(one[:, 0:1], rows[:, :], AX_X, ALU.max))
            dve.tensor_scalar(one[:, 1:2], one[:, 0:1], -1.0, None, ALU.mult).then_inc(neg_ready, 1)
            dve.wait_ge(exp_done, 1)
            link(dve.reciprocal(one[:, 3:4], one[:, 2:3]))
            dve.tensor_scalar(rows[:, :], rows[:, :], one[:, 3:4], None, ALU.mult).then_inc(prob_ready, 1)
            dve.wait_ge(prob_ready, 1)
            dve.tensor_scalar(dnew[:, :], const(k, "ident")[0:R, 0:R], rows[:, PAST:PAST + 1], None, ALU.mult).then_inc(prob_ready, 1)
            dve.wait_ge(pt_ready, 1)
            dve.wait_ge(k.zeroed, 1)
            dve.tensor_copy(pt[:, :, :].rearrange("p g (s x) -> p g s x", s=S)[:, :, :, 0:HA],
                            t_bank[:, 0:NPG * R].rearrange("p (g s h) -> p g s h", g=NPG, s=S)).then_inc(pt_moved, 1)
            link(dve.tensor_tensor(vn[:, :, :], k.v_new[:, :, :].rearrange("p h s -> p s h"),
                                   n_bank[:, 0:R].rearrange("p (s h) -> p s h", h=HA), ALU.mult))
            dve.wait_ge(turned, 1)
            dve.tensor_tensor(k.cat[:, 0:HA, TP:NT], vn[:, :, :].rearrange("p s h -> p h s"),
                              q_bank[0][:, 0:R].rearrange("p (h s) -> p h s", h=HA), ALU.add).then_inc(k.quiet, 1)


def block_output(k, L):
    nc, d = k.nc, k.dram
    with ExitStack() as ctx:
        ps = lambda n, s: ctx.enter_context(nc.psum_tensor(n, s, F32))
        slot = [ps(f"oslot{i}", [P, SLOT]) for i in range(2)]
        st = ps("ost", [P, BANK])
        sb = lambda n, s: ctx.enter_context(nc.sbuf_tensor(n, s, F32))
        sq, acc = [sb(f"osq{i}", [P, NT]) for i in range(2)], sb("oacc", [P, NT])
        v, t = sb("ov", [P, TC]), sb("ot", [P, TC])
        raw_ready = [k.sem("raw_ready0"), k.sem("raw_ready1")]
        x_hi, x_lo, hi_done, lo_done, tile_done, moved, passed, sq_ready, summed, sums_ready, link_v = (k.sem(n) for n in (
            "x_hi", "x_lo", "hi_done", "lo_done", "tile_done", "moved", "passed_o", "sq_ready", "summed", "sums_ready", "link_v"))
        block = ctx.enter_context(nc.Block())

        @block.sync
        def _(sp):
            w = d["w_o"][L].rearrange("(k p) n -> p k n", p=P)
            with sp.Fori(0, KD // 2 - 1) as i:
                for s in range(2):
                    gated(sp, lo_done, i * 2 + (s + 3), passed)
                    sp.dma_start(k.w_raw[s][:, :, :], w[:, :, bass.ds((i * 2 + (s + 2)) * P, P)]).then_inc(raw_ready[s], 16)

        @block.gpsimd
        def _(pool):
            for _ in range(4):
                pool.sem_inc(lo_done, 1)
            with pool.Fori(0, KD // 2 - 1) as i:
                for s in range(2):
                    gated(pool, hi_done, i * 2 + (s + 3), passed)
                    gated(pool, tile_done, i * 2 + (s + 3), passed)
                    pool.tensor_tensor(k.w_lo[s][:, :, :], k.w_raw[s][:, :, :], k.w_hi[s][:, :, :].bitcast(F32),
                                       ALU.subtract).then_inc(lo_done, 1)

        @block.tensor
        def _(pe):
            pe.sem_inc(tile_done, 1)
            pe.sem_inc(tile_done, 1)
            with pe.Fori(0, KD // 2) as i:
                for s in range(2):
                    pe.wait_ge(lo_done, i * 2 + (s + 3))
                    pe.wait_ge(moved, i * 2 + (s + 1))
                    product3(pe, slot[s], k.w_hi[s], k.w_lo[s], k.h_hi, k.h_lo, KD, slice(0, P),
                             lambda e, kk: e.wait_ge(x_lo, kk + 1)).then_inc(tile_done, 1)
            pe.wait_ge(summed, 1 + KD)
            pe_token_sums(k, pe, st, acc, True, True).then_inc(sums_ready, 1)

        @block.scalar
        def _(act):
            act.sem_inc(moved, 1)
            act.sem_inc(moved, 1)

            def hi(i, s):
                gated(act, raw_ready[s], i * 16 + 16, passed)
                gated(act, tile_done, i * 2 + (s + 1), passed)
                act.activation(k.w_hi[s][:, :, :], k.w_raw[s][:, :, :], ACT.Copy).then_inc(hi_done, 1)

            for s in range(2):
                act.sem_inc(raw_ready[s], 16)
                act.sem_inc(hi_done, 1)
            for kk in range(KD):
                act.activation(k.h_hi[:, kk, :], k.cat[:, kk, :], ACT.Copy).then_inc(x_hi, 1)

            def finish(i, more):
                for s in range(2):
                    gated(act, tile_done, i * 2 + (s + 3), passed)
                    gated(act, summed, i * 2 + (s + 1), passed)
                    act.activation(sq[s][:, :], slot[s][:, OFF:OFF + NT], ACT.Square).then_inc(sq_ready, 1)
                    act.activation(k.cat[:, bass.ds(i * 2 + s, 1), :].rearrange("p o n -> p (o n)"), slot[s][:, OFF:OFF + NT],
                                   ACT.Copy).then_inc(moved, 1)
                    if more:
                        hi(i + 1, s)

            with act.Fori(0, KD // 2 - 1) as i:
                finish(i, True)
            finish(KD // 2 - 1, False)

        @block.vector
        def _(dve):
            for kk in range(KD):
                dve.wait_ge(x_hi, kk + 1)
                dve.tensor_tensor(k.h_lo[:, kk, :], k.cat[:, kk, :], k.h_hi[:, kk, :].bitcast(F32), ALU.subtract).then_inc(x_lo, 1)
            dve.memset(acc[:, :], 0.0).then_inc(summed, 1)
            with dve.Fori(0, KD // 2) as i:
                for s in range(2):
                    dve.wait_ge(sq_ready, i * 2 + (s + 1))
                    dve.wait_ge(summed, i * 2 + (s + 1))
                    dve.tensor_tensor(acc[:, :], acc[:, :], sq[s][:, :], ALU.add).then_inc(summed, 1)
            link = Link(dve, link_v)
            dve.wait_ge(sums_ready, 1)
            dve_inverse_rms(k, dve, link, st, v, t)


SLOT_OF = (1, 0, 1, 0, 0, 1, 0, 1)
LAST_USE = [(FT - 1) * 5 + 1 + m // 2 for m in range(KD)]


def block_ffn(k, L):
    nc, d = k.nc, k.dram
    with ExitStack() as ctx:
        sb = lambda n, s, t=F32: ctx.enter_context(nc.sbuf_tensor(n, s, t))
        ps = lambda n, s: ctx.enter_context(nc.psum_tensor(n, s, F32))
        raw = sb("raw", [P, NT])
        t_ab = [sb(f"t_ab{i}", [P, NT]) for i in range(2)]
        f_hi, f_lo = ([sb(f"f_{n}{i}", [P, NT], F32R) for i in range(2)] for n in ("hi", "lo"))
        d_raw = sb("d_raw", [P, D_MODEL])
        d_hi, d_lo = sb("d_hi", [P, D_MODEL], F32R), sb("d_lo", [P, D_MODEL], F32R)
        srow = sb("srow", [2 * S, 2, P])
        sctx = sb("sctx", [P, 2, 2 * S])
        keep = sb("keep", [P, 2, 10])
        tail = sb("ftail", [10, 2, P])
        slot = k.slots
        hs = sb("fhs", [P, KD, S])
        normed = Normed(k, slot[1], [t_ab[0][:, 0:TP], t_ab[1][:, 0:TP], raw[:, 0:TP]], hs, 3, 4)
        v, t = sb("fv", [P, TC]), sb("ftmp", [P, TC])
        sq, acc = (raw, t_ab[0]), t_ab[1]
        c_bank, t_bank = ps("c_bank", [P, 512]), ps("ft_bank", [P, 512])
        raw_ready = [k.sem("raw_ready0"), k.sem("raw_ready1")]
        free = [k.sem("free0"), k.sem("free1")]
        (hi_done, lo_done, up_done, down_done, d_ready, d_hi_done, d_lo_done, s_ready, ctx_turned, ctx_moved, tapped, kept,
         conv, gate_done, f_done, f_hi_done, f_lo_done, tail_turned, tail_moved, stored, passed, samp, raw_used, sq_ready, summed, sums_ready, link_v) = (k.sem(n) for n in (
             "hi_done", "lo_done", "up_done", "down_done", "d_ready", "d_hi_done", "d_lo_done", "s_ready", "ctx_turned",
             "ctx_moved", "tapped", "kept", "conv", "gate_done", "f_done", "f_hi_done", "f_lo_done", "tail_turned",
             "tail_moved", "stored", "passed_f", "samp", "raw_used", "sq_ready", "summed",
             "sums_ready", "link_v"))
        block = ctx.enter_context(nc.Block())
        vec = k.vecs
        up = d["ffn_up"][L].rearrange("(k p) n -> p k n", p=P)

        @block.sync
        def _(sp):
            sp.dma_start(d["ffn_conv_sample"][L, :, 0, :], d["state_ffn_conv"][L, :, 1, :]).then_inc(stored, 16)

            def load_up(i):
                for half in range(2):
                    at = i * P + half * D_FF
                    gated(sp, lo_done, i * 2 + (half + 1), passed)
                    sp.dma_start(k.w_raw[half][:, :, :], up[:, :, bass.ds(at, P)]).then_inc(raw_ready[half], 16)

            def load_rest(i):
                gated(sp, ctx_turned, i + 1, passed)
                for half in range(2):
                    sp.dma_start(srow[:, half, :], d["state_ffn_conv"][L, :, :, bass.ds(i * P + half * D_FF, P)].rearrange(
                        "s r n -> (s r) n")).then_inc(s_ready, 16)
                gated(sp, d_lo_done, i + 1, passed)
                sp.dma_start(d_raw[:, :], d["ffn_down"][L, bass.ds(i * P, P), :]).then_inc(d_ready, 16)

            load_rest(0)
            with sp.Fori(0, FT - 1) as i:
                load_up(i + 1)
                load_rest(i + 1)
            sp.wait_ge(stored, 32 + 64 * FT)

        @block.gpsimd
        def _(pool):
            for _ in range(4):
                pool.sem_inc(lo_done, 1)
            normed.on_pool(pool)
            pool.sem_inc(d_lo_done, 1)
            pool.memset(k.cat[:, :, :], 0.0).then_inc(k.zeroed, 1)

            def lo(i, half):
                gated(pool, hi_done, i * 2 + (half + 1), passed)
                gated(pool, up_done, i * 2 + (half + 1), passed)
                pool.tensor_tensor(k.w_lo[half][:, :, :], k.w_raw[half][:, :, :], k.w_hi[half][:, :, :].bitcast(F32),
                                   ALU.subtract).then_inc(lo_done, 1)

            def down_lo(i):
                gated(pool, d_hi_done, i + 1, passed)
                gated(pool, down_done, i * 8 + 1, passed)
                pool.tensor_tensor(d_lo[:, :], d_raw[:, :], d_hi[:, :].bitcast(F32), ALU.subtract).then_inc(d_lo_done, 1)

            lo(1, 0)
            lo(1, 1)
            with pool.Fori(0, FT - 2) as i:
                down_lo(i)
                lo(i + 2, 0)
                lo(i + 2, 1)
            down_lo(FT - 2)
            down_lo(FT - 1)

        @block.tensor
        def _(pe):
            ident = const(k, "ident")
            pe.sem_inc(up_done, 1)
            pe.sem_inc(up_done, 1)
            pe.sem_inc(down_done, 1)
            pe.sem_inc(ctx_turned, 1)

            def turn_context(i):
                pe.wait_ge(s_ready, i * 32 + 32)
                pe.wait_ge(ctx_moved, i + 1)
                for half in range(2):
                    last = pe.matmul(c_bank[:, 16 * half:16 * half + 16], srow[:, half, :], ident[0:16, 0:16], start=True, stop=True)
                last.then_inc(ctx_turned, 1)

            def turn_tail(i):
                pe.wait_ge(kept, i * 2 + 2)
                pe.wait_ge(tail_moved, i + 1)
                for half in range(2):
                    last = pe.matmul(t_bank[0:10, P * half:P * half + P], keep[:, half, :], ident, start=True, stop=True)
                last.then_inc(tail_turned, 1)

            def project_up(i, half, use, x_ready=None):
                pe.wait_ge(lo_done, i * 2 + (half + 3))
                pe.wait_ge(free[half], use + 1)
                product3(pe, slot[half], k.w_hi[half], k.w_lo[half], k.h_hi, k.h_lo, KD, slice(0, P),
                         x_ready).then_inc(up_done, 1)

            def project_down(m, use, b):
                s = SLOT_OF[m]
                pe.wait_ge(free[s], use + 1)
                cols = slice(P * m, P * m + P)
                for w, x, n in ((d_hi, f_hi[b], 0), (d_hi, f_lo[b], 1), (d_lo, f_hi[b], 2)):
                    for lo, hi in CHUNKS:
                        last = pe.matmul(slot[s][:, OFF + lo:OFF + hi], w[:, cols], x[:, lo:hi], start=(n == 0), stop=(n == 2))
                last.then_inc(down_done, 1)

            def step(i, b):
                turn_context(i + 1)
                project_up(i + 1, 0, i * 5 + 1)
                pe.wait_ge(f_lo_done, i + 1)
                pe.wait_ge(d_lo_done, i + 2)
                for m, use in ((0, 1), (1, 2), (2, 2), (3, 3)):
                    project_down(m, i * 5 + use, b)
                project_up(i + 1, 1, i * 5 + 3)
                for m, use in ((4, 4), (5, 4)):
                    project_down(m, i * 5 + use, b)
                turn_tail(i + 1)
                for m, use in ((6, 5), (7, 5)):
                    project_down(m, i * 5 + use, b)

            project_up(0, 0, 0, normed.on_pe)
            turn_context(0)
            project_up(0, 1, 0)
            turn_tail(0)
            with pe.Fori(0, FT // 2 - 1) as n:
                for b in range(2):
                    step(n * 2 + b, b)
            step(FT - 2, 0)
            pe.wait_ge(f_lo_done, FT)
            pe.wait_ge(d_lo_done, FT + 1)
            for m in range(KD):
                project_down(m, LAST_USE[m], 1)
            pe.wait_ge(summed, KD - 1)
            pe.wait_ge(ctx_moved, FT + 1)
            pe_token_sums(k, pe, c_bank, acc, True, True).then_inc(sums_ready, 1)

        @block.scalar
        def _(act):
            act.sem_inc(ctx_moved, 1)
            act.sem_inc(tail_moved, 1)
            act.sem_inc(stored, 16)
            normed.on_act(act)

            def split(i, half):
                gated(act, raw_ready[half], i * 16 + 16, passed)
                gated(act, up_done, i * 2 + (half + 1), passed)
                act.activation(k.w_hi[half][:, :, :], k.w_raw[half][:, :, :], ACT.Copy).then_inc(hi_done, 1)

            def split_down(i):
                gated(act, d_ready, i * 16 + 16, passed)
                gated(act, down_done, i * 8 + 1, passed)
                act.activation(d_hi[:, :], d_raw[:, :], ACT.Copy).then_inc(d_hi_done, 1)

            def context(i):
                gated(act, ctx_turned, i + 2, passed)
                if not isinstance(i, int) or i > 0:
                    gated(act, samp, i * 2, passed)
                act.activation(sctx[:, :, :], c_bank[:, 0:32].rearrange("p (a n) -> p a n", a=2), ACT.Copy).then_inc(ctx_moved, 1)

            def read_out(i, half, use):
                first = isinstance(i, int) and i == 0
                gated(act, up_done, i * 2 + (half + 3), passed)
                if half or not first:
                    gated(act, raw_used, i * 2 + half, passed)
                if not first:
                    gated(act, kept, i * 2 + half, passed)
                elif half:
                    act.wait_ge(kept, 1)
                act.activation(raw[:, :], slot[half][:, OFF:OFF + NT], ACT.Copy).then_inc(free[half], 1)
                gated(act, free[half], use + 2, passed)
                if not first:
                    if half == 0:
                        gated(act, f_done, i, passed)
                    else:
                        gated(act, f_hi_done, i, passed)
                        gated(act, f_lo_done, i, passed)
                c = i + (FT if half else 0)
                act.activation(t_ab[half][:, :], raw[:, :], ACT.Identity, scale=vec[:, 3, bass.ds(c, 1)],
                               bias=vec[:, 3, bass.ds(c + 2 * FT, 1)]).then_inc(tapped, 1)
                if not first:
                    gated(act, tail_turned, i, passed)
                act.activation(keep[:, half, :], raw[:, TP - 2:NT], ACT.Copy).then_inc(kept, 1)

            def gate(i):
                gated(act, samp, i * 2 + 1, passed)
                gated(act, raw_used, i * 2 + 1, passed)
                act.activation(t_ab[0][:, :], t_ab[0][:, :], ACT.Silu).then_inc(gate_done, 1)

            def split_hidden(i, b):
                gated(act, f_done, i + 1, passed)
                act.activation(f_hi[b][:, :], t_ab[1][:, :], ACT.Copy).then_inc(f_hi_done, 1)

            def tail_out(i):
                gated(act, tail_turned, i + 1, passed)
                gated(act, stored, i * 64 + 32, passed)
                act.activation(tail[:, :, :], t_bank[0:10, 0:2 * P].rearrange("p (a n) -> p a n", a=2), ACT.Copy).then_inc(tail_moved, 1)
                gated(act, tail_moved, i + 2, passed)
                for half in range(2):
                    cols = bass.ds(i * P + half * D_FF, P)
                    act.dma_start(d["ffn_conv_prompt"][L, 0, :, cols], tail[0:2, half, :]).then_inc(stored, 16)
                    act.dma_start(d["ffn_conv_sample"][L, :, 1, cols], tail[2:10, half, :]).then_inc(stored, 16)

            def step(i, b, ahead):
                split_down(i)
                split_hidden(i, b)
                context(i + 1)
                read_out(i + 1, 0, i * 5 + 1)
                if ahead:
                    split(i + 2, 0)
                tail_out(i)
                read_out(i + 1, 1, i * 5 + 3)
                gate(i + 1)
                if ahead:
                    split(i + 2, 1)

            for half in range(2):
                act.sem_inc(raw_ready[half], 16)
                act.sem_inc(hi_done, 1)
            context(0)
            read_out(0, 0, 0)
            split(1, 0)
            read_out(0, 1, 0)
            gate(0)
            split(1, 1)
            with act.Fori(0, FT // 2 - 1) as n:
                for b in range(2):
                    step(n * 2 + b, b, True)
            step(FT - 2, 0, False)
            split_down(FT - 1)
            split_hidden(FT - 1, 1)
            tail_out(FT - 1)
            act.wait_ge(f_lo_done, FT)
            for m in range(KD):
                act.wait_ge(free[SLOT_OF[m]], LAST_USE[m] + 2)
                if m >= 2:
                    act.wait_ge(summed, max(1, m - 2))
                act.activation(sq[m % 2][:, :], k.cat[:, m, :], ACT.Square).then_inc(sq_ready, 1)

        @block.vector
        def _(dve):
            dve.sem_inc(free[0], 1)
            dve.sem_inc(free[1], 1)
            normed.on_dve(dve)
            dve.wait_ge(k.zeroed, 1)

            def taps(i, half):
                dve.wait_ge(tapped, i * 2 + (half + 1))
                dve.wait_ge(ctx_moved, i + 2)
                t, c = t_ab[half], i + (FT if half else 0)
                tap0, tap1 = vec[:, 2, bass.ds(c, 1)], vec[:, 2, bass.ds(c + 2 * FT, 1)]
                dve.scalar_tensor_tensor(t[:, 1:TP], raw[:, 0:TP - 1], tap1, t[:, 1:TP], ALU.mult, ALU.add).then_inc(conv, 1)
                dve.scalar_tensor_tensor(t[:, TP:NT], sctx[:, half, 1:16:2], tap1, t[:, TP:NT], ALU.mult, ALU.add).then_inc(conv, 1)
                dve.wait_ge(conv, i * 4 + (2 * half + 2))
                dve.scalar_tensor_tensor(t[:, 2:TP], raw[:, 0:TP - 2], tap0, t[:, 2:TP], ALU.mult, ALU.add).then_inc(raw_used, 1)
                dve.scalar_tensor_tensor(t[:, TP:NT], sctx[:, half, 0:16:2], tap0, t[:, TP:NT], ALU.mult, ALU.add).then_inc(samp, 1)

            def product(i, b):
                dve.wait_ge(gate_done, i + 1)
                dve.wait_ge(raw_used, i * 2 + 2)
                dve.wait_ge(samp, i * 2 + 2)
                dve.tensor_tensor(t_ab[1][:, :], t_ab[0][:, :], t_ab[1][:, :], ALU.mult).then_inc(f_done, 1)
                dve.wait_ge(f_hi_done, i + 1)
                dve.tensor_tensor(f_lo[b][:, :], t_ab[1][:, :], f_hi[b][:, :].bitcast(F32), ALU.subtract).then_inc(f_lo_done, 1)

            def gather(i, some):
                for m in some:
                    s = SLOT_OF[m]
                    dve.wait_ge(down_done, i * 8 + (m + 2))
                    dve.tensor_tensor(k.cat[:, m, :], k.cat[:, m, :], slot[s][:, OFF:OFF + NT], ALU.add).then_inc(free[s], 1)

            def step(i, b):
                gather(i, range(4))
                taps(i + 1, 0)
                gather(i, range(4, 8))
                taps(i + 1, 1)
                product(i + 1, 1 - b)

            taps(0, 0)
            taps(0, 1)
            product(0, 0)
            with dve.Fori(0, FT // 2 - 1) as n:
                for b in range(2):
                    step(n * 2 + b, b)
            step(FT - 2, 0)
            gather(FT - 1, range(2))
            for m in range(1, KD):
                if m + 1 < KD:
                    gather(FT - 1, (m + 1,))
                dve.wait_ge(sq_ready, m + 1)
                if m > 1:
                    dve.wait_ge(summed, m - 1)
                dve.tensor_tensor(acc[:, :], sq[0][:, :] if m == 1 else acc[:, :], sq[m % 2][:, :], ALU.add).then_inc(summed, 1)
            link = Link(dve, link_v)
            dve.wait_ge(sums_ready, 1)
            dve_inverse_rms(k, dve, link, c_bank, v, t)


def block_exit(k):
    nc, d = k.nc, k.dram
    with ExitStack() as ctx:
        sb = lambda n, s, t=F32: ctx.enter_context(nc.sbuf_tensor(n, s, t))
        ps = lambda n, s, t=F32: ctx.enter_context(nc.psum_tensor(n, s, t))
        sem = lambda n: ctx.enter_context(nc.semaphore(n))
        yrow = sb("yrow", [P, TC, D_MODEL])
        bank = [ps(f"ybank{i}", [P, 512]) for i in range(2)]
        turned, moved, stored = sem("y_turned"), [sem("y_moved_dve"), sem("y_moved_act")], sem("y_stored")
        block = ctx.enter_context(nc.Block())
        steps = [(c, half) for c in range(TC) for half in range(2)]

        @block.tensor
        def _(pe):
            for n, (c, half) in enumerate(steps):
                if n >= 2:
                    pe.wait_ge(moved[n % 2], n // 2)
                w = min(P, NT - c * P)
                for j in range(4):
                    src = k.x[:, 4 * half + j, P * c:P * c + w]
                    out = bank[n % 2][0:w, P * j:P * j + P]
                    last = pe.transpose(out, src, const(k, "ident")) if w == P else pe.matmul(out, src, const(k, "ident"), start=True, stop=True)
                last.then_inc(turned, 1)

        @block.vector
        def _(dve):
            for n in range(0, len(steps), 2):
                dve.wait_ge(turned, n + 1)
                c = steps[n][0]
                w = min(P, NT - c * P)
                dve.tensor_copy(yrow[0:w, c, 0:512], bank[0][0:w, :]).then_inc(moved[0], 1)

        @block.scalar
        def _(act):
            for n in range(1, len(steps), 2):
                act.wait_ge(turned, n + 1)
                c = steps[n][0]
                w = min(P, NT - c * P)
                act.activation(yrow[0:w, c, 512:1024], bank[1][0:w, :], ACT.Copy).then_inc(moved[1], 1)

        @block.sync
        def _(sp):
            for c in range(TC):
                sp.wait_ge(moved[0], c + 1)
                sp.wait_ge(moved[1], c + 1)
                if c < NC8:
                    sp.dma_start(d["y_prompt"][0, P * c:P * c + P, :], yrow[:, c, :]).then_inc(stored, 16)
                else:
                    sp.dma_start(d["y_sample"][:, 0, :], yrow[0:S, c, :]).then_inc(stored, 16)
            sp.wait_ge(stored, 16 * TC)


def trunk(nc, dram):
    k = K()
    k.nc, k.dram = nc, dram
    with ExitStack() as ctx:
        sb = lambda n, s, t=F32: ctx.enter_context(nc.sbuf_tensor(n, s, t))
        k.x = sb("x_res", [P, KD, NT])
        k.cat = sb("cat", [P, KD, NT])
        k.consts = sb("consts", [P, N_CONST])
        k.ident_bf, k.mask_bf = sb("ident_bf", [P, P], BF16), sb("mask_bf", [P, P], BF16)
        k.pages = sb("pages", [1, S * NPG], I32)
        k.cT = sb("cT", [P, KD, 9])
        k.mod = sb("mod", [P, 6, KD, 9])
        k.vecs = sb("vecs", [P, 4, P])
        k.inv = sb("inv", [P, TC])
        k.logf = sb("logf", [P, TC * HA])
        k.ncum = sb("ncum", [P, NC8 * HA])
        k.q_new, k.k_new, k.v_new = (sb(n, [P, HA, S]) for n in ("q_new", "k_new", "v_new"))
        k.w_raw = [sb(f"w_raw{i}", [P, KD, P]) for i in range(2)]
        k.w_hi = [sb(f"w_hi{i}", [P, KD, P], F32R) for i in range(2)]
        k.w_lo = [sb(f"w_lo{i}", [P, KD, P], F32R) for i in range(2)]
        k.v_ret, k.q_ret = k.cat[:, 0:2, :], k.cat[:, 2:4, :]
        signals = [ctx.enter_context(nc.semaphore(f"signal{i}")) for i in range(44)]
        first, final = signals[0].num, signals[-1].num
        assert final - first == len(signals) - 1
        taken = [0]

        def signal(name):
            taken[0] += 1
            return signals[taken[0] - 1]

        k.sem = signal

        def run(block, *args):
            taken[0] = 0
            k.quiet = signal("quiet")
            k.zeroed = signal("zeroed")
            block(k, *args)
            nc.all_engine_barrier(sems_to_clear=range(first, final + 1))

        block_entry(k)
        with nc.Fori(0, DEPTH) as L:
            run(block_modulation, L)
            with ExitStack() as wide:
                k.h_hi, k.h_lo = (wide.enter_context(nc.sbuf_tensor(n, [P, KD, NT], F32R)) for n in ("h_hi", "h_lo"))
                with nc.sbuf_tensor("k_ret", [P, 2, NT], F32) as k.k_ret:
                    run(block_project, L)
                    run(block_retention, L)
                    run(block_group_norms, L)
                run(block_heads, L)
            run(block_samples, L)
            with ExitStack() as wide:
                k.h_hi, k.h_lo = (wide.enter_context(nc.sbuf_tensor(n, [P, KD, NT], F32R)) for n in ("g_hi", "g_lo"))
                run(block_output, L)
                k.slots = [wide.enter_context(nc.psum_tensor(f"slots{i}", [P, SLOT], F32)) for i in range(2)]
                up = dram["ffn_up"][L].rearrange("(k p) n -> p k n", p=P)
                run(block_join, L, "_j1", 2, [up[:, :, 0:P], up[:, :, D_FF:D_FF + P]])
                run(block_ffn, L)
                run(block_join, L, "_j2", 5)
        block_exit(k)


_INS = ["x_prompt", "x_sample", "cache_k", "cache_v", "cache_logf", "state_ret", "state_conv", "state_ffn_conv", "page_table",
        "c_prompt", "c_sample", "ada_w", "ada_b", "norms", "w_in", "b_f", "ret_gn_g", "conv_w", "conv_b", "conv_ln_g",
        "conv_ln_b", "w_o", "ffn_up", "ffn_conv_w", "ffn_conv_b", "ffn_down"]
_OUTS = [("y_prompt", (1, TP, D_MODEL)), ("y_sample", (S, 1, D_MODEL)),
         ("k_prompt", (DEPTH, 1, TP, HA, DA)), ("v_prompt", (DEPTH, 1, TP, HA, DA)), ("logf_prompt", (DEPTH, 1, TP, HA)),
         ("ret_prompt", (DEPTH, 1, HB, DB, DB)), ("conv_prompt", (DEPTH, 1, CTX, DC)),
         ("ffn_conv_prompt", (DEPTH, 1, FW - 1, 2 * D_FF)),
         ("k_sample", (DEPTH, S, 1, HA, DA)), ("v_sample", (DEPTH, S, 1, HA, DA)), ("logf_sample", (DEPTH, S, 1, HA)),
         ("ret_sample", (DEPTH, S, HB, DB, DB)), ("conv_sample", (DEPTH, S, CTX, DC)),
         ("ffn_conv_sample", (DEPTH, S, FW - 1, 2 * D_FF))]


def kernel(**inputs):
    import numpy as _np
    import concourse.bacc as _bacc
    from concourse import mybir as _mybir
    from concourse.bass_utils import run_bass_kernel_spmd as _run

    nc = _bacc.Bacc("TRN2", target_bir_lowering=False, num_devices=1)
    arrays, dram = {}, {}
    consts, rope = constants()
    for name, a in [(n, inputs[n]) for n in _INS] + [("consts", consts), ("rope", rope)]:
        a = _np.ascontiguousarray(a)
        arrays[f"in_{name}_dram"] = a
        dram[name] = nc.dram_tensor(f"in_{name}_dram", a.shape, _mybir.dt.from_np(a.dtype), kind="ExternalInput").ap()
    for name, shape in _OUTS:
        dram[name] = nc.dram_tensor(f"out_{name}_dram", shape, F32, kind="ExternalOutput").ap()
    trunk(nc, dram)
    r = _run(nc, [arrays], core_ids=[0])
    return tuple(r.results[0][f"out_{name}_dram"] for name, _ in _OUTS)
```
